# Optimizing a Trainium2 kernel written in Bass

```python
import math
import jax, jax.numpy as jnp
from jax import lax
import numpy as np

D_MODEL = 1024
BATCH = 1
SEQ = 256
DEPTH = 2

N_META = 16
N_MIXERS = 2
N_A_LAYERS = (DEPTH + 1) // 2
N_B_LAYERS = DEPTH // 2

DA_HEADS = 8
DA_HEAD_DIM = D_MODEL // (2 * DA_HEADS)
DA_V_DIM = 2 * DA_HEAD_DIM
Q_BLOCK = 128
SUBLN_EPS = 1e-5

RW_HEAD_DIM = 64
RW_HEADS = D_MODEL // RW_HEAD_DIM
RW_DECAY_LORA = 64
RW_AAA_LORA = 64
RW_GATE_LORA = 160
RW_N_MIX = 6
RW_LNX_EPS = 64e-5

D_FF = 2816
N_EXPERTS = 8
TOP_K = 2
D_FF_EXPERT = 3584

LN_EPS = 1e-5
DEEPNORM_ALPHA = (2.0 * DEPTH) ** 0.25
DEEPNORM_BETA = (8.0 * DEPTH) ** -0.25


def layer_norm(x, g, b):
    xf = x.astype(jnp.float32)
    mu = jnp.mean(xf, -1, keepdims=True)
    var = jnp.mean(jnp.square(xf - mu), -1, keepdims=True)
    return ((xf - mu) * lax.rsqrt(var + LN_EPS) * g + b).astype(x.dtype)

def diff_attention(x, w_in, w_o, lq1, lk1, lq2, lk2, subln_g, layer_idx):
    B, L, D = x.shape
    H, Dh, Dv = DA_HEADS, DA_HEAD_DIM, DA_V_DIM
    Lp = -(-L // Q_BLOCK) * Q_BLOCK
    nblk = Lp // Q_BLOCK
    qkv = jnp.einsum('bld,de->ble', x, w_in)
    qkv = jnp.pad(qkv, ((0, 0), (0, Lp - L), (0, 0)))
    q, k, v = jnp.split(qkv, 3, axis=-1)
    q = q.reshape(B, Lp, H, 2, Dh)
    k = k.reshape(B, Lp, H, 2, Dh)
    vf = v.reshape(B, Lp, H, Dv).astype(jnp.float32)
    lam_init = 0.8 - 0.6 * math.exp(-0.3 * layer_idx)
    lam = (jnp.exp(jnp.sum(lq1 * lk1).astype(jnp.float32))
           - jnp.exp(jnp.sum(lq2 * lk2).astype(jnp.float32)) + lam_init)
    slopes = 2.0 ** (-(8.0 / H) * jnp.arange(1, H + 1, dtype=jnp.float32))
    kpos = jnp.arange(Lp, dtype=jnp.int32)
    kvalid = kpos < L
    scale = Dh ** -0.5
    qb = q.reshape(B, nblk, Q_BLOCK, H, 2, Dh).transpose(1, 0, 2, 3, 4, 5)
    starts = jnp.arange(nblk, dtype=jnp.int32) * Q_BLOCK

    def block(args):
        qblk, start = args
        s = jnp.einsum('bqhcd,bkhcd->bhcqk', qblk, k).astype(jnp.float32) * scale
        qpos = start + jnp.arange(Q_BLOCK, dtype=jnp.int32)
        dist = jnp.abs(qpos[:, None] - kpos[None, :]).astype(jnp.float32)
        s = s - slopes[None, :, None, None, None] * dist
        s = jnp.where(kvalid, s, -jnp.inf)
        p = jax.nn.softmax(s, axis=-1)
        a = p[:, :, 0] - lam * p[:, :, 1]
        return jnp.einsum('bhqk,bkhe->bqhe', a, vf)

    o = lax.map(block, (qb, starts))
    o = o.transpose(1, 0, 2, 3, 4).reshape(B, Lp, H, Dv)[:, :L]
    o = o * lax.rsqrt(jnp.mean(o * o, -1, keepdims=True) + SUBLN_EPS) * subln_g * (1.0 - lam_init)
    o = o.reshape(B, L, H * Dv).astype(x.dtype)
    return jnp.einsum('ble,ed->bld', o, w_o)

def _wkv7_step(S, inp):
    r, w, k, v, kk, a = inp
    sa = jnp.einsum('bhvk,bhk->bhv', S, kk)
    S = S * w[:, :, None, :] - sa[..., None] * (kk * a)[:, :, None, :] + v[..., None] * k[:, :, None, :]
    y = jnp.einsum('bhvk,bhk->bhv', S, r)
    return S, y

def rwkv7_time_mix(x, mu, w_rkv, w0, w1, w2, a0, a1, a2, g1, g2, k_k, k_a, r_k, lnx_g, lnx_b, w_o):
    B, L, D = x.shape
    H, N = RW_HEADS, RW_HEAD_DIM
    zero = jnp.zeros_like(x[:, :1])
    dx_prev = jnp.concatenate([zero, x[:, :-1]], 1) - x
    dx_next = jnp.concatenate([x[:, 1:], zero], 1) - x
    xs = x[None] + mu[0][:, None, None, :] * dx_prev[None] + mu[1][:, None, None, :] * dx_next[None]
    r, k, v = jnp.einsum('ibld,ide->ible', xs[:3], w_rkv)
    lw = jnp.einsum('nblr,nrd->nbld', jnp.tanh(jnp.einsum('bld,ndr->nblr', xs[3], w1)), w2)
    w_log = -jax.nn.softplus(-(w0[:, None, None, :] + lw).astype(jnp.float32)) - 0.5
    decay = jnp.exp(-jnp.exp(w_log))
    la = jnp.einsum('nblr,nrd->nbld', jnp.einsum('bld,ndr->nblr', xs[4], a1), a2)
    a = jax.nn.sigmoid((a0[:, None, None, :] + la).astype(jnp.float32))
    g = jnp.einsum('blr,rd->bld', jax.nn.sigmoid(jnp.einsum('bld,dr->blr', xs[5], g1)), g2)
    kf = k.astype(jnp.float32)
    kk = (kf * k_k).reshape(B, L, H, N)
    kk = kk / jnp.maximum(jnp.sqrt(jnp.sum(kk * kk, -1, keepdims=True)), 1e-12)
    kd = kf[None] * (1.0 + (a - 1.0) * k_a)

    def tm(t):
        return jnp.swapaxes(t.reshape(B, L, H, N), 0, 1).astype(jnp.float32)

    r_t, v_t, kk_t = tm(r), tm(v), jnp.swapaxes(kk, 0, 1)
    S0 = jnp.zeros((B, H, N, N), jnp.float32)
    _, y_fwd = lax.scan(_wkv7_step, S0, (r_t, tm(decay[0]), tm(kd[0]), v_t, kk_t, tm(a[0])))
    _, y_bwd = lax.scan(_wkv7_step, S0, (r_t, tm(decay[1]), tm(kd[1]), v_t, kk_t, tm(a[1])), reverse=True)
    y = jnp.swapaxes(y_fwd + y_bwd, 0, 1)
    ym = jnp.mean(y, -1, keepdims=True)
    yv = jnp.mean(jnp.square(y - ym), -1, keepdims=True)
    y = ((y - ym) * lax.rsqrt(yv + RW_LNX_EPS)).reshape(B, L, D) * lnx_g + lnx_b
    rh = r.reshape(B, L, H, N).astype(jnp.float32)
    kdh = (kd[0] + kd[1]).reshape(B, L, H, N)
    bonus = jnp.sum(rh * kdh * r_k, -1, keepdims=True) * v.reshape(B, L, H, N).astype(jnp.float32)
    out = ((y + bonus.reshape(B, L, D)) * g).astype(x.dtype)
    return jnp.einsum('bld,de->ble', out, w_o)

def swiglu(x, w_gate, w_up, w_down):
    return (jax.nn.silu(x @ w_gate) * (x @ w_up)) @ w_down

def moe_swiglu(x, w_router, b_router, w_gate, w_up, w_down):
    logits = (jnp.einsum('bld,de->ble', x, w_router) + b_router).astype(jnp.float32)
    probs = jax.nn.softmax(logits, -1)
    top_p, top_i = lax.top_k(probs, TOP_K)
    top_p = top_p / jnp.sum(top_p, -1, keepdims=True)
    gates = jnp.sum(jax.nn.one_hot(top_i, N_EXPERTS, dtype=jnp.float32) * top_p[..., None], -2)
    y = jnp.zeros(x.shape, jnp.float32)
    for e in range(N_EXPERTS):
        y = y + gates[..., e:e + 1] * swiglu(x, w_gate[e], w_up[e], w_down[e]).astype(jnp.float32)
    return y.astype(x.dtype)

def first_inputs(seed: int = 0) -> dict:
    key = jax.random.key(seed)
    ks = iter(jax.random.split(key, 48))
    f32 = jnp.float32
    D, F, FE, E = D_MODEL, D_FF, D_FF_EXPERT, N_EXPERTS
    nA, nB = N_A_LAYERS, N_B_LAYERS

    def nrm(shape, scale):
        return jax.random.normal(next(ks), shape, f32) * scale

    inp = {}
    inp['x'] = nrm((BATCH, SEQ, D), 1.0)
    inp['meta'] = nrm((N_META, D), 1.0)
    inp['ln_g'] = 1.0 + nrm((DEPTH, 2, D), 0.02)
    inp['ln_b'] = nrm((DEPTH, 2, D), 0.02)
    inp['attn_w_in'] = nrm((nA, D, 3 * D), D ** -0.5)
    inp['attn_w_o'] = nrm((nA, D, D), D ** -0.5 * DEEPNORM_BETA)
    inp['attn_lam_q1'] = nrm((nA, DA_HEAD_DIM), 0.1)
    inp['attn_lam_k1'] = nrm((nA, DA_HEAD_DIM), 0.1)
    inp['attn_lam_q2'] = nrm((nA, DA_HEAD_DIM), 0.1)
    inp['attn_lam_k2'] = nrm((nA, DA_HEAD_DIM), 0.1)
    inp['attn_subln_g'] = 1.0 + nrm((nA, DA_V_DIM), 0.02)
    inp['ffn_w_gate'] = nrm((nA, D, F), D ** -0.5)
    inp['ffn_w_up'] = nrm((nA, D, F), D ** -0.5)
    inp['ffn_w_down'] = nrm((nA, F, D), F ** -0.5 * DEEPNORM_BETA)
    inp['rw_mu'] = jax.random.uniform(next(ks), (nB, 2, RW_N_MIX, D), f32, 0.0, 0.5)
    inp['rw_w_rkv'] = nrm((nB, 3, D, D), D ** -0.5)
    inp['rw_w0'] = -1.0 + nrm((nB, 2, D), 0.5)
    inp['rw_w1'] = nrm((nB, 2, D, RW_DECAY_LORA), D ** -0.5)
    inp['rw_w2'] = nrm((nB, 2, RW_DECAY_LORA, D), 0.5 * RW_DECAY_LORA ** -0.5)
    inp['rw_a0'] = nrm((nB, 2, D), 0.1)
    inp['rw_a1'] = nrm((nB, 2, D, RW_AAA_LORA), D ** -0.5)
    inp['rw_a2'] = nrm((nB, 2, RW_AAA_LORA, D), 0.5 * RW_AAA_LORA ** -0.5)
    inp['rw_g1'] = nrm((nB, D, RW_GATE_LORA), D ** -0.5)
    inp['rw_g2'] = nrm((nB, RW_GATE_LORA, D), RW_GATE_LORA ** -0.5)
    inp['rw_k_k'] = 0.85 + nrm((nB, D), 0.05)
    inp['rw_k_a'] = 1.0 + nrm((nB, D), 0.05)
    inp['rw_r_k'] = nrm((nB, RW_HEADS, RW_HEAD_DIM), 0.1)
    inp['rw_lnx_g'] = 1.0 + nrm((nB, D), 0.02)
    inp['rw_lnx_b'] = nrm((nB, D), 0.02)
    inp['rw_w_o'] = nrm((nB, D, D), D ** -0.5 * DEEPNORM_BETA)
    inp['moe_w_router'] = nrm((nB, D, E), D ** -0.5)
    inp['moe_b_router'] = nrm((nB, E), 0.01)
    inp['moe_w_gate'] = nrm((nB, E, D, FE), D ** -0.5)
    inp['moe_w_up'] = nrm((nB, E, D, FE), D ** -0.5)
    inp['moe_w_down'] = nrm((nB, E, FE, D), FE ** -0.5 * DEEPNORM_BETA)
    return inp

def first_block(x, meta, ln_g, ln_b, attn_w_in, attn_w_o, attn_lam_q1, attn_lam_k1, attn_lam_q2,
              attn_lam_k2, attn_subln_g, ffn_w_gate, ffn_w_up, ffn_w_down, rw_mu, rw_w_rkv, rw_w0,
              rw_w1, rw_w2, rw_a0, rw_a1, rw_a2, rw_g1, rw_g2, rw_k_k, rw_k_a, rw_r_k, rw_lnx_g,
              rw_lnx_b, rw_w_o, moe_w_router, moe_b_router, moe_w_gate, moe_w_up, moe_w_down):
    B = x.shape[0]
    h = jnp.concatenate([jnp.broadcast_to(meta[None].astype(x.dtype), (B, N_META, D_MODEL)), x], 1)
    for i in range(DEPTH):
        j = i // N_MIXERS
        if i % N_MIXERS == 0:
            mix = diff_attention(h, attn_w_in[j], attn_w_o[j], attn_lam_q1[j], attn_lam_k1[j],
                                 attn_lam_q2[j], attn_lam_k2[j], attn_subln_g[j], i)
        else:
            mix = rwkv7_time_mix(h, rw_mu[j], rw_w_rkv[j], rw_w0[j], rw_w1[j], rw_w2[j], rw_a0[j],
                                 rw_a1[j], rw_a2[j], rw_g1[j], rw_g2[j], rw_k_k[j], rw_k_a[j],
                                 rw_r_k[j], rw_lnx_g[j], rw_lnx_b[j], rw_w_o[j])
        h = layer_norm(DEEPNORM_ALPHA * h + mix, ln_g[i, 0], ln_b[i, 0])
        if i % 2 == 0:
            ff = swiglu(h, ffn_w_gate[j], ffn_w_up[j], ffn_w_down[j])
        else:
            ff = moe_swiglu(h, moe_w_router[j], moe_b_router[j], moe_w_gate[j], moe_w_up[j], moe_w_down[j])
        h = layer_norm(DEEPNORM_ALPHA * h + ff, ln_g[i, 1], ln_b[i, 1])
    return h[:, N_META:]


N_HEADS = 8
HEAD_DIM = 128
ATTN_WIDTH = N_HEADS * HEAD_DIM
IDX_HEADS = 16
IDX_DIM = 64
TOPK_MAX = 256
D_RNN = 1408
RNN_BLOCKS = 16
RNN_BLOCK_DIM = D_RNN // RNN_BLOCKS
CONV_WIDTH = 4
LRU_C = 8.0
ROPE_THETA = 10000.0
NORM_EPS = 1e-6

SPLIT_SIZES = (ATTN_WIDTH, ATTN_WIDTH, ATTN_WIDTH, ATTN_WIDTH,
               IDX_HEADS * IDX_DIM, IDX_DIM, IDX_HEADS,
               D_RNN, D_RNN, D_MODEL, D_MODEL)
N_IN = sum(SPLIT_SIZES)


def rmsnorm(x, g):
    xf = x.astype(jnp.float32)
    y = xf * lax.rsqrt(jnp.mean(xf * xf, axis=-1, keepdims=True) + NORM_EPS)
    return (y * g.astype(jnp.float32)).astype(x.dtype)

def rope_tables(positions, dim):
    inv = ROPE_THETA ** (-jnp.arange(0, dim, 2, dtype=jnp.float32) / dim)
    ang = positions.astype(jnp.float32)[..., None] * inv
    return jnp.cos(ang), jnp.sin(ang)

def apply_rope(x, cos, sin):
    extra = x.ndim - cos.ndim
    shape = cos.shape[:2] + (1,) * extra + cos.shape[2:]
    c, s = cos.reshape(shape), sin.reshape(shape)
    x1, x2 = jnp.split(x.astype(jnp.float32), 2, axis=-1)
    return jnp.concatenate([x1 * c - x2 * s, x2 * c + x1 * s], axis=-1).astype(x.dtype)

def dsa_attention(q, k, v, iq, ik, iw):
    B, S, H, Dh = q.shape
    topk = min(TOPK_MAX, S // 4)
    n_blk = S // Q_BLOCK
    key_pos = jnp.arange(S)
    scale = HEAD_DIM ** -0.5
    iw = iw.astype(jnp.float32) * (IDX_HEADS ** -0.5) * (IDX_DIM ** -0.5)

    def block(i):
        q0 = i * Q_BLOCK
        qb = lax.dynamic_slice_in_dim(q, q0, Q_BLOCK, axis=1)
        iqb = lax.dynamic_slice_in_dim(iq, q0, Q_BLOCK, axis=1)
        iwb = lax.dynamic_slice_in_dim(iw, q0, Q_BLOCK, axis=1)
        qpos = q0 + jnp.arange(Q_BLOCK)
        causal = key_pos[None, :] <= qpos[:, None]
        dots = jnp.einsum('bqhd,bsd->bqhs', iqb, ik, preferred_element_type=jnp.float32)
        idx_score = jnp.einsum('bqh,bqhs->bqs', iwb, jax.nn.relu(dots))
        idx_score = jnp.where(causal[None], idx_score, -jnp.inf)
        _, sel = lax.top_k(idx_score, topk)
        valid = sel <= qpos[None, :, None]
        k_sel = jax.vmap(lambda kb, ib: kb[ib])(k, sel)
        v_sel = jax.vmap(lambda vb, ib: vb[ib])(v, sel)
        logits = jnp.einsum('bqhd,bqkhd->bhqk', qb, k_sel, preferred_element_type=jnp.float32) * scale
        logits = jnp.where(valid[:, None], logits, -jnp.inf)
        p = jax.nn.softmax(logits, axis=-1)
        return jnp.einsum('bhqk,bqkhd->bqhd', p.astype(v.dtype), v_sel)

    out = lax.map(block, jnp.arange(n_blk))
    return out.transpose(1, 0, 2, 3, 4).reshape(B, S, H, Dh)

def causal_depthwise_conv(x, w, b):
    y = lax.conv_general_dilated(
        x, w[:, None, :].astype(x.dtype), window_strides=(1,),
        padding=[(CONV_WIDTH - 1, 0)], dimension_numbers=('NWC', 'WIO', 'NWC'),
        feature_group_count=x.shape[-1])
    return y + b.astype(x.dtype)

def rg_lru(x, w_r, b_r, w_i, b_i, lam):
    B, S, _ = x.shape
    xb = x.reshape(B, S, RNN_BLOCKS, RNN_BLOCK_DIM)
    r = jax.nn.sigmoid((jnp.einsum('bsnc,ncd->bsnd', xb, w_r).reshape(B, S, D_RNN) + b_r).astype(jnp.float32))
    i = jax.nn.sigmoid((jnp.einsum('bsnc,ncd->bsnd', xb, w_i).reshape(B, S, D_RNN) + b_i).astype(jnp.float32))
    log_a = -LRU_C * r * jax.nn.softplus(-lam.astype(jnp.float32))
    a = jnp.exp(log_a)
    u = jnp.sqrt(-jnp.expm1(2.0 * log_a)) * (i * x.astype(jnp.float32))

    def combine(left, right):
        a_l, b_l = left
        a_r, b_r = right
        return a_l * a_r, a_r * b_l + b_r

    _, h = lax.associative_scan(combine, (a, u), axis=1)
    return h.astype(x.dtype)

def second_inputs(seed: int = 0) -> dict:
    key = jax.random.key(seed)
    ks = jax.random.split(key, 16)
    f32 = jnp.float32
    x = jax.random.normal(ks[0], (BATCH, SEQ, D_MODEL), f32)
    positions = jnp.broadcast_to(jnp.arange(SEQ, dtype=jnp.int32), (BATCH, SEQ))
    norm_g = 1.0 + 0.02 * jax.random.normal(ks[1], (DEPTH, D_MODEL), f32)
    w_in = jax.random.normal(ks[2], (DEPTH, D_MODEL, N_IN), f32) * D_MODEL ** -0.5
    conv_w = jax.random.normal(ks[3], (DEPTH, CONV_WIDTH, D_RNN), f32) * CONV_WIDTH ** -0.5
    conv_b = 0.01 * jax.random.normal(ks[4], (DEPTH, D_RNN), f32)
    w_rg = jax.random.normal(ks[5], (DEPTH, RNN_BLOCKS, RNN_BLOCK_DIM, RNN_BLOCK_DIM), f32) * RNN_BLOCK_DIM ** -0.5
    b_rg = 0.01 * jax.random.normal(ks[6], (DEPTH, D_RNN), f32)
    w_ig = jax.random.normal(ks[7], (DEPTH, RNN_BLOCKS, RNN_BLOCK_DIM, RNN_BLOCK_DIM), f32) * RNN_BLOCK_DIM ** -0.5
    b_ig = 0.01 * jax.random.normal(ks[8], (DEPTH, D_RNN), f32)
    a0 = jax.random.uniform(ks[9], (DEPTH, D_RNN), f32, 0.9, 0.999)
    p = a0 ** (1.0 / LRU_C)
    lru_lambda = jnp.log(p) - jnp.log1p(-p)
    w_out_attn = jax.random.normal(ks[10], (DEPTH, ATTN_WIDTH, D_MODEL), f32) * ATTN_WIDTH ** -0.5
    w_out_rnn = jax.random.normal(ks[11], (DEPTH, D_RNN, D_MODEL), f32) * D_RNN ** -0.5
    w_o = jax.random.normal(ks[12], (DEPTH, D_MODEL, D_MODEL), f32) * D_MODEL ** -0.5
    final_g = 1.0 + 0.02 * jax.random.normal(ks[13], (D_MODEL,), f32)
    return {"x": x, "positions": positions, "norm_g": norm_g, "w_in": w_in,
            "conv_w": conv_w, "conv_b": conv_b, "w_rg": w_rg, "b_rg": b_rg,
            "w_ig": w_ig, "b_ig": b_ig, "lru_lambda": lru_lambda,
            "w_out_attn": w_out_attn, "w_out_rnn": w_out_rnn, "w_o": w_o,
            "final_g": final_g}

def second_block(x, positions, norm_g, w_in, conv_w, conv_b, w_rg, b_rg, w_ig, b_ig,
              lru_lambda, w_out_attn, w_out_rnn, w_o, final_g):
    B, S, _ = x.shape
    offsets = np.cumsum(SPLIT_SIZES)[:-1].tolist()
    cos_a, sin_a = rope_tables(positions, HEAD_DIM)
    cos_i, sin_i = rope_tables(positions, IDX_DIM)
    for l in range(DEPTH):
        h = rmsnorm(x, norm_g[l])
        proj = h @ w_in[l]
        q, k, v, ga, iq, ik, iw, xr, gr, ma, mb = jnp.split(proj, offsets, axis=-1)
        q = apply_rope(q.reshape(B, S, N_HEADS, HEAD_DIM), cos_a, sin_a)
        k = apply_rope(k.reshape(B, S, N_HEADS, HEAD_DIM), cos_a, sin_a)
        v = v.reshape(B, S, N_HEADS, HEAD_DIM)
        iq = apply_rope(iq.reshape(B, S, IDX_HEADS, IDX_DIM), cos_i, sin_i)
        ik = apply_rope(ik, cos_i, sin_i)
        attn = dsa_attention(q, k, v, iq, ik, iw).reshape(B, S, ATTN_WIDTH)
        y_a = (attn * jax.nn.silu(ga)) @ w_out_attn[l]
        xr = causal_depthwise_conv(xr, conv_w[l], conv_b[l])
        hr = rg_lru(xr, w_rg[l], b_rg[l], w_ig[l], b_ig[l], lru_lambda[l])
        y_b = (hr * jax.nn.silu(gr)) @ w_out_rnn[l]
        merged = jax.nn.sigmoid(ma) * y_a + jax.nn.sigmoid(mb) * y_b
        x = x + merged @ w_o[l]
    return rmsnorm(x, final_g)


def setup_inputs(seed=0):
    out = dict(first_inputs(seed))
    for name, value in second_inputs(seed + 1).items():
        if name != "x":
            out[name + "_2"] = value
    return out


def reference(
    x, meta, ln_g, ln_b, attn_w_in, attn_w_o, attn_lam_q1, attn_lam_k1, attn_lam_q2,
    attn_lam_k2, attn_subln_g, ffn_w_gate, ffn_w_up, ffn_w_down, rw_mu, rw_w_rkv, rw_w0, rw_w1,
    rw_w2, rw_a0, rw_a1, rw_a2, rw_g1, rw_g2, rw_k_k, rw_k_a, rw_r_k, rw_lnx_g, rw_lnx_b,
    rw_w_o, moe_w_router, moe_b_router, moe_w_gate, moe_w_up, moe_w_down, positions_2, norm_g_2,
    w_in_2, conv_w_2, conv_b_2, w_rg_2, b_rg_2, w_ig_2, b_ig_2, lru_lambda_2, w_out_attn_2,
    w_out_rnn_2, w_o_2, final_g_2,
):
    x = first_block(
        x, meta, ln_g, ln_b, attn_w_in, attn_w_o, attn_lam_q1, attn_lam_k1, attn_lam_q2,
        attn_lam_k2, attn_subln_g, ffn_w_gate, ffn_w_up, ffn_w_down, rw_mu, rw_w_rkv, rw_w0,
        rw_w1, rw_w2, rw_a0, rw_a1, rw_a2, rw_g1, rw_g2, rw_k_k, rw_k_a, rw_r_k, rw_lnx_g,
        rw_lnx_b, rw_w_o, moe_w_router, moe_b_router, moe_w_gate, moe_w_up, moe_w_down,
    )
    return second_block(
        x, positions_2, norm_g_2, w_in_2, conv_w_2, conv_b_2, w_rg_2, b_rg_2, w_ig_2, b_ig_2,
        lru_lambda_2, w_out_attn_2, w_out_rnn_2, w_o_2, final_g_2,
    )


_drawn_inputs = setup_inputs


def setup_inputs(seed=0):
    import zlib

    import numpy as np

    out = dict(_drawn_inputs(seed))
    spreads = {}
    factors = {'attn_lam_q1': 3.078,
     'attn_lam_k2': 6.847,
     'attn_subln_g': 3.672,
     'rw_a0': 3.207,
     'rw_k_k': 4.384,
     'rw_lnx_g': 4.879,
     'rw_lnx_b': 3.946,
     'moe_b_router': 3.097,
     'norm_g_2': 3.511,
     'conv_b_2': 3.013,
     'b_rg_2': 8.0,
     'b_ig_2': 8.0,
     'final_g_2': 2.776}
    for name, (base, spread) in spreads.items():
        noise = np.random.default_rng([zlib.crc32(name.encode()), seed]).standard_normal(out[name].shape)
        drawn = base * np.exp(spread * noise) if base else spread * noise
        out[name] = __import__('jax').numpy.asarray(drawn.astype(out[name].dtype))
    for name, factor in factors.items():
        out[name] = (out[name] * factor).astype(out[name].dtype)
    return out
```

```python
import concourse.bass as bass
from concourse import mybir
from contextlib import ExitStack
import numpy as np

F32 = mybir.dt.float32
I32 = mybir.dt.int32
ALU = mybir.AluOpType
ACT = mybir.ActivationFunctionType
AX = mybir.AxisListType.X
MUL, ADD, SUB, MAX = ALU.mult, ALU.add, ALU.subtract, ALU.max

D = 1024
KC = 8
NMETA = 16
SEQ = 256
T = NMETA + SEQ
ALPHA = 4.0 ** 0.25
QT = [(0, 96), (96, 96), (192, 80)]
CH = 68
NCH = T // CH
MID = CH // 2
NRING = 5
NEG = -1.0e30
TAKEN = -3.0e38
FFN = 2816
FE = 3584
NE = 8
RB = 88
NRB = 16
SCAN_LEVELS = [1, 2, 4, 8, 16, 32, 64]
TWO_PI = 2.0 * np.pi

PARAMS = [("ln_g", 32), ("ln_b", 32), ("subln", 1), ("mu", 96), ("w0", 16), ("a0", 16), ("k_k", 8), ("k_a", 8),
          ("r_k", 8), ("lnx_g", 8), ("lnx_b", 8), ("norm_g", 16), ("final_g", 8), ("conv_w", 128),
          ("conv_b", 32), ("b_rg", 32), ("b_ig", 32), ("lam", 32), ("lamv", 256), ("b_router", 8)]
POFF = {}
_o = 0
for _n, _w in PARAMS:
    POFF[_n] = _o
    _o += _w
NPAR = _o

C_SCAN = 0
C_LVL = C_SCAN + T
C_AM = C_LVL + 2 * len(SCAN_LEVELS) * CH
NC_RW = C_AM + 4 * 2 * CH
NC_B2 = 256 + 512 + 2


class Engine:

    def __init__(self, sem):
        self.sem, self.n, self.items, self.passed = sem, 0, [], {}

    def wait(self, *toks):
        for sem, val in toks:
            if self.passed.get(id(sem), 0) < val:
                self.passed[id(sem)] = val
                self.items.append((sem, val))

    def op(self, fn, *waits, own=True, inc=True):
        self.wait(*waits)
        if own and self.n:
            self.wait((self.sem, self.n))
        if inc:
            self.n += 1
        self.items.append((fn, inc))
        return self.last()

    def last(self):
        return (self.sem, self.n)

    def emit(self, e):
        for a, b in self.items:
            if callable(a):
                ins = a(e)
                if b:
                    ins.then_inc(self.sem, 1)
            else:
                e.wait_ge(a, b)


class Loads:

    def __init__(self):
        self.items = []

    def start(self, dst, src, sem, count, *waits):
        for s, v in waits:
            self.items.append((s, v))
        self.items.append((lambda e: e.dma_start(dst, src), sem))
        return (sem, count)

    def emit(self, e):
        for a, b in self.items:
            if callable(a):
                a(e).then_inc(b, 16)
            else:
                e.wait_ge(a, b)


def build(nc, A, out, stages=99):
    ctx = ExitStack()
    with ctx:
        def sb(name, shape, dt=F32):
            return ctx.enter_context(nc.sbuf_tensor(name, shape, dt))

        def sem(name):
            return ctx.enter_context(nc.semaphore(name))

        RING = sb("RING", [128, NRING, 2048])
        PAR = sb("PAR", [128, NPAR])
        CB = sb("CB", [128, 384])
        H = sb("H", [128, KC, T])[:, :, :]
        NAR = 37600
        AR = sb("AR", [128, NAR])
        PS = ctx.enter_context(nc.psum_tensor("PS", [128, 8, 512], F32))

        ident = CB[:, 0:128]
        ones = CB[:, 128:256]
        blk = CB[:, 256:384]

        s_pe, s_dve, s_act, s_pool = sem("s_pe"), sem("s_dve"), sem("s_act"), sem("s_pool")
        s_ring = [sem(f"s_ring{i}") for i in range(NRING)]
        s_in = [sem(f"s_in{i}") for i in range(8)]
        s_out = sem("s_out")
        pe, dve, act, pool, sp = Engine(s_pe), Engine(s_dve), Engine(s_act), Engine(s_pool), Loads()

        def par(name, i=0, n=1, p=128):
            o = POFF[name] + i
            return PAR[0:p, o:o + n]

        top = [0]

        def ar(cols):
            o = top[0]
            top[0] += cols
            assert top[0] <= NAR, (top[0], NAR)
            return AR[:, o:o + cols]

        def ar3(a, b):
            return ar(a * b).rearrange("p (a b) -> p a b", a=a)

        def barrier():
            toks = [x.last() for x in (pe, dve, act, pool) if x.n]
            for x in (pe, dve, act, pool):
                x.wait(*toks)
            return toks

        free = [[] for _ in range(8)]
        turn = [0]

        def bank():
            b = turn[0] % 8
            turn[0] += 1
            return b

        def take(b):
            t, free[b] = free[b], []
            return t

        nload = [0]
        ring_count = [0] * NRING
        ring_free = [[] for _ in range(NRING)]

        def load(pairs):
            s = nload[0] % NRING
            nload[0] += 1
            slot = RING[:, s, :]
            waits = ring_free[s]
            for view, src in pairs:
                ring_count[s] += 16
                sp.start(view(slot), src, s_ring[s], ring_count[s], *waits)
                waits = []
            return s, slot, (s_ring[s], ring_count[s])

        def done(s, tok):
            ring_free[s] = [tok]

        def cols(W, c0, n):
            def view(slot):
                return slot[:, 0:KC * n].rearrange("p (k n) -> p k n", k=KC)
            s, slot, tok = load([(view, W[:, c0:c0 + n].rearrange("(k p) n -> p k n", p=128))])
            return s, view(slot), tok

        def rows(W, f0, nf, c0, p=128):
            def view(slot):
                return slot[0:p, 0:nf * 512].rearrange("p (k n) -> p k n", k=nf)
            s, slot, tok = load([(view, W[f0 * p:(f0 + nf) * p, c0:c0 + 512].rearrange("(k p) n -> p k n", p=p))])
            return s, view(slot), tok

        def mm(o, lhsT, rhs, start, stop, *waits, inc=False):
            return pe.op(lambda e: e.matmul(o, lhsT, rhs, start=start, stop=stop), *waits, own=False, inc=inc)

        def tr(o, i, idn, *waits, inc=False):
            return pe.op(lambda e: e.transpose(o, i, idn), *waits, own=False, inc=inc)

        def tt(eng, o, a, b, op, *waits, own=True):
            return eng.op(lambda e: e.tensor_tensor(o, a, b, op), *waits, own=own)

        def ts(eng, o, a, s1, s2, op0, op1=ALU.bypass, *waits, own=True):
            return eng.op(lambda e: e.tensor_scalar(o, a, s1, s2, op0, op1), *waits, own=own)

        def stt(o, a, s, b, op0, op1, *waits, own=True):
            return dve.op(lambda e: e.scalar_tensor_tensor(o, a, s, b, op0, op1), *waits, own=own)

        def actv(o, i, f, *waits, bias=0.0, scale=1.0, accum=None, own=True):
            if accum is None:
                return act.op(lambda e: e.activation(o, i, f, bias=bias, scale=scale), *waits, own=own)
            return act.op(lambda e: e.activation(o, i, f, bias=bias, scale=scale, accum_out=accum), *waits, own=own)

        def cp(o, i, *waits, own=True):
            return dve.op(lambda e: e.tensor_copy(o, i), *waits, own=own)

        def bc(a, shape, axis):
            return a.unsqueeze(axis).to_broadcast(shape)

        def flat(a):
            return a.rearrange("p a b -> p (a b)")

        def project(W, c0, n, X, Tn, evac, *waits, step=128):
            per = 256 // step
            pe.wait(*waits)
            i = 0
            for u0 in range(0, n, per * step):
                w = min(per * step, n - u0)
                s, wv, tok = cols(W, c0 + u0, w)
                for j0 in range(0, w, step):
                    m = min(step, w - j0)
                    b = bank()
                    o = PS[0:m, b, 0:Tn]
                    for k in range(KC):
                        t = mm(o, wv[:, k, j0:j0 + m], X[:, k, :], k == 0, k == KC - 1, tok, *take(b),
                               inc=(k == KC - 1))
                    free[b] = [evac(i, o, t)]
                    i += 1
                done(s, t)

        def contract(W, nf, X, Tn, evac, *waits, p=128):
            pe.wait(*waits)
            for half in range(2):
                bs = [bank() for _ in range(4)]
                for f0 in range(0, nf, 4):
                    n = min(4, nf - f0)
                    s, wv, tok = rows(W, f0, n, half * 512, p)
                    for f in range(n):
                        for j in range(4):
                            t = mm(PS[:, bs[j], 0:Tn], wv[:, f, j * 128:(j + 1) * 128], X[0:p, f0 + f, :],
                                   f0 + f == 0, f0 + f == nf - 1, tok, *take(bs[j]),
                                   inc=(f == n - 1 and (j == 3 or f0 + f == nf - 1)))
                            if f0 + f == nf - 1:
                                free[bs[j]] = [evac(half * 4 + j, PS[:, bs[j], 0:Tn], t)]
                    done(s, t)

        def copy_to(dst):
            def evac(i, o, t):
                if i % 2:
                    return actv(dst(i), o, ACT.Copy, t)
                return cp(dst(i), o, t)
            return evac

        def sum_rows(X, n, Tn, lhsT, *waits):
            b = bank()
            pe.wait(*waits)
            for k in range(n):
                t = mm(PS[:, b, 0:Tn], lhsT, X[:, k, :], k == 0, k == n - 1, *take(b), inc=(k == n - 1))
            return b, PS[:, b, 0:Tn], t

        def rsqrt(dst, src, scale, eps, tmp, *waits):
            t = ts(dve, tmp, src, scale, eps, MUL, ADD, *waits)
            t1 = actv(tmp, tmp, ACT.Sqrt, t)
            return t, dve.op(lambda e: e.reciprocal(dst, tmp), t1)

        def layer_norm(Z, gi, Tn, O, *waits):
            m0 = top[0]
            Q, R, R2 = ar3(KC, Tn), ar(Tn), ar(Tn)
            b, s, t = sum_rows(Z, KC, Tn, ones, *waits)
            td = stt(Z, bc(s, [128, KC, Tn], 1), -1.0 / D, Z, MUL, ADD, t)
            free[b] = [td]
            tq = actv(flat(Q), flat(Z), ACT.Square, td)
            b, s, t = sum_rows(Q, KC, Tn, ones, tq)
            t1, t2 = rsqrt(R, s, 1.0 / D, 1e-5, R2, t)
            free[b] = [t1]
            tt(dve, Z, Z, bc(R, [128, KC, Tn], 1), MUL)
            for k in range(KC):
                t = ts(dve, O[:, k, :], Z[:, k, :], par("ln_g", gi * 8 + k), par("ln_b", gi * 8 + k), MUL, ADD,
                       own=(k == 0))
            barrier()
            top[0] = m0
            return t

        t_par = sp.start(PAR[:, :], A["par"], s_in[0], 32)
        t_par = sp.start(CB[:, :], A["c_base"], s_in[0], 32)
        t_h = sp.start(flat(H[:, :, :]), A["hT"], s_in[1], 16)
        for x in (pe, dve, act):
            x.wait(t_par, t_h)

        def attention():
            m0 = top[0]
            q, k, oT = ar3(KC, T), ar3(KC, T), ar3(KC, T)
            V = ar3(3, D)
            dist = ar3(3, T)
            NP_ = 3
            S = [ar3(2, T) for _ in range(NP_)]
            Ex = [ar3(2, T) for _ in range(NP_)]
            Ac = [ar(T) for _ in range(NP_)]
            aT = [ar3(3, T) for _ in range(2)]
            st = [ar(8) for _ in range(NP_)]
            sm = ar(64)
            lam = ar(4)
            osq, rs, rs2 = ar3(1, T), ar(T), ar(T)
            t_dist = sp.start(flat(dist), A["c_dist"], s_in[2], 16)
            W = A["attn_w_in"][0]
            lv = POFF["lamv"]
            for i in range(2):
                a, b = PAR[:, lv + i * 128:lv + i * 128 + 64], PAR[:, lv + i * 128 + 64:lv + i * 128 + 128]
                tt(dve, sm, a, b, MUL)
                t = dve.op(lambda e, i=i: e.tensor_reduce(lam[:, i:i + 1], sm, AX, ADD))
            t = actv(lam[:, 0:2], lam[:, 0:2], ACT.Exp, t)
            tt(dve, lam[:, 2:3], lam[:, 1:2], lam[:, 0:1], SUB, t)
            ts(dve, lam[:, 2:3], lam[:, 2:3], -0.2, None, ADD)
            project(W, 0, D, H, T, copy_to(lambda i: q[:, i, :]))
            project(W, D, D, H, T, copy_to(lambda i: k[:, i, :]))
            for u in range(4):
                s, wv, tok = cols(W, 2 * D + u * 256, 256)
                for i, (q0, qn) in enumerate(QT):
                    b = bank()
                    for kk in range(KC):
                        t = mm(PS[0:qn, b, 0:256], H[:, kk, q0:q0 + qn], wv[:, kk, :], kk == 0, kk == KC - 1, tok,
                               *take(b), inc=(kk == KC - 1))
                    dst = V[0:qn, i, u * 256:(u + 1) * 256]
                    free[b] = [actv(dst, PS[0:qn, b, 0:256], ACT.Copy, t)]
                done(s, t)
            barrier()
            dve.wait(t_dist)
            items = [(h, i) for h in range(8) for i in range(3)]
            t_ex, t_comb, t_aT, t_trcp, t_pv = {}, {}, {}, {}, {}

            def first(n):
                h, i = items[n]
                q0, qn = QT[i]
                b = (n % 2) * 2
                slot = n % NP_
                slope = 2.0 ** (-(h + 1))
                for c in range(2):
                    t = mm(PS[0:qn, b + c, 0:T], q[64 * c:64 * c + 64, h, q0:q0 + qn], k[64 * c:64 * c + 64, h, :],
                           True, True, *take(b + c), inc=(c == 1))
                s_, e_, x_ = S[slot][0:qn], Ex[slot][0:qn], st[slot][0:qn]
                w = [t_comb[n - NP_]] if n >= NP_ else []
                t = stt(s_, bc(dist[0:qn, i, :], [qn, 2, T], 1), -slope * 8.0, PS[0:qn, b:b + 2, 0:T], MUL, ADD, t,
                        *w, *([t_ex[n - NP_]] if n >= NP_ else []))
                free[b], free[b + 1] = [t], [t]
                dve.op(lambda e: e.tensor_reduce(x_[:, 0:2], s_, AX, MAX))
                t = ts(dve, x_[:, 2:4], x_[:, 0:2], -0.125, None, MUL)
                for c in range(2):
                    t_ex[n] = actv(e_[:, c, :], s_[:, c, :], ACT.Exp, t, bias=x_[:, 2 + c:3 + c], scale=0.125,
                                   accum=x_[:, 4 + c:5 + c], own=False)

            def second(n):
                h, i = items[n]
                q0, qn = QT[i]
                slot = n % NP_
                e_, x_, a_ = Ex[slot][0:qn], st[slot][0:qn], Ac[slot][0:qn]
                dve.op(lambda e: e.reciprocal(x_[:, 6:8], x_[:, 4:6]), t_ex[n],
                       *([t_aT[n - NP_]] if n >= NP_ else []))
                ts(dve, x_[:, 7:8], x_[:, 7:8], lam[0:qn, 2:3], None, MUL)
                ts(dve, a_, e_[:, 1, :], x_[:, 7:8], None, MUL)
                t_comb[n] = stt(a_, e_[:, 0, :], x_[:, 6:7], a_, MUL, ADD)

            def third(n):
                h, i = items[n]
                q0, qn = QT[i]
                a_ = Ac[n % NP_][0:qn]
                b = 4 + n % 2
                w = take(b)
                for kt, (k0, kn) in enumerate(QT):
                    t = tr(PS[0:kn, b, kt * 128:kt * 128 + qn], a_[:, k0:k0 + kn], ident[0:qn, 0:qn], t_comb[n], *w,
                           inc=(kt == 2))
                t_aT[n] = t
                dst = aT[h % 2]
                wv = [t_pv[h - 2]] if h >= 2 else []
                src = PS[:, b, 0:384].rearrange("p (a b) -> p a b", a=3)
                actv(dst[0:96, 0:2, q0:q0 + qn], src[0:96, 0:2, 0:qn], ACT.Copy, t, *wv, own=False)
                t_trcp[n] = actv(dst[0:80, 2, q0:q0 + qn], src[0:80, 2, 0:qn], ACT.Copy, own=False)
                free[b] = [t_trcp[n]]
                if i == 2:
                    b = 6 + h % 2
                    for kt, (k0, kn) in enumerate(QT):
                        t = mm(PS[:, b, 0:T], V[0:kn, kt, h * 128:(h + 1) * 128], aT[h % 2][0:kn, kt, :], kt == 0,
                               kt == 2, t_trcp[n], *take(b), inc=(kt == 2))
                    t_pv[h] = t
                    free[b] = [cp(oT[:, h, :], PS[:, b, 0:T], t)]

            for n in range(len(items) + 2):
                if n < len(items):
                    first(n)
                if 1 <= n <= len(items):
                    second(n - 1)
                if n >= 2:
                    third(n - 2)
            barrier()
            for h in range(8):
                tq = actv(osq[:, 0, :], oT[:, h, :], ACT.Square, dve.last(), pe.last())
                b, s, t = sum_rows(osq, 1, T, ones, tq)
                t1, t2 = rsqrt(rs, s, 1.0 / 128, 1e-5, rs2, t)
                free[b] = [t1]
                tt(dve, oT[:, h, :], oT[:, h, :], rs, MUL)
                t = ts(dve, oT[:, h, :], oT[:, h, :], par("subln"), 0.8, MUL, MUL)

            def add(i, o, t):
                return stt(H[:, i, :], H[:, i, :], ALPHA, o, MUL, ADD, t)
            project(A["attn_w_o"][0], 0, D, oT, T, add, t)
            barrier()
            top[0] = m0
            layer_norm(H, 0, T, H, dve.last())

        def gated(Wg, Wu, Wd, nf, hT, tmp, evac):
            used = [None] * len(tmp)
            bars = dve.last(), act.last(), pe.last()
            pe.wait(*bars)
            act.wait(*bars)
            dve.wait(*bars)
            n = 0
            for f0 in range(0, nf, 2):
                sg, wg, tg = cols(Wg, f0 * 128, 256)
                su, wu, tu = cols(Wu, f0 * 128, 256)
                for j in range(2):
                    bg, bu = bank(), bank()
                    for k in range(KC):
                        t1 = mm(PS[:, bg, 0:T], wg[:, k, j * 128:(j + 1) * 128], H[:, k, :], k == 0, k == KC - 1, tg,
                                *take(bg), inc=(k == KC - 1))
                    for k in range(KC):
                        t2 = mm(PS[:, bu, 0:T], wu[:, k, j * 128:(j + 1) * 128], H[:, k, :], k == 0, k == KC - 1, tu,
                                *take(bu), inc=(k == KC - 1))
                    x = n % len(tmp)
                    t = actv(tmp[x], PS[:, bg, 0:T], ACT.Silu, t1, *([used[x]] if used[x] else []), own=False)
                    free[bg] = [t]
                    used[x] = tt(dve, hT[:, f0 + j, :], tmp[x], PS[:, bu, 0:T], MUL, t, t2, own=False)
                    free[bu] = [used[x]]
                    n += 1
                done(sg, t1)
                done(su, t2)
            contract(Wd, nf, hT, T, evac, dve.last())

        def ffn():
            m0 = top[0]
            hT = ar3(FFN // 128, T)
            tmp = [ar(T) for _ in range(3)]

            def add(i, o, t):
                return stt(H[:, i, :], H[:, i, :], ALPHA, o, MUL, ADD, t)
            gated(A["ffn_w_gate"][0], A["ffn_w_up"][0], A["ffn_w_down"][0], FFN // 128, hT, tmp, add)
            barrier()
            top[0] = m0
            layer_norm(H, 1, T, H, dve.last())

        def rwkv():
            m0 = top[0]
            cst = ar(NC_RW)
            t_c = sp.start(cst, A["c_rw"], s_in[3], 16, *barrier())
            r, k, v, kk = ar3(KC, T), ar3(KC, T), ar3(KC, T), ar3(KC, T)
            a = [ar3(KC, T) for _ in range(2)]
            c = [ar3(KC, T) for _ in range(2)]
            gh = ar(2 * T).rearrange("p (a b) -> p a b", a=2)
            m1 = top[0]
            dp, dn = ar3(KC, T), ar3(KC, T)
            xs = [ar3(KC, T) for _ in range(2)]
            lh = ar(T)
            lg = [ar(T) for _ in range(2)]
            tt(dve, dp[:, :, 1:T], H[:, :, 0:T - 1], H[:, :, 1:T], SUB)
            ts(dve, dp[:, :, 0:1], H[:, :, 0:1], -1.0, None, MUL, own=False)
            tt(dve, dn[:, :, 0:T - 1], H[:, :, 1:T], H[:, :, 0:T - 1], SUB, own=False)
            t = ts(dve, dn[:, :, T - 1:T], H[:, :, T - 1:T], -1.0, None, MUL, own=False)
            used = [None, None]

            def mix(i, slot):
                X = xs[slot]
                w = [used[slot]] if used[slot] else []
                for kc in range(KC):
                    stt(X[:, kc, :], dp[:, kc, :], par("mu", i * 8 + kc), H[:, kc, :], MUL, ADD, *w, own=(kc == 0))
                for kc in range(KC):
                    t = stt(X[:, kc, :], dn[:, kc, :], par("mu", 48 + i * 8 + kc), X[:, kc, :], MUL, ADD,
                            own=(kc == 0))
                return X, t

            for n, (i, dst) in enumerate([(0, r), (1, k), (2, v)]):
                X, t = mix(i, n % 2)
                project(A["rw_w_rkv"][0, i], 0, D, X, T, copy_to(lambda f, dst=dst: dst[:, f, :]), t)
                used[n % 2] = pe.last()

            def quarter(n):
                return lambda slot: slot[:, :].rearrange("p (k q r) -> p k q r", k=KC, q=4)[:, :, n, :]

            s1, w1v, tok1 = load([(quarter(n), A[nm][0, n % 2].rearrange("(k p) r -> p k r", p=128))
                                  for n, nm in enumerate(["rw_w1", "rw_w1", "rw_a1", "rw_a1"])])
            w1v = w1v.rearrange("p (k q) -> p k q", k=KC)
            s2, w2v, tok2 = load([(lambda sl: sl[:, 0:D], A["rw_w2"][0].rearrange("n r d -> (n r) d")),
                                  (lambda sl: sl[:, D:2 * D], A["rw_a2"][0].rearrange("n r d -> (n r) d"))])

            def lora(i, slot, which, func, fin):
                X, t = mix(i, slot)
                b = bank()
                for kc in range(KC):
                    t1 = mm(PS[:, b, 0:T], w1v[:, kc, which * 128:(which + 1) * 128], X[:, kc, :], kc == 0,
                            kc == KC - 1, t, tok1, *take(b), inc=(kc == KC - 1))
                used[slot] = t1
                t2 = actv(lh, PS[:, b, 0:T], func, t1, pe.last())
                free[b] = [t2]
                for f in range(KC):
                    for n in range(2):
                        b = bank()
                        t3 = mm(PS[:, b, 0:T], w2v[64 * n:64 * n + 64, which * D + f * 128:which * D + (f + 1) * 128],
                                lh[64 * n:64 * n + 64, :], True, True, t2, tok2, *take(b), inc=True)
                        free[b] = [fin(n, f, PS[:, b, 0:T], t3)]
                return t1, t3

            _, t3 = lora(3, 1, 0, ACT.Tanh, lambda n, f, o, t: actv(
                c[n][:, f, :], o, ACT.Sigmoid, t, bias=par("w0", n * 8 + f), own=False))
            t1, t3 = lora(4, 0, 1, ACT.Copy, lambda n, f, o, t: actv(
                a[n][:, f, :], o, ACT.Sigmoid, t, bias=par("a0", n * 8 + f), own=False))
            done(s1, t1)
            done(s2, t3)
            X, t = mix(5, 1)
            sg, gv, tokg = cols(A["rw_g1"][0], 0, 160)
            for j, m in enumerate([128, 32]):
                b = bank()
                for kc in range(KC):
                    t1 = mm(PS[0:m, b, 0:T], gv[:, kc, j * 128:j * 128 + m], X[:, kc, :], kc == 0, kc == KC - 1, t,
                            tokg, *take(b), inc=(kc == KC - 1))
                free[b] = [actv(gh[0:m, j, :], PS[0:m, b, 0:T], ACT.Sigmoid, t1)]
            done(sg, t1)
            barrier()
            top[0] = m1
            LD = ar3(KC, T)
            Q, RN, R2 = ar3(KC, T), ar3(KC, T), ar3(KC, T)
            dve.wait(t_c)
            g4 = [128, KC * NCH, CH]

            def by_chunk(x):
                return flat(x).rearrange("p (a b) -> p a b", b=CH)
            for n in range(2):
                ts(dve, flat(LD), flat(c[n]), -float(np.exp(-0.5)), None, MUL)
                for f in range(KC):
                    dve.op(lambda e, n=n, f=f: e.tensor_tensor_scan(
                        c[n][:, f, :], cst[:, C_SCAN:C_SCAN + T], LD[:, f, :], 0.0, MUL, ADD), own=(f == 0))
                if n == 1:
                    tt(dve, flat(LD), flat(LD), flat(c[n]), SUB)
                    x = by_chunk(c[n])
                    cp(Q[:, 0, 0:KC * NCH], x[:, :, CH - 1])
                    tt(dve, x, by_chunk(LD), bc(Q[:, 0, 0:KC * NCH], g4, 2), ADD)
            tt(dve, kk, k, bc(par("k_k", 0, 8), [128, KC, T], 2), MUL)
            tq = actv(flat(Q), flat(kk), ACT.Square, dve.last())
            for f in range(KC):
                t = mm(PS[:, f, 0:T], blk, Q[:, f, :], True, True, tq, *take(f), inc=True)
            t = ts(dve, R2, PS[:, :, 0:T], 1e-24, None, MAX, ALU.bypass, t)
            for f in range(8):
                free[f] = [t]
            t = actv(flat(R2), flat(R2), ACT.Sqrt, t)
            dve.op(lambda e: e.reciprocal(flat(RN), flat(R2)), t)
            tt(dve, flat(kk), flat(kk), flat(RN), MUL)
            barrier()
            top[0] = m1
            y = ar3(KC, T)
            St = [ar3(KC, 64) for _ in range(2)]
            NB = 2
            B = []
            for _ in range(NB):
                B.append(dict(
                    X=ar(8 * CH), XT=ar(8 * CH), W=ar(8 * CH),
                    akp=ar(8 * 2 * CH).rearrange("p (h x) -> p h x", h=8),
                    abp=ar(8 * 2 * CH).rearrange("p (h x) -> p h x", h=8),
                    ar=ar(4 * 2 * CH).rearrange("p (f x t) -> p f x t", f=4, x=2),
                    ka=ar3(4, CH), be=ar3(4, CH), e1=ar3(4, CH + 1), e2=ar3(4, CH), t1=ar3(4, CH),
                    kt=ar(512), bt=ar(512), vt=ar(512), em=ar(8)))
                w = B[-1]
                w.update(R=w["W"][:, 0:512], U=w["X"][:, 0:512], sm=flat(w["t1"])[:, 0:256].rearrange("p (f v) -> p f v", f=4))
            for n in range(2):
                t_st = dve.op(lambda e, n=n: e.memset(flat(St[n]), 0.0))
            C_I = ident[0:CH, 0:CH]

            def hd(x):
                return x.rearrange("p (h t) -> p h t", h=8)

            def lvl(d, l, tr_):
                o = C_LVL + ((d ^ tr_) * len(SCAN_LEVELS) + l) * CH
                return bc(cst[0:CH, o:o + CH], [CH, 8, CH], 1)

            groups = []
            for i in range(NCH):
                for hf in range(2):
                    groups += [(0, i, hf), (1, NCH - 1 - i, hf)]
            last_seq = {}

            def prep(g):
                d, ci, hf = groups[g]
                W = B[g % NB]
                z = 4 * (g % 2)
                f0, t0 = 4 * hf, ci * CH
                sl = (slice(None), slice(f0, f0 + 4), slice(t0, t0 + CH))
                cc, rr, kv, kkv, av, vv = c[d][sl], r[sl], k[sl], kk[sl], a[d][sl], v[sl]
                sh = [128, 4, CH]
                e1, e2, t1 = W["e1"], W["e2"], W["t1"]
                inn, prv = (slice(1, CH + 1), slice(0, CH)) if d == 0 else (slice(0, CH), slice(1, CH + 1))
                edge = 0 if d == 0 else CH
                mid = cc[:, :, MID:MID + 1]
                pre = last_seq.get(g - NB, [])
                tt(dve, e1[:, :, inn], cc, mid.to_broadcast(sh), SUB, *pre)
                t = ts(dve, e1[:, :, edge:edge + 1], mid, -1.0, None, MUL)
                actv(e2, e1[:, :, inn], ACT.Exp, t, scale=-1.0, own=False)
                actv(W["em"][:, 0:4], mid.rearrange("p a b -> p (a b)"), ACT.Exp, own=False)
                te = actv(e1, e1, ACT.Exp)
                ka_b = bc(par("k_a", f0, 4), sh, 2)
                stt(t1, av, -1.0, ka_b, ADD, MUL)
                stt(t1, t1, 1.0, kv, ADD, MUL)
                tka = tt(dve, W["ka"], t1, e2, MUL, te)
                tt(dve, t1, kkv, av, MUL)
                tt(dve, W["be"], t1, e2, MUL)
                tt(dve, W["ar"][:, :, 0, :], kkv, e1[:, :, prv], MUL, own=False)
                tf = tt(dve, W["ar"][:, :, 1, :], rr, e1[:, :, inn], MUL, own=False)
                for x, (src, dst, sc) in enumerate([(W["ka"], W["kt"], 1.0), (W["be"], W["bt"], -1.0), (vv, W["vt"], 1.0)]):
                    b = z + x
                    for f in range(4):
                        t = tr(PS[0:CH, b, f * 128:(f + 1) * 128], src[:, f, :], ident, tf, *take(b), inc=(f == 3))
                    free[b] = [actv(dst[0:CH, :], PS[0:CH, b, 0:512], ACT.Copy, t, *pre, scale=sc, own=False)]
                for x, (src, dst) in enumerate([("ka", "akp"), ("be", "abp")]):
                    for i0 in (0, 2):
                        for h in range(2 * i0, 2 * i0 + 4):
                            p0 = 64 * (h % 2)
                            bk = z + i0 + h % 2
                            t = mm(PS[0:CH, bk, (h // 2 - i0) * 136:(h // 2 - i0 + 1) * 136],
                                   W[src][p0:p0 + 64, h // 2, :],
                                   W["ar"][p0:p0 + 64, h // 2, :, :].rearrange("p x t -> p (x t)"), True, True, tf,
                                   *take(bk), inc=(h == 2 * i0 + 3))
                        o = C_AM + (2 * d + x) * 136
                        t = tt(dve, W[dst][0:CH, 2 * i0:2 * i0 + 4, :].rearrange("p (i a) x -> p a i x", a=2),
                               PS[0:CH, z + i0:z + i0 + 2, 0:272].rearrange("p a (i x) -> p a i x", i=2),
                               cst[0:CH, o:o + 136].unsqueeze(1).unsqueeze(1).to_broadcast([CH, 2, 2, 136]), MUL, t,
                               own=False)
                        free[z + i0] = free[z + i0 + 1] = [t]
                return dve.last()

            def two(z):
                return PS[0:CH, z:z + 2, 0:4 * CH].rearrange("p a (h t) -> p a h t", h=4)

            def quad(x):
                return x[0:CH].rearrange("p (a h t) -> p a h t", a=2, h=4)

            def square(o0, lhs, rhs, *waits):
                for h in range(8):
                    b = o0 + h // 4
                    t = mm(PS[0:CH, b, (h % 4) * CH:(h % 4 + 1) * CH], lhs(h), rhs(h), True, True, *waits, *take(b),
                           inc=(h == 7))
                return t

            def wide(x):
                return quad(x).rearrange("p a h t -> p a (h t)")

            def level(g, l, part, tw):
                d, ci, hf = groups[g]
                W = B[g % NB]
                z = 4 * (g % 2)
                X, XT, Wm = W["X"], W["XT"], W["W"]

                def at(x):
                    return lambda h: x[0:CH, h * CH:(h + 1) * CH]
                mb = lambda tr_: lvl(d, l, tr_)
                if part == 0:
                    rhs = at(X) if l else (lambda h: C_I)
                    t = square(z, lambda h: W["abp"][0:CH, h, 0:CH], rhs, tw)
                    for hb in range(2):
                        t2 = tt(dve, hd(Wm)[0:CH, 4 * hb:4 * hb + 4, :],
                                PS[0:CH, z + hb, 0:4 * CH].rearrange("p (h t) -> p h t", h=4),
                                mb(0)[:, 0:4, :], MUL, t, own=False)
                    free[z] = free[z + 1] = [t2]
                    if l == 0:
                        ib = bc(C_I, [CH, 8, CH], 1)
                        tt(dve, hd(X)[0:CH], ib, hd(Wm)[0:CH], SUB)
                        tt(dve, hd(XT)[0:CH], W["abp"][0:CH, :, 0:CH], mb(1), MUL, own=False)
                        t2 = tt(dve, hd(XT)[0:CH], ib, hd(XT)[0:CH], SUB)
                    return t2
                if l == 0:
                    return tw
                if l < len(SCAN_LEVELS) - 1:
                    tx = square(z + 2, at(XT), at(Wm), tw)
                t = square(z, at(Wm), at(XT), tw)
                t2 = tw
                if l < len(SCAN_LEVELS) - 1:
                    t2 = tt(dve, wide(X), wide(X), PS[0:CH, z + 2:z + 4, 0:4 * CH], SUB, t, own=False)
                    free[z + 2] = free[z + 3] = [t2]
                t3 = tt(dve, wide(XT), wide(XT), PS[0:CH, z:z + 2, 0:4 * CH], SUB, t, own=False)
                free[z] = free[z + 1] = [t3]
                return t3

            def seq(g):
                d, ci, hf = groups[g]
                W = B[g % NB]
                z = 4 * (g % 2)
                f0, t0 = 4 * hf, ci * CH
                S = St[d][:, f0:f0 + 4, :]
                sm = W["sm"]
                tsm = tt(dve, sm, S, bc(W["em"][:, 0:4], [128, 4, 64], 2), MUL, act.last())
                for h in range(8):
                    p0, f = 64 * (h % 2), h // 2
                    o = PS[0:CH, z + h % 2, f * 64:(f + 1) * 64]
                    mm(o, W["ar"][p0:p0 + 64, f, 0, :], sm[p0:p0 + 64, f, :], True, False, tsm, *take(z + h % 2))
                    t = mm(o, W["akp"][0:CH, h, 0:CH], W["vt"][0:CH, h * 64:(h + 1) * 64], False, True, inc=(h == 7))
                t = actv(W["R"][0:CH].rearrange("p (f a v) -> p a f v", a=2, v=64),
                         PS[0:CH, z:z + 2, 0:256].rearrange("p a (f v) -> p a f v", v=64), ACT.Copy, t, own=False)
                free[z] = free[z + 1] = [t]
                for h in range(8):
                    hs = slice(h * 64, (h + 1) * 64)
                    t2 = mm(PS[0:CH, z + 2, hs], W["XT"][0:CH, h * CH:(h + 1) * CH], W["R"][0:CH, hs], True, True, t,
                            *take(z + 2), inc=(h == 7))
                t = actv(W["U"][0:CH], PS[0:CH, z + 2, 0:512], ACT.Copy, t2, own=False)
                free[z + 2] = [t]
                for h in range(8):
                    p0, f = 64 * (h % 2), h // 2
                    hs = slice(h * 64, (h + 1) * 64)
                    o = PS[p0:p0 + 64, z + 3, f * 64:(f + 1) * 64]
                    mm(o, W["kt"][0:CH, hs], W["vt"][0:CH, hs], True, False, t, *take(z + 3))
                    ts_ = mm(o, W["bt"][0:CH, hs], W["U"][0:CH, hs], False, True, inc=(h == 7))
                for h in range(8):
                    p0, f = 64 * (h % 2), h // 2
                    hs = slice(h * 64, (h + 1) * 64)
                    o = PS[p0:p0 + 64, z, f * CH:(f + 1) * CH]
                    mm(o, sm[p0:p0 + 64, f, :], W["ar"][p0:p0 + 64, f, 1, :], True, False, *take(z))
                    mm(o, W["vt"][0:CH, hs], W["akp"][0:CH, h, CH:2 * CH], False, False)
                    ty = mm(o, W["U"][0:CH, hs], W["abp"][0:CH, h, CH:2 * CH], False, True, inc=(h == 7))
                end = W["e1"][:, :, CH if d == 0 else 0]
                t1 = tt(dve, sm, sm, PS[:, z + 3, 0:256].rearrange("p (f v) -> p f v", f=4), ADD, ts_, ty)
                free[z + 3] = [t1]
                tt(dve, S, sm, bc(end, [128, 4, 64], 2), MUL)
                yv = y[:, f0:f0 + 4, t0:t0 + CH]
                src = PS[:, z, 0:4 * CH].rearrange("p (f t) -> p f t", f=4)
                first = (d == 0) == (ci < NCH // 2)
                if first:
                    t2 = cp(yv, src, ty, own=False)
                else:
                    t2 = tt(dve, yv, yv, src, ADD, ty)
                free[z] = [t2]
                last_seq[g] = [t2, ty, act.last()]

            for g0 in range(0, len(groups), NB):
                gs = list(range(g0, g0 + NB))
                tw = {g: prep(g) for g in gs}
                for l in range(len(SCAN_LEVELS)):
                    for part in range(2):
                        for g in gs:
                            tw[g] = level(g, l, part, tw[g])
                for g in gs:
                    pe.wait(tw[g])
                    seq(g)
            barrier()
            top[0] = m1 + KC * T
            Q, G, E2 = ar3(KC, T), ar3(KC, T), ar3(KC, T)
            sh = [128, KC, T]

            def heads(X, t):
                for f in range(KC):
                    t2 = mm(PS[:, f, 0:T], blk, X[:, f, :], True, True, t, *take(f), inc=(f == KC - 1))
                return t2

            def freed(t):
                for f in range(8):
                    free[f] = [t]
                return t
            t = heads(y, dve.last())
            t = freed(stt(y, PS[:, :, 0:T], -1.0 / 64, y, MUL, ADD, t))
            t = actv(flat(Q), flat(y), ACT.Square, t)
            t = heads(Q, t)
            t = freed(ts(dve, G, PS[:, :, 0:T], 1.0 / 64, 64e-5, MUL, ADD, t))
            t = actv(flat(G), flat(G), ACT.Sqrt, t)
            dve.op(lambda e: e.reciprocal(flat(E2), flat(G)), t)
            tt(dve, flat(y), flat(y), flat(E2), MUL)
            tt(dve, y, y, bc(par("lnx_g", 0, 8), sh, 2), MUL)
            tt(dve, y, y, bc(par("lnx_b", 0, 8), sh, 2), ADD)
            tt(dve, flat(Q), flat(a[0]), flat(a[1]), ADD)
            stt(Q, Q, -2.0, bc(par("k_a", 0, 8), sh, 2), ADD, MUL)
            stt(flat(Q), flat(Q), 2.0, flat(k), ADD, MUL)
            tt(dve, flat(Q), flat(Q), flat(r), MUL)
            t = tt(dve, Q, Q, bc(par("r_k", 0, 8), sh, 2), MUL)
            t = heads(Q, t)
            t = freed(tt(dve, Q, v, PS[:, :, 0:T], MUL, t))
            tt(dve, flat(y), flat(y), flat(Q), ADD)
            s, slot, tok = load([(lambda sl: sl[:, 0:D], A["rw_g2"][0, 0:128, :]),
                                 (lambda sl: sl[0:32, D:2 * D], A["rw_g2"][0, 128:160, :])])
            for f in range(KC):
                w = take(f)
                mm(PS[:, f, 0:T], slot[:, f * 128:(f + 1) * 128], gh[:, 0, :], True, False, tok, *w)
                t = mm(PS[:, f, 0:T], slot[0:32, D + f * 128:D + (f + 1) * 128], gh[0:32, 1, :], False, True, inc=True)
            done(s, t)
            t = freed(tt(dve, y, y, PS[:, :, 0:T], MUL, t))

            def add(i, o, t):
                return stt(H[:, i, :], H[:, i, :], ALPHA, o, MUL, ADD, t)
            project(A["rw_w_o"][0], 0, D, y, T, add, t)
            barrier()
            top[0] = m0
            layer_norm(H, 2, T, H, dve.last())

        def moe():
            m0 = top[0]
            hT = ar3(FE // 128, T)
            tmp = [ar(T) for _ in range(3)]
            acc, GB = ar3(KC, T), ar3(KC, T)
            gt = ar(T)
            sc = [ar(64) for _ in range(3)]
            ws, wr, tok = cols(A["moe_w_router"][0], 0, NE)
            for i, (q0, qn) in enumerate(QT):
                b = bank()
                x = sc[i][0:qn]
                for kc in range(KC):
                    t = mm(PS[0:qn, b, 0:NE], H[:, kc, q0:q0 + qn], wr[:, kc, :], kc == 0, kc == KC - 1, tok,
                           dve.last(), *take(b), inc=(kc == KC - 1))
                free[b] = [tt(dve, x[:, 0:8], PS[0:qn, b, 0:NE], par("b_router", 0, 8, qn), ADD, t)]
                dve.op(lambda e, x=x: e.max(x[:, 8:16], x[:, 0:8]))
                t = ts(dve, x[:, 16:17], x[:, 8:9], -1.0, None, MUL)
                t = actv(x[:, 24:32], x[:, 0:8], ACT.Exp, t, bias=x[:, 16:17], accum=x[:, 17:18])
                dve.op(lambda e, x=x: e.reciprocal(x[:, 18:19], x[:, 17:18]), t)
                ts(dve, x[:, 24:32], x[:, 24:32], x[:, 18:19], None, MUL)
                dve.op(lambda e, x=x: e.max(x[:, 32:40], x[:, 24:32]))
                tt(dve, x[:, 19:20], x[:, 32:33], x[:, 33:34], ADD)
                dve.op(lambda e, x=x: e.reciprocal(x[:, 20:21], x[:, 19:20]))
                cp(x[:, 40:42], x[:, 32:34])
                dve.op(lambda e, x=x: e.memset(x[:, 42:48], -2.0))
                dve.op(lambda e, x=x: e.match_replace(x[:, 48:56], x[:, 40:48], x[:, 24:32], -1.0))
                ts(dve, x[:, 48:56], x[:, 48:56], -1.0, x[:, 20:21], ALU.is_equal, MUL)
                t = tt(dve, x[:, 56:64], x[:, 48:56], x[:, 24:32], MUL)
                b = bank()
                t = tr(PS[0:NE, b, 0:qn], x[:, 56:64], ident[0:qn, 0:qn], t, *take(b), inc=True)
                t = cp(gt[0:NE, q0:q0 + qn], PS[0:NE, b, 0:qn], t)
                free[b] = [t]
            done(ws, pe.last())
            for e_ in range(NE):
                b = bank()
                t = mm(PS[:, b, 0:T], ident[0:NE, e_:e_ + 1].to_broadcast([NE, 128]), gt[0:NE, :], True, True, t,
                       *take(b), inc=True)
                t = cp(GB[:, e_, :], PS[:, b, 0:T], t)
                free[b] = [t]
            for e_ in range(NE):
                def add(i, o, t, e_=e_):
                    if e_ == 0:
                        return tt(dve, acc[:, i, :], GB[:, e_, :], o, MUL, t)
                    x = tmp[0]
                    t = tt(dve, x, GB[:, e_, :], o, MUL, t)
                    tt(dve, acc[:, i, :], acc[:, i, :], x, ADD)
                    return t
                gated(A["moe_w_gate"][0, e_], A["moe_w_up"][0, e_], A["moe_w_down"][0, e_], FE // 128, hT, tmp, add)
            stt(flat(H[:, :, :]), flat(H[:, :, :]), ALPHA, flat(acc), MUL, ADD)
            barrier()
            top[0] = m0
            layer_norm(H, 3, T, H, dve.last())

        B2 = {}

        def tables():
            cst = ar(NC_B2)
            pos = ar(SEQ)
            bars = barrier()
            t_c = sp.start(cst, A["c_b2"], s_in[4], 32, *bars)
            t_c = sp.start(pos.bitcast(I32), A["pos"], s_in[4], 32)
            B2.update(rot=[cst[:, 0:128], cst[:, 128:256]], causal=cst[:, 256:768].rearrange("p (a b) -> p a b", a=2))
            pf, y, kf = ar(SEQ), ar(SEQ), ar(SEQ)
            B2["cs"] = [(ar(SEQ), ar(SEQ)) for _ in range(2)]
            cp(pf, pos.bitcast(I32), t_c)
            c1 = 6.28125
            c2 = float(np.float32(round((TWO_PI - c1) * 2 ** 20) / 2 ** 20))
            c3 = float(TWO_PI - c1 - c2)
            for i in range(2):
                co, si = B2["cs"][i]
                ts(dve, y, pf, cst[:, 768 + i:769 + i], None, MUL)
                ts(dve, kf, y, float(1.0 / TWO_PI), None, MUL)
                ts(dve, kf, kf, 12582912.0, None, ADD)
                ts(dve, kf, kf, -12582912.0, None, ADD)
                for cc in (c1, c2, c3):
                    stt(y, kf, -cc, y, MUL, ADD)
                ts(dve, y, y, 3.1415925, -3.1415925, ALU.min, MAX)
                t = ts(dve, co, y, -1.0, None, MUL)
                tt(dve, co, co, y, MAX)
                t = ts(dve, co, co, -1.0, float(np.pi / 2), MUL, ADD)
                actv(si, y, ACT.Sin, t)
                t = actv(co, co, ACT.Sin)
                dve.wait(t)

        X2 = H[:, :, NMETA:T]

        def rms(O, gain, *waits):
            m0 = top[0]
            Q, R, R2 = ar3(KC, SEQ), ar(SEQ), ar(SEQ)
            tq = actv(Q, X2, ACT.Square, *waits)
            b, s, t = sum_rows(Q, KC, SEQ, ones, tq)
            t1, t2 = rsqrt(R, s, 1.0 / D, 1e-6, R2, t)
            free[b] = [t1]
            tt(dve, Q, X2, bc(R, [128, KC, SEQ], 1), MUL)
            t = tt(dve, O, Q, bc(gain, [128, KC, SEQ], 2), MUL)
            top[0] = m0
            return t

        def second(l):
            m0 = top[0]
            W = A["w_in_2"][l]
            o_q, o_k, o_v, o_ga, o_iq, o_ik, o_xr, o_gr, o_ma, o_mb = (
                0, 1024, 2048, 3072, 4096, 5120, 5200, 6608, 8016, 9040)
            hn = ar3(KC, SEQ)
            M = ar3(KC, SEQ)
            MA = ar3(KC, SEQ)
            m1 = top[0]
            barrier()
            t_hn = rms(hn, par("norm_g", l * 8, 8), dve.last())
            barrier()

            def evac_act(dst, func):
                return lambda i, o, t: actv(dst(i), o, func, t, own=False)

            XR = ar3(NRB, SEQ + 3)
            GR, CX, RR, II, HR = [ar3(NRB, SEQ) for _ in range(5)]
            AA = flat(XR)[:, 0:NRB * SEQ].rearrange("p (a b) -> p a b", a=NRB)
            spv = ar(NRB * 6).rearrange("p (a b) -> p a b", a=6)[0:RB]
            XR_, GR_, CX_, RR_, II_, HR_, AA_ = [x[0:RB] for x in (XR, GR, CX, RR, II, HR, AA)]
            dve.op(lambda e: e.memset(XR_[:, :, 0:3], 0.0))
            lamp = par("lam", l * NRB, NRB, RB)
            e0, ab, u1, mk, ln, nsp = [spv[:, i, :] for i in range(6)]
            ts(dve, ab, lamp, -1.0, None, MUL)
            t = tt(dve, ab, ab, lamp, ALU.min)
            t = actv(e0, ab, ACT.Exp, t)
            t = ts(dve, u1, e0, 1.0, None, ADD, ALU.bypass, t)
            t = actv(ln, u1, ACT.Ln, t)
            ts(dve, u1, u1, -1.0, None, ADD, ALU.bypass, t)
            ts(dve, mk, u1, 0.0, None, ALU.is_equal)
            tt(dve, u1, u1, mk, ADD)
            tt(dve, ln, ln, mk, ADD)
            dve.op(lambda e: e.reciprocal(u1, u1))
            tt(dve, ln, ln, u1, MUL)
            tt(dve, ln, ln, e0, MUL)
            ts(dve, mk, lamp, -1.0, 0.0, MUL, MAX)
            tt(dve, nsp, ln, mk, ADD)
            ts(dve, nsp, nsp, -8.0, None, MUL)
            project(W, o_xr, RB * NRB, hn, SEQ, lambda i, o, t: cp(XR_[:, i, 3:SEQ + 3], o, t, own=False), step=RB)
            for n in range(NRB):
                cw = lambda i: par("conv_w", (l * 4 + i) * NRB + n, 1, RB)
                ts(dve, CX_[:, n, :], XR_[:, n, 0:SEQ], cw(0), par("conv_b", l * NRB + n, 1, RB), MUL, ADD)
            for i in range(1, 4):
                for n in range(NRB):
                    t_cx = stt(CX_[:, n, :], XR_[:, n, i:i + SEQ], par("conv_w", (l * 4 + i) * NRB + n, 1, RB),
                               CX_[:, n, :], MUL, ADD, own=(n == 0))
            project(W, o_gr, RB * NRB, hn, SEQ, evac_act(lambda i: GR_[:, i, :], ACT.Silu), step=RB)
            pe.wait(t_cx)
            for nm, dst, bn in (("w_rg_2", RR_, "b_rg"), ("w_ig_2", II_, "b_ig")):
                def view(slot):
                    return slot[0:RB, 0:NRB * RB].rearrange("p (n d) -> p n d", n=NRB)
                s, slot, tok = load([(view, A[nm][l].rearrange("n c d -> c n d"))])
                for n in range(NRB):
                    b = bank()
                    t = mm(PS[0:RB, b, 0:SEQ], view(slot)[:, n, :], CX_[:, n, :], True, True, tok, *take(b), inc=True)
                    free[b] = [actv(dst[:, n, :], PS[0:RB, b, 0:SEQ], ACT.Sigmoid, t,
                                    bias=par(bn, l * NRB + n, 1, RB), own=False)]
                done(s, t)
            t_ri = act.last()
            project(W, o_ma, D, hn, SEQ, evac_act(lambda i: MA[:, i, :], ACT.Sigmoid))
            project(W, o_mb, D, hn, SEQ, evac_act(lambda i: M[:, i, :], ACT.Sigmoid))
            t = tt(dve, RR_, RR_, bc(nsp, [RB, NRB, SEQ], 2), MUL, t_ri)
            t = actv(flat(AA_), flat(RR_), ACT.Exp, t)
            t = actv(flat(RR_), flat(RR_), ACT.Tanh, scale=-1.0)
            tt(dve, flat(HR_), flat(AA_), flat(AA_), MUL, t)
            t = stt(flat(HR_), flat(HR_), 1.0, flat(RR_), ADD, MUL)
            t = actv(flat(HR_), flat(HR_), ACT.Sqrt, t)
            tt(dve, flat(II_), flat(II_), flat(CX_), MUL)
            tt(dve, flat(II_), flat(II_), flat(HR_), MUL, t)
            dve.op(lambda e: e.memset(AA_[:, :, 0:1], 0.0))
            dve.op(lambda e: e.tensor_tensor_scan(flat(HR_), flat(AA_), flat(II_), 0.0, MUL, ADD))
            t = tt(dve, flat(HR_), flat(HR_), flat(GR_), MUL, act.last())
            contract(A["w_out_rnn_2"][l], NRB, HR, SEQ, lambda i, o, t: tt(dve, M[:, i, :], M[:, i, :], o, MUL, t),
                     t, p=RB)
            barrier()
            top[0] = m1

            q, k, iq, GA = [ar3(KC, SEQ) for _ in range(4)]
            V = ar3(2, D)
            ik, iw = ar(SEQ), ar(32).rearrange("p (a b) -> p a b", a=2)
            raw = ar3(KC, SEQ)
            t1 = ar3(KC, SEQ)

            def rotate(dst, i, n):
                co, si = B2["cs"][i]
                t = barrier()
                nb = (n + 1) // 2
                for f in range(n):
                    t = mm(PS[:, f // 2, (f % 2) * 256:(f % 2 + 1) * 256], B2["rot"][i], raw[:, f, :], True, True,
                           *take(f // 2), inc=(f == n - 1))
                x = PS[:, 0:nb, :].rearrange("p b (c t) -> p (b c) t", c=2)[:, 0:n, :]
                sh = [128, n, SEQ]
                t = tt(dve, t1[:, 0:n, :], x, bc(si, sh, 1), MUL, t)
                for b in range(nb):
                    free[b] = [t]
                tt(dve, raw[:, 0:n, :], raw[:, 0:n, :], bc(co, sh, 1), MUL)
                t = tt(dve, dst, raw[:, 0:n, :], t1[:, 0:n, :], ADD)
                pe.wait(t)
                act.wait(t)

            for o, dst, i in ((o_q, q, 0), (o_k, k, 0), (o_iq, iq, 1)):
                project(W, o, D, hn, SEQ, copy_to(lambda f: raw[:, f, :]))
                rotate(dst, i, KC)
            s, slot, tok = load([
                (lambda sl, c=c, n=n: sl[:, 0:KC * 144].rearrange("p (k n) -> p k n", k=KC)[:, :, c:c + n],
                 W[:, o:o + n].rearrange("(k p) n -> p k n", p=128))
                for c, o, n in ((0, o_ik, 64), (64, o_ik, 80))])
            wv = slot[:, 0:KC * 144].rearrange("p (k n) -> p k n", k=KC)
            b = bank()
            for kc in range(KC):
                t = mm(PS[:, b, 0:SEQ], wv[:, kc, 0:128], hn[:, kc, :], kc == 0, kc == KC - 1, tok, *take(b),
                       inc=(kc == KC - 1))
            free[b] = [cp(raw[:, 0, :], PS[:, b, 0:SEQ], t)]
            for i in range(2):
                b = bank()
                for kc in range(KC):
                    t = mm(PS[:, b, 0:16], hn[:, kc, i * 128:(i + 1) * 128], wv[:, kc, 128:144], kc == 0, kc == KC - 1,
                           *take(b), inc=(kc == KC - 1))
                free[b] = [ts(dve, iw[:, i, :], PS[:, b, 0:16], 1.0 / 32, None, MUL, ALU.bypass, t)]
            done(s, t)
            rotate(ik.unsqueeze(1), 1, 1)
            for u in range(4):
                s, wv, tok = cols(W, o_v + u * 256, 256)
                for i in range(2):
                    b = bank()
                    for kc in range(KC):
                        t = mm(PS[:, b, 0:256], hn[:, kc, i * 128:(i + 1) * 128], wv[:, kc, :], kc == 0, kc == KC - 1,
                               tok, *take(b), inc=(kc == KC - 1))
                    free[b] = [cp(V[:, i, u * 256:(u + 1) * 256], PS[:, b, 0:256], t)]
                done(s, t)
            project(W, o_ga, D, hn, SEQ, evac_act(lambda i: GA[:, i, :], ACT.Silu))
            barrier()
            score, work, bias = [ar3(2, SEQ) for _ in range(3)]
            rel = [ar(SEQ) for _ in range(4)]
            m8 = ar(16)
            used = [None] * 4
            for i in range(2):
                nk = 128 * (i + 1)
                for h in range(16):
                    p0 = 64 * (h % 2)
                    b = bank()
                    t = mm(PS[:, b, 0:nk], iq[p0:p0 + 64, h // 2, i * 128:(i + 1) * 128], ik[p0:p0 + 64, 0:nk], True,
                           True, *take(b), inc=True)
                    x = rel[h % 4][:, 0:nk]
                    t = actv(x, PS[:, b, 0:nk], ACT.Relu, t, *([used[h % 4]] if used[h % 4] else []), own=False)
                    free[b] = [t]
                    o = score[:, i, 0:nk]
                    if h == 0:
                        t = ts(dve, o, x, iw[:, i, h:h + 1], None, MUL, ALU.bypass, t)
                    else:
                        t = stt(o, x, iw[:, i, h:h + 1], o, MUL, ADD, t)
                    used[h % 4] = t
            for i in range(2):
                nk = 128 * (i + 1)
                o, w, ca = score[:, i, 0:nk], work[:, i, 0:nk], B2["causal"][:, i, 0:nk]
                tt(dve, w, o, ca, ADD)
                for r in range(8):
                    mx = m8[:, 8 * (r % 2):8 * (r % 2) + 8]
                    dve.op(lambda e, mx=mx, w=w: e.max(mx, w))
                    dve.op(lambda e, mx=mx, w=w: e.match_replace(w, mx, w, TAKEN))
                ts(dve, w, w, TAKEN, -NEG, ALU.is_equal, MUL)
                stt(bias[:, i, 0:nk], w, NEG, ca, ADD, ADD)
            NP_ = 4
            S = [ar(SEQ) for _ in range(NP_)]
            Ex = [ar(SEQ) for _ in range(NP_)]
            st = [ar(4) for _ in range(NP_)]
            pT = [ar3(2, 128) for _ in range(2)]
            oT = raw
            items = [(h, i) for h in range(8) for i in range(2)]
            t_ex, t_nrm, t_tr, t_pc, t_pv = {}, {}, {}, {}, {}
            SC = float(128 ** -0.5)

            def first(n):
                h, i = items[n]
                nk = 128 * (i + 1)
                b = n % 3
                t = mm(PS[:, b, 0:nk], q[:, h, i * 128:(i + 1) * 128], k[:, h, 0:nk], True, True, *take(b), inc=True)
                s_, x_ = S[n % NP_][:, 0:nk], st[n % NP_]
                w = [t_ex[n - NP_]] if n >= NP_ else []
                t = tt(dve, s_, PS[:, b, 0:nk], bias[:, i, 0:nk], ADD, t, *w)
                free[b] = [t]
                dve.op(lambda e: e.tensor_reduce(x_[:, 0:1], s_, AX, MAX))
                t = ts(dve, x_[:, 1:2], x_[:, 0:1], -SC, None, MUL)
                w = [t_nrm[n - NP_], t_tr[n - NP_]] if n >= NP_ else []
                t_ex[n] = actv(Ex[n % NP_][:, 0:nk], s_, ACT.Exp, t, *w, bias=x_[:, 1:2], scale=SC,
                               accum=x_[:, 2:3], own=False)

            def second_(n):
                h, i = items[n]
                nk = 128 * (i + 1)
                e_, x_ = Ex[n % NP_][:, 0:nk], st[n % NP_]
                dve.op(lambda e: e.reciprocal(x_[:, 3:4], x_[:, 2:3]), t_ex[n])
                t_nrm[n] = ts(dve, e_, e_, x_[:, 3:4], None, MUL)

            def third(n):
                h, i = items[n]
                e_ = Ex[n % NP_]
                b = 3 + n % 2
                w = take(b)
                for kt in range(i + 1):
                    t = tr(PS[:, b, kt * 128:(kt + 1) * 128], e_[:, kt * 128:(kt + 1) * 128], ident, t_nrm[n], *w,
                           inc=(kt == i))
                t_tr[n] = t
                p_ = pT[n % 2]
                t = actv(flat(p_)[:, 0:128 * (i + 1)], PS[:, b, 0:128 * (i + 1)], ACT.Copy, t,
                         *([t_pv[n - 2]] if n >= 2 else []), own=False)
                free[b] = [t]
                b = 5 + n % 3
                for kt in range(i + 1):
                    t = mm(PS[:, b, 0:128], V[:, kt, h * 128:(h + 1) * 128], p_[:, kt, :], kt == 0, kt == i, t,
                           *take(b), inc=(kt == i))
                t_pv[n] = t
                g = GA[:, h, i * 128:(i + 1) * 128]
                free[b] = [tt(dve, oT[:, h, i * 128:(i + 1) * 128], PS[:, b, 0:128], g, MUL, t, own=False)]

            for n in range(len(items) + 2):
                if n < len(items):
                    first(n)
                if 1 <= n <= len(items):
                    second_(n - 1)
                if n >= 2:
                    third(n - 2)
            barrier()
            tmp = [ar(SEQ) for _ in range(2)]

            def merge(i, o, t):
                x = tmp[i % 2]
                t = tt(dve, x, MA[:, i, :], o, MUL, t)
                tt(dve, M[:, i, :], M[:, i, :], x, ADD)
                return t
            project(A["w_out_attn_2"][l], 0, D, oT, SEQ, merge)

            def residual(i, o, t):
                return tt(dve, X2[:, i, :], X2[:, i, :], o, ADD, t)
            project(A["w_o_2"][l], 0, D, M, SEQ, residual, dve.last())
            barrier()
            top[0] = m0

        def final():
            O = ar3(KC, SEQ)
            t = rms(O, par("final_g", 0, 8), dve.last())
            B2["out"] = O

        stage_list = [attention, ffn, rwkv, moe, tables, lambda: second(0), lambda: second(1), final]
        for st_ in stage_list[:stages]:
            st_()
        toks = [x.last() for x in (pe, dve, act, pool) if x.n]
        src = B2["out"] if stages > 7 else H
        fin = sp.start(out, src, s_out, 16, *toks)
        sp.items.append(fin)

        block = ctx.enter_context(nc.Block())

        @block.sync
        def _(e):
            sp.emit(e)

        @block.tensor
        def _(e):
            pe.emit(e)

        @block.vector
        def _(e):
            dve.emit(e)

        @block.scalar
        def _(e):
            act.emit(e)

        @block.gpsimd
        def _(e):
            pool.emit(e)


def constants():
    f = np.float32
    base = np.zeros((128, 384), f)
    base[:, 0:128] = np.eye(128)
    base[:, 128:256] = 1.0
    base[0:64, 256:320] = 1.0
    base[64:128, 320:384] = 1.0
    dist = np.zeros((128, 3, T), f)
    for i, (q0, qn) in enumerate(QT):
        dist[0:qn, i, :] = np.abs(np.arange(q0, q0 + qn)[:, None] - np.arange(T)[None, :])
    rw = np.zeros((128, NC_RW), f)
    rw[:, C_SCAN:C_SCAN + T] = (np.arange(T) % CH != 0)
    i = np.arange(CH)
    for l, s in enumerate(SCAN_LEVELS):
        same = (i[:, None] // (2 * s)) == (i[None, :] // (2 * s))
        low = same & (i[:, None] % (2 * s) >= s) & (i[None, :] % (2 * s) < s)
        for x, m in enumerate([low, low.T]):
            o = C_LVL + (x * len(SCAN_LEVELS) + l) * CH
            rw[0:CH, o:o + CH] = m
    for d in range(2):
        j, t = i[:, None], i[None, :]
        strict, incl = (j < t, j <= t) if d == 0 else (j > t, j >= t)
        for x in range(2):
            o = C_AM + (2 * d + x) * 2 * CH
            rw[0:CH, o:o + CH] = strict
            rw[0:CH, o + CH:o + 2 * CH] = incl * (-1.0 if x else 1.0)
    b2 = np.zeros((128, NC_B2), f)
    for x, half in enumerate((64, 32)):
        for m in range(128):
            if m % (2 * half) < half:
                b2[m + half, x * 128 + m] = -1.0
            else:
                b2[m - half, x * 128 + m] = 1.0
        dim = 2 * half
        inv = np.float32(10000.0) ** (-np.arange(0, dim, 2, dtype=f) / np.float32(dim))
        b2[:, 768 + x] = inv[np.arange(128) % half]
    for x in range(2):
        qp = x * 128 + np.arange(128)
        b2[:, 256 + x * 256:512 + x * 256] = np.where(np.arange(SEQ)[None, :] <= qp[:, None], 0.0, NEG)
    return {"c_b2": b2, "c_base": base, "c_dist": dist.reshape(128, 3 * T), "c_rw": rw}


def by_partition(v, p=128):
    return np.ascontiguousarray(v.reshape(-1, p).T)


def lay_out(inputs):
    g = {k: np.asarray(v) for k, v in inputs.items()}
    par = np.zeros((128, NPAR), np.float32)

    def put(name, m):
        o = POFF[name]
        par[0:m.shape[0], o:o + m.shape[1]] = m
    for name, src in (("ln_g", "ln_g"), ("ln_b", "ln_b"), ("subln", "attn_subln_g"), ("mu", "rw_mu"), ("w0", "rw_w0"),
                      ("a0", "rw_a0"), ("k_k", "rw_k_k"), ("k_a", "rw_k_a"), ("r_k", "rw_r_k"),
                      ("lnx_g", "rw_lnx_g"), ("lnx_b", "rw_lnx_b"), ("norm_g", "norm_g_2"), ("final_g", "final_g_2")):
        put(name, by_partition(g[src]))
    for name, src in (("conv_w", "conv_w_2"), ("conv_b", "conv_b_2"), ("b_rg", "b_rg_2"), ("b_ig", "b_ig_2"),
                      ("lam", "lru_lambda_2")):
        put(name, by_partition(g[src], RB))
    lam = np.concatenate([g[n].reshape(-1) for n in ("attn_lam_q1", "attn_lam_k1", "attn_lam_q2", "attn_lam_k2")])
    put("lamv", np.broadcast_to(lam, (128, 256)))
    put("b_router", np.broadcast_to(g["moe_b_router"].reshape(-1), (128, NE)))
    h = np.concatenate([g["meta"], g["x"][0]], 0)
    hT = h.T.reshape(KC, 128, T).transpose(1, 0, 2).reshape(128, KC * T)
    arrays = {"par": par, "hT": np.ascontiguousarray(hT)}
    arrays["pos"] = np.ascontiguousarray(np.broadcast_to(g["positions_2"].reshape(1, SEQ), (128, SEQ)))
    arrays.update(constants())
    for n in BIG:
        arrays[n] = np.ascontiguousarray(g[n])
    return arrays


BIG = ["attn_w_in", "attn_w_o", "ffn_w_gate", "ffn_w_up", "ffn_w_down", "rw_w_rkv", "rw_w1", "rw_w2", "rw_a1", "rw_a2",
       "rw_g1", "rw_g2", "rw_w_o", "moe_w_router", "moe_w_gate", "moe_w_up", "moe_w_down",
       "w_in_2", "w_rg_2", "w_ig_2", "w_out_attn_2", "w_out_rnn_2", "w_o_2"]


def kernel(**inputs):
    import concourse.bacc as bacc
    from concourse.bass_utils import run_bass_kernel_spmd

    arrays = lay_out(inputs)
    nc = bacc.Bacc("TRN2", target_bir_lowering=False, num_devices=1)
    A = {n: nc.dram_tensor(f"in_{n}", a.shape, mybir.dt.from_np(a.dtype), kind="ExternalInput").ap()
         for n, a in arrays.items()}
    out = nc.dram_tensor("out_dram", (128, KC, SEQ), F32, kind="ExternalOutput").ap()
    build(nc, A, out)
    r = run_bass_kernel_spmd(nc, [{f"in_{n}": a for n, a in arrays.items()}], core_ids=[0])
    o = r.results[0]["out_dram"]
    return np.ascontiguousarray(o.transpose(2, 1, 0).reshape(1, SEQ, D))
```

```python
import concourse.bass as bass
from concourse import mybir
from contextlib import ExitStack
import numpy as np

F32 = mybir.dt.float32
I32 = mybir.dt.int32
ALU = mybir.AluOpType
ACT = mybir.ActivationFunctionType
AX = mybir.AxisListType.X
MUL, ADD, SUB, MAX = ALU.mult, ALU.add, ALU.subtract, ALU.max

D = 1024
KC = 8
NMETA = 16
SEQ = 256
T = NMETA + SEQ
ALPHA = 4.0 ** 0.25
QT = [(0, 96), (96, 96), (192, 80)]
CH = 55
NCH = 5
TS = 284
MID = CH // 2
NRING = 4
NMORE = 6
CAP = 96
NEG = -1.0e30
SKIP = None
TAKEN = -3.0e38
FFN = 2816
FE = 3584
NE = 8
RB = 88
NRB = 16
SCAN_LEVELS = [1, 2, 4, 8, 16, 32]
TWO_PI = 2.0 * np.pi

PARAMS = [("ln_g", 32), ("ln_b", 32), ("subln", 1), ("mu", 96), ("w0", 16), ("a0", 16), ("k_k", 8), ("k_a", 8),
          ("r_k", 8), ("lnx_g", 8), ("lnx_b", 8), ("norm_g", 16), ("final_g", 8), ("conv_w", 128),
          ("conv_b", 32), ("b_rg", 32), ("b_ig", 32), ("lam", 32), ("lamv", 256), ("b_router", 8)]
POFF = {}
_o = 0
for _n, _w in PARAMS:
    POFF[_n] = _o
    _o += _w
NPAR = _o

C_SCAN = 0
C_LVL = C_SCAN + TS
C_AM = C_LVL + 2 * len(SCAN_LEVELS) * 64
NC_RW = C_AM + 4 * 128
NC_B2 = 256 + 512 + 2


class Engine:

    def __init__(self, sem):
        self.sem, self.n, self.items, self.passed = sem, 0, [], {}

    def wait(self, *toks):
        for sem, val in toks:
            if self.passed.get(id(sem), 0) < val:
                self.passed[id(sem)] = val
                self.items.append((sem, val))

    def op(self, fn, *waits, own=True, inc=True):
        self.wait(*waits)
        if own and self.n:
            self.wait((self.sem, self.n))
        if inc:
            self.n += 1
        self.items.append((fn, inc))
        return self.last()

    def last(self):
        return (self.sem, self.n)

    def emit(self, e, items=None):
        for it in self.items if items is None else items:
            a, b = it[0], it[1]
            if a == "branch":
                flag = e.value_load(b)
                with e.If(flag != 0):
                    self.emit(e, it[2])
                with e.Else():
                    self.emit(e, it[3])
            elif callable(a):
                ins = a(e)
                if b:
                    ins.then_inc(self.sem, 1)
            else:
                e.wait_ge(a, b)


class Loads:

    def __init__(self):
        self.items = []

    def start(self, dst, src, sem, count, *waits):
        for s, v in waits:
            self.items.append((s, v))
        self.items.append((lambda e: e.dma_start(dst, src), sem))
        return (sem, count)

    def emit(self, e, items=None):
        for it in self.items if items is None else items:
            a, b = it[0], it[1]
            if a == "branch":
                flag = e.value_load(b)
                with e.If(flag != 0):
                    self.emit(e, it[2])
                with e.Else():
                    self.emit(e, it[3])
            elif callable(a):
                a(e).then_inc(b, 16)
            else:
                e.wait_ge(a, b)


def build(nc, A, out, stages=99):
    ctx = ExitStack()
    with ctx:
        def sb(name, shape, dt=F32):
            return ctx.enter_context(nc.sbuf_tensor(name, shape, dt))

        def sem(name):
            return ctx.enter_context(nc.semaphore(name))

        RING = sb("RING", [128, NRING, 2048])
        PAR = sb("PAR", [128, NPAR])
        CB = sb("CB", [128, 448])
        H = sb("H", [128, KC, T])[:, :, :]
        flag = sb("flag", [128, 1], I32)[:, :]
        NAR = 39856
        AR = sb("AR", [128, NAR])
        PS = ctx.enter_context(nc.psum_tensor("PS", [128, 8, 512], F32))

        ident = CB[:, 0:128]
        ones = CB[:, 128:256]
        blk = CB[:, 256:384]

        s_pe, s_dve, s_act, s_pool = sem("s_pe"), sem("s_dve"), sem("s_act"), sem("s_pool")
        s_ring = [sem(f"s_ring{i}") for i in range(NRING + NMORE)]
        s_in = [sem(f"s_in{i}") for i in range(8)]
        s_out = sem("s_out")
        s_move = sem("s_move")
        nmove = [0]
        pe, dve, act, pool, sp = Engine(s_pe), Engine(s_dve), Engine(s_act), Engine(s_pool), Loads()

        def par(name, i=0, n=1, p=128):
            o = POFF[name] + i
            return PAR[0:p, o:o + n]

        top = [0]

        def ar(cols):
            o = top[0]
            top[0] += cols
            assert top[0] <= NAR, (top[0], NAR)
            return AR[:, o:o + cols]

        def ar3(a, b):
            return ar(a * b).rearrange("p (a b) -> p a b", a=a)

        def barrier():
            toks = [x.last() for x in (pe, dve, act, pool) if x.n]
            for x in (pe, dve, act, pool):
                x.wait(*toks)
            return toks

        free = [[] for _ in range(8)]
        turn = [0]

        def bank():
            b = turn[0] % 8
            turn[0] += 1
            return b

        def take(b):
            t, free[b] = free[b], []
            return t

        nload = [0]
        slots = [RING[:, i, :] for i in range(NRING)]
        ring_count = [0] * (NRING + NMORE)
        ring_free = [[] for _ in range(NRING + NMORE)]

        def load(pairs):
            s = nload[0] % len(slots)
            nload[0] += 1
            slot = slots[s]
            waits = ring_free[s]
            for view, src in pairs:
                ring_count[s] += 16
                sp.start(view(slot), src, s_ring[s], ring_count[s], *waits)
                waits = []
            return s, slot, (s_ring[s], ring_count[s])

        def done(s, tok):
            ring_free[s] = [tok]

        def cols(W, c0, n):
            def view(slot):
                return slot[:, 0:KC * n].rearrange("p (k n) -> p k n", k=KC)
            s, slot, tok = load([(view, W[:, c0:c0 + n].rearrange("(k p) n -> p k n", p=128))])
            return s, view(slot), tok

        def rows(W, f0, nf, c0, p=128):
            def view(slot):
                return slot[0:p, 0:nf * 512].rearrange("p (k n) -> p k n", k=nf)
            s, slot, tok = load([(view, W[f0 * p:(f0 + nf) * p, c0:c0 + 512].rearrange("(k p) n -> p k n", p=p))])
            return s, view(slot), tok

        def mm(o, lhsT, rhs, start, stop, *waits, inc=False):
            return pe.op(lambda e: e.matmul(o, lhsT, rhs, start=start, stop=stop), *waits, own=False, inc=inc)

        def tr(o, i, idn, *waits, inc=False):
            return pe.op(lambda e: e.transpose(o, i, idn), *waits, own=False, inc=inc)

        def tt(eng, o, a, b, op, *waits, own=True):
            return eng.op(lambda e: e.tensor_tensor(o, a, b, op), *waits, own=own)

        def ts(eng, o, a, s1, s2, op0, op1=ALU.bypass, *waits, own=True):
            return eng.op(lambda e: e.tensor_scalar(o, a, s1, s2, op0, op1), *waits, own=own)

        def stt(o, a, s, b, op0, op1, *waits, own=True):
            return dve.op(lambda e: e.scalar_tensor_tensor(o, a, s, b, op0, op1), *waits, own=own)

        def actv(o, i, f, *waits, bias=0.0, scale=1.0, accum=None, own=True):
            if accum is None:
                return act.op(lambda e: e.activation(o, i, f, bias=bias, scale=scale), *waits, own=own)
            return act.op(lambda e: e.activation(o, i, f, bias=bias, scale=scale, accum_out=accum), *waits, own=own)

        def cp(o, i, *waits, own=True):
            return dve.op(lambda e: e.tensor_copy(o, i), *waits, own=own)

        def bc(a, shape, axis):
            return a.unsqueeze(axis).to_broadcast(shape)

        def flat(a):
            return a.rearrange("p a b -> p (a b)")

        def branch(flag, *sides):
            engines = (pe, dve, act, pool)
            begin = [(x.n, dict(x.passed), x.items) for x in engines]
            sp_items, mem, start = sp.items, top[0], (list(ring_count), list(ring_free), nload[0], list(free))
            ends, queues, counts = [], [], []
            for side in sides:
                for x, (n, passed, _) in zip(engines, begin):
                    x.n, x.passed, x.items = n, dict(passed), []
                sp.items, top[0], nload[0] = [], mem, start[2]
                ring_count[:], ring_free[:], free[:] = start[0], start[1], start[3]
                side()
                ends.append([x.n for x in engines])
                queues.append([x.items for x in engines] + [sp.items])
                counts.append((list(ring_count), nload[0]))
            assert counts[0] == counts[1]
            for i, (x, (n, passed, items)) in enumerate(zip(engines, begin)):
                most = max(e[i] for e in ends)
                for e, q in zip(ends, queues):
                    if e[i] < most:
                        q[i].append((x.sem, e[i]))
                        q[i].append((lambda eng, x=x, k=most - e[i]: eng.sem_inc(x.sem, k), False))
                x.n, x.passed, x.items = most, dict(passed), items
                if queues[0][i] or queues[1][i]:
                    items.append(("branch", flag, queues[0][i], queues[1][i]))
            sp.items = sp_items
            sp.items.append(("branch", flag, queues[0][4], queues[1][4]))
            top[0] = mem
            toks = [x.last() for x in engines if x.n]
            for f in range(8):
                free[f] = list(toks)
            for f in range(len(ring_free)):
                ring_free[f] = [pe.last()]

        def project(*args, **kw):
            for _ in project_units(*args, **kw):
                pass

        def project_units(W, c0, n, X, Tn, evac, *waits, step=128):
            per = 256 // step
            pe.wait(*waits)
            i = 0
            for u0 in range(0, n, per * step):
                w = min(per * step, n - u0)
                s, wv, tok = cols(W, c0 + u0, w)
                for j0 in range(0, w, step):
                    m = min(step, w - j0)
                    b = bank()
                    o = PS[0:m, b, 0:Tn]
                    for k in range(KC):
                        t = mm(o, wv[:, k, j0:j0 + m], X[:, k, :], k == 0, k == KC - 1, tok, *take(b),
                               inc=(k == KC - 1))
                    free[b] = [evac(i, o, t)]
                    i += 1
                done(s, t)
                yield

        def contract(*args, **kw):
            for _ in contract_units(*args, **kw):
                pass

        def contract_units(W, nf, X, Tn, evac, *waits, p=128, banks=None):
            pe.wait(*waits)
            for half in range(2):
                bs = banks or [bank() for _ in range(4)]
                for f0 in range(0, nf, 4):
                    n = min(4, nf - f0)
                    s, wv, tok = rows(W, f0, n, half * 512, p)
                    for f in range(n):
                        for j in range(4):
                            t = mm(PS[:, bs[j], 0:Tn], wv[:, f, j * 128:(j + 1) * 128], X[0:p, f0 + f, :],
                                   f0 + f == 0, f0 + f == nf - 1, tok, *take(bs[j]),
                                   inc=(f == n - 1 and (j == 3 or f0 + f == nf - 1)))
                            if f0 + f == nf - 1:
                                free[bs[j]] = [evac(half * 4 + j, PS[:, bs[j], 0:Tn], t)]
                    done(s, t)
                    yield

        def copy_to(dst):
            def evac(i, o, t):
                if i % 2:
                    return actv(dst(i), o, ACT.Copy, t)
                return cp(dst(i), o, t)
            return evac

        def sum_rows(X, n, Tn, lhsT, *waits):
            b = bank()
            pe.wait(*waits)
            for k in range(n):
                t = mm(PS[:, b, 0:Tn], lhsT, X[:, k, :], k == 0, k == n - 1, *take(b), inc=(k == n - 1))
            return b, PS[:, b, 0:Tn], t

        def rsqrt(dst, src, scale, eps, tmp, *waits):
            t = ts(dve, tmp, src, scale, eps, MUL, ADD, *waits)
            t1 = actv(tmp, tmp, ACT.Sqrt, t)
            return t, dve.op(lambda e: e.reciprocal(dst, tmp), t1)

        def layer_norm(Z, gi, Tn, O, *waits):
            m0 = top[0]
            Q, R, R2 = ar3(KC, Tn), ar(Tn), ar(Tn)
            b, s, t = sum_rows(Z, KC, Tn, ones, *waits)
            td = stt(Z, bc(s, [128, KC, Tn], 1), -1.0 / D, Z, MUL, ADD, t)
            free[b] = [td]
            tq = actv(flat(Q), flat(Z), ACT.Square, td)
            b, s, t = sum_rows(Q, KC, Tn, ones, tq)
            t1, t2 = rsqrt(R, s, 1.0 / D, 1e-5, R2, t)
            free[b] = [t1]
            tt(dve, Z, Z, bc(R, [128, KC, Tn], 1), MUL)
            for k in range(KC):
                t = ts(dve, O[:, k, :], Z[:, k, :], par("ln_g", gi * 8 + k), par("ln_b", gi * 8 + k), MUL, ADD,
                       own=(k == 0))
            barrier()
            top[0] = m0
            return t

        t_par = sp.start(PAR[:, :], A["par"], s_in[0], 32)
        t_par = sp.start(CB[:, :], A["c_base"], s_in[0], 32)
        t_h = sp.start(flat(H[:, :, :]), A["hT"], s_in[1], 16)
        for x in (pe, dve, act):
            x.wait(t_par, t_h)

        def attention():
            m0 = top[0]
            q, k, oT = ar3(KC, T), ar3(KC, T), ar3(KC, T)
            V = ar3(3, D)
            dist = ar3(3, T)
            NP_ = 3
            S = [ar3(2, T) for _ in range(NP_)]
            Ex = [ar3(2, T) for _ in range(NP_)]
            Ac = [ar(T) for _ in range(NP_)]
            aT = [ar3(3, T) for _ in range(2)]
            st = [ar(8) for _ in range(NP_)]
            sm = ar(64)
            lam = ar(4)
            osq, rs, rs2 = ar3(1, T), ar(T), ar(T)
            t_dist = sp.start(flat(dist), A["c_dist"], s_in[2], 16)
            W = A["attn_w_in"][0]
            lv = POFF["lamv"]
            for i in range(2):
                a, b = PAR[:, lv + i * 128:lv + i * 128 + 64], PAR[:, lv + i * 128 + 64:lv + i * 128 + 128]
                tt(dve, sm, a, b, MUL)
                t = dve.op(lambda e, i=i: e.tensor_reduce(lam[:, i:i + 1], sm, AX, ADD))
            t = actv(lam[:, 0:2], lam[:, 0:2], ACT.Exp, t)
            tt(dve, lam[:, 2:3], lam[:, 1:2], lam[:, 0:1], SUB, t)
            ts(dve, lam[:, 2:3], lam[:, 2:3], -0.2, None, ADD)
            project(W, 0, D, H, T, copy_to(lambda i: q[:, i, :]))
            project(W, D, D, H, T, copy_to(lambda i: k[:, i, :]))
            for u in range(4):
                s, wv, tok = cols(W, 2 * D + u * 256, 256)
                for i, (q0, qn) in enumerate(QT):
                    b = bank()
                    for kk in range(KC):
                        t = mm(PS[0:qn, b, 0:256], H[:, kk, q0:q0 + qn], wv[:, kk, :], kk == 0, kk == KC - 1, tok,
                               *take(b), inc=(kk == KC - 1))
                    dst = V[0:qn, i, u * 256:(u + 1) * 256]
                    free[b] = [actv(dst, PS[0:qn, b, 0:256], ACT.Copy, t)]
                done(s, t)
            barrier()
            dve.wait(t_dist)
            items = [(h, i) for h in range(8) for i in range(3)]
            t_ex, t_comb, t_aT, t_trcp, t_pv = {}, {}, {}, {}, {}

            def first(n):
                h, i = items[n]
                q0, qn = QT[i]
                b = (n % 2) * 2
                slot = n % NP_
                slope = 2.0 ** (-(h + 1))
                for c in range(2):
                    t = mm(PS[0:qn, b + c, 0:T], q[64 * c:64 * c + 64, h, q0:q0 + qn], k[64 * c:64 * c + 64, h, :],
                           True, True, *take(b + c), inc=(c == 1))
                s_, e_, x_ = S[slot][0:qn], Ex[slot][0:qn], st[slot][0:qn]
                w = [t_comb[n - NP_]] if n >= NP_ else []
                t = stt(s_, bc(dist[0:qn, i, :], [qn, 2, T], 1), -slope * 8.0, PS[0:qn, b:b + 2, 0:T], MUL, ADD, t,
                        *w, *([t_ex[n - NP_]] if n >= NP_ else []))
                free[b], free[b + 1] = [t], [t]
                dve.op(lambda e: e.tensor_reduce(x_[:, 0:2], s_, AX, MAX))
                t = ts(dve, x_[:, 2:4], x_[:, 0:2], -0.125, None, MUL)
                for c in range(2):
                    t_ex[n] = actv(e_[:, c, :], s_[:, c, :], ACT.Exp, t, bias=x_[:, 2 + c:3 + c], scale=0.125,
                                   accum=x_[:, 4 + c:5 + c], own=False)

            def second(n):
                h, i = items[n]
                q0, qn = QT[i]
                slot = n % NP_
                e_, x_, a_ = Ex[slot][0:qn], st[slot][0:qn], Ac[slot][0:qn]
                dve.op(lambda e: e.reciprocal(x_[:, 6:8], x_[:, 4:6]), t_ex[n],
                       *([t_aT[n - NP_]] if n >= NP_ else []))
                ts(dve, x_[:, 7:8], x_[:, 7:8], lam[0:qn, 2:3], None, MUL)
                ts(dve, a_, e_[:, 1, :], x_[:, 7:8], None, MUL)
                t_comb[n] = stt(a_, e_[:, 0, :], x_[:, 6:7], a_, MUL, ADD)

            def third(n):
                h, i = items[n]
                q0, qn = QT[i]
                a_ = Ac[n % NP_][0:qn]
                b = 4 + n % 2
                w = take(b)
                for kt, (k0, kn) in enumerate(QT):
                    t = tr(PS[0:kn, b, kt * 128:kt * 128 + qn], a_[:, k0:k0 + kn], ident[0:qn, 0:qn], t_comb[n], *w,
                           inc=(kt == 2))
                t_aT[n] = t
                dst = aT[h % 2]
                wv = [t_pv[h - 2]] if h >= 2 else []
                src = PS[:, b, 0:384].rearrange("p (a b) -> p a b", a=3)
                actv(dst[0:96, 0:2, q0:q0 + qn], src[0:96, 0:2, 0:qn], ACT.Copy, t, *wv, own=False)
                t_trcp[n] = actv(dst[0:80, 2, q0:q0 + qn], src[0:80, 2, 0:qn], ACT.Copy, own=False)
                free[b] = [t_trcp[n]]
                if i == 2:
                    b = 6 + h % 2
                    for kt, (k0, kn) in enumerate(QT):
                        t = mm(PS[:, b, 0:T], V[0:kn, kt, h * 128:(h + 1) * 128], aT[h % 2][0:kn, kt, :], kt == 0,
                               kt == 2, t_trcp[n], *take(b), inc=(kt == 2))
                    t_pv[h] = t
                    free[b] = [cp(oT[:, h, :], PS[:, b, 0:T], t)]

            for n in range(len(items) + 2):
                if n < len(items):
                    first(n)
                if 1 <= n <= len(items):
                    second(n - 1)
                if n >= 2:
                    third(n - 2)
            barrier()
            for h in range(8):
                tq = actv(osq[:, 0, :], oT[:, h, :], ACT.Square, dve.last(), pe.last())
                b, s, t = sum_rows(osq, 1, T, ones, tq)
                t1, t2 = rsqrt(rs, s, 1.0 / 128, 1e-5, rs2, t)
                free[b] = [t1]
                tt(dve, oT[:, h, :], oT[:, h, :], rs, MUL)
                t = ts(dve, oT[:, h, :], oT[:, h, :], par("subln"), 0.8, MUL, MUL)

            def add(i, o, t):
                return stt(H[:, i, :], H[:, i, :], ALPHA, o, MUL, ADD, t)
            project(A["attn_w_o"][0], 0, D, oT, T, add, t)
            barrier()
            top[0] = m0
            layer_norm(H, 0, T, H, dve.last())

        def gated(Wg, Wu, Wd, nf, hT, tmp, evac):
            used = [None] * len(tmp)
            bars = dve.last(), act.last(), pe.last()
            pe.wait(*bars)
            act.wait(*bars)
            dve.wait(*bars)
            n = 0
            for f0 in range(0, nf, 2):
                sg, wg, tg = cols(Wg, f0 * 128, 256)
                su, wu, tu = cols(Wu, f0 * 128, 256)
                for j in range(2):
                    bg, bu = bank(), bank()
                    for k in range(KC):
                        t1 = mm(PS[:, bg, 0:T], wg[:, k, j * 128:(j + 1) * 128], H[:, k, :], k == 0, k == KC - 1, tg,
                                *take(bg), inc=(k == KC - 1))
                    for k in range(KC):
                        t2 = mm(PS[:, bu, 0:T], wu[:, k, j * 128:(j + 1) * 128], H[:, k, :], k == 0, k == KC - 1, tu,
                                *take(bu), inc=(k == KC - 1))
                    x = n % len(tmp)
                    t = actv(tmp[x], PS[:, bg, 0:T], ACT.Silu, t1, *([used[x]] if used[x] else []), own=False)
                    free[bg] = [t]
                    used[x] = tt(dve, hT[:, f0 + j, :], tmp[x], PS[:, bu, 0:T], MUL, t, t2, own=False)
                    free[bu] = [used[x]]
                    n += 1
                done(sg, t1)
                done(su, t2)
            contract(Wd, nf, hT, T, evac, dve.last())

        def ffn():
            m0 = top[0]
            hT = ar3(FFN // 128, T)
            tmp = [ar(T) for _ in range(3)]

            def add(i, o, t):
                return stt(H[:, i, :], H[:, i, :], ALPHA, o, MUL, ADD, t)
            gated(A["ffn_w_gate"][0], A["ffn_w_up"][0], A["ffn_w_down"][0], FFN // 128, hT, tmp, add)
            barrier()
            top[0] = m0
            layer_norm(H, 1, T, H, dve.last())

        def rwkv():
            m0 = top[0]
            cst = ar(NC_RW)
            t_c = sp.start(cst, A["c_rw"], s_in[3], 16, *barrier())
            r, k, v, kk = [ar3(KC, TS) for _ in range(4)]
            a = [ar3(KC, TS) for _ in range(2)]
            c = [ar3(KC, TS) for _ in range(2)]
            for x in (r, k, v, kk, *a, *c):
                dve.op(lambda e, x=x: e.memset(x[:, :, T:TS], 0.0), own=False)
            gh = ar(2 * T).rearrange("p (a b) -> p a b", a=2)
            m1 = top[0]
            dp, dn = ar3(KC, T), ar3(KC, T)
            xs = [ar3(KC, T) for _ in range(2)]
            lh = ar(T)
            lg = [ar(T) for _ in range(2)]
            tt(dve, dp[:, :, 1:T], H[:, :, 0:T - 1], H[:, :, 1:T], SUB)
            ts(dve, dp[:, :, 0:1], H[:, :, 0:1], -1.0, None, MUL, own=False)
            tt(dve, dn[:, :, 0:T - 1], H[:, :, 1:T], H[:, :, 0:T - 1], SUB, own=False)
            t = ts(dve, dn[:, :, T - 1:T], H[:, :, T - 1:T], -1.0, None, MUL, own=False)
            used = [None, None]

            def mix(i, slot):
                X = xs[slot]
                w = [used[slot]] if used[slot] else []
                for kc in range(KC):
                    stt(X[:, kc, :], dp[:, kc, :], par("mu", i * 8 + kc), H[:, kc, :], MUL, ADD, *w, own=(kc == 0))
                for kc in range(KC):
                    t = stt(X[:, kc, :], dn[:, kc, :], par("mu", 48 + i * 8 + kc), X[:, kc, :], MUL, ADD,
                            own=(kc == 0))
                return X, t

            for n, (i, dst) in enumerate([(0, r), (1, k), (2, v)]):
                X, t = mix(i, n % 2)
                project(A["rw_w_rkv"][0, i], 0, D, X, T, copy_to(lambda f, dst=dst: dst[:, f, 0:T]), t)
                used[n % 2] = pe.last()

            def quarter(n):
                return lambda slot: slot[:, :].rearrange("p (k q r) -> p k q r", k=KC, q=4)[:, :, n, :]

            s1, w1v, tok1 = load([(quarter(n), A[nm][0, n % 2].rearrange("(k p) r -> p k r", p=128))
                                  for n, nm in enumerate(["rw_w1", "rw_w1", "rw_a1", "rw_a1"])])
            w1v = w1v.rearrange("p (k q) -> p k q", k=KC)
            s2, w2v, tok2 = load([(lambda sl: sl[:, 0:D], A["rw_w2"][0].rearrange("n r d -> (n r) d")),
                                  (lambda sl: sl[:, D:2 * D], A["rw_a2"][0].rearrange("n r d -> (n r) d"))])

            def lora(i, slot, which, func, fin):
                X, t = mix(i, slot)
                b = bank()
                for kc in range(KC):
                    t1 = mm(PS[:, b, 0:T], w1v[:, kc, which * 128:(which + 1) * 128], X[:, kc, :], kc == 0,
                            kc == KC - 1, t, tok1, *take(b), inc=(kc == KC - 1))
                used[slot] = t1
                t2 = actv(lh, PS[:, b, 0:T], func, t1, pe.last())
                free[b] = [t2]
                for f in range(KC):
                    for n in range(2):
                        b = bank()
                        t3 = mm(PS[:, b, 0:T], w2v[64 * n:64 * n + 64, which * D + f * 128:which * D + (f + 1) * 128],
                                lh[64 * n:64 * n + 64, :], True, True, t2, tok2, *take(b), inc=True)
                        free[b] = [fin(n, f, PS[:, b, 0:T], t3)]
                return t1, t3

            _, t3 = lora(3, 1, 0, ACT.Tanh, lambda n, f, o, t: actv(
                c[n][:, f, 0:T], o, ACT.Sigmoid, t, bias=par("w0", n * 8 + f), own=False))
            t1, t3 = lora(4, 0, 1, ACT.Copy, lambda n, f, o, t: actv(
                a[n][:, f, 0:T], o, ACT.Sigmoid, t, bias=par("a0", n * 8 + f), own=False))
            done(s1, t1)
            done(s2, t3)
            X, t = mix(5, 1)
            sg, gv, tokg = cols(A["rw_g1"][0], 0, 160)
            for j, m in enumerate([128, 32]):
                b = bank()
                for kc in range(KC):
                    t1 = mm(PS[0:m, b, 0:T], gv[:, kc, j * 128:j * 128 + m], X[:, kc, :], kc == 0, kc == KC - 1, t,
                            tokg, *take(b), inc=(kc == KC - 1))
                free[b] = [actv(gh[0:m, j, :], PS[0:m, b, 0:T], ACT.Sigmoid, t1)]
            done(sg, t1)
            barrier()
            top[0] = m1
            LD = ar3(KC, TS)
            Q, RN, R2 = ar3(KC, T), ar3(KC, T), ar3(KC, T)
            tot = ar3(KC, NCH)
            dve.wait(t_c)
            c4 = [128, KC, NCH, CH]

            def by_chunk(x):
                return x[:, :, 0:NCH * CH].rearrange("p f (c t) -> p f c t", t=CH)
            for n in range(2):
                ts(dve, flat(LD), flat(c[n]), -float(np.exp(-0.5)), None, MUL)
                for f in range(KC):
                    dve.op(lambda e, n=n, f=f: e.tensor_tensor_scan(
                        c[n][:, f, :], cst[:, C_SCAN:C_SCAN + TS], LD[:, f, :], 0.0, MUL, ADD), own=(f == 0))
                if n == 1:
                    tt(dve, flat(LD), flat(LD), flat(c[n]), SUB)
                    x = by_chunk(c[n])
                    cp(tot, x[:, :, :, CH - 1])
                    tt(dve, x, by_chunk(LD), bc(tot, c4, 3), ADD)
            kT, kkT = k[:, :, 0:T], kk[:, :, 0:T]
            t = tt(dve, kkT, kT, bc(par("k_k", 0, 8), [128, KC, T], 2), MUL)
            tq = actv(Q, kkT, ACT.Square, t)
            for f in range(KC):
                t = mm(PS[:, f, 0:T], blk, Q[:, f, :], True, True, tq, *take(f), inc=True)
            t = ts(dve, R2, PS[:, :, 0:T], 1e-24, None, MAX, ALU.bypass, t)
            for f in range(8):
                free[f] = [t]
            t = actv(flat(R2), flat(R2), ACT.Sqrt, t)
            dve.op(lambda e: e.reciprocal(flat(RN), flat(R2)), t)
            tt(dve, kkT, kkT, RN, MUL)
            barrier()
            top[0] = m1
            y = ar3(KC, TS)
            St = [ar3(KC, 64) for _ in range(2)]
            NB = 2
            B = []
            for _ in range(NB):
                w = dict(X=ar3(KC, 64), XT=ar3(KC, 64), W=ar3(KC, 64), akp=ar3(KC, 128), abp=ar3(KC, 128),
                         ar=ar3(KC, 128), ka=ar3(KC, 64), be=ar3(KC, 64), e1=ar3(KC, CH + 1),
                         t1=ar(KC * 64), kt=ar3(KC, 64), bt=ar3(KC, 64), vt=ar3(KC, 64), em=ar(8))
                w.update(e2=flat(w["X"])[:, 0:KC * CH].rearrange("p (f t) -> p f t", f=KC))
                w.update(R=w["W"], U=w["X"], sm=w["t1"].rearrange("p (f v) -> p f v", f=KC))
                B.append(w)
                for x in (w["ka"], w["be"], w["ar"][:, :, 0:64], w["ar"][:, :, 64:128]):
                    dve.op(lambda e, x=x: e.memset(x[:, :, CH:64], 0.0), own=False)
            for n in range(2):
                dve.op(lambda e, n=n: e.memset(flat(St[n]), 0.0), own=False)
            act.wait(dve.last())
            pe.wait(dve.last())
            ib = bc(CB[:, 384:448], [128, KC, 64], 1)

            def lvl(d, l, tr_):
                o = C_LVL + ((d ^ tr_) * len(SCAN_LEVELS) + l) * 64
                return bc(cst[:, o:o + 64], [128, KC, 64], 1)

            groups = []
            for i in range(NCH):
                groups += [(0, i), (1, NCH - 1 - i)]
            last_seq = {}

            def each(o, lhsT, rhs, *waits, add=None):
                pe.wait(*waits)
                for h in range(16):
                    p, f = slice(64 * (h % 2), 64 * (h % 2) + 64), h // 2
                    terms = [(lhsT, rhs)] + (add or [])
                    for n, (a_, b_) in enumerate(terms):
                        t = mm(o(p, f), a_(p, f), b_(p, f), n == 0, n == len(terms) - 1,
                               inc=(h == 15 and n == len(terms) - 1))
                return t

            def head(x, o=0, n=64):
                return lambda p, f: x[p, f, o:o + n]

            def bankof(b, n=64):
                return lambda p, f: PS[p, b, f * n:(f + 1) * n]

            def whole(b):
                return PS[:, b, :].rearrange("p (f t) -> p f t", f=KC)

            def prep(g):
                d, ci = groups[g]
                W = B[g % NB]
                z = 4 * (g % 2)
                t0 = ci * CH
                sl = (slice(None), slice(None), slice(t0, t0 + CH))
                cc, rr, kv, kkv, av = c[d][sl], r[sl], k[sl], kk[sl], a[d][sl]
                sh = [128, KC, CH]
                e1, e2, t1 = W["e1"], W["e2"], W["t1"][:, 0:KC * CH].rearrange("p (f t) -> p f t", f=KC)
                inn, prv = (slice(1, CH + 1), slice(0, CH)) if d == 0 else (slice(0, CH), slice(1, CH + 1))
                edge = 0 if d == 0 else CH
                mid = cc[:, :, MID:MID + 1]
                pre = last_seq.get(g - NB, [])
                pe.wait(*pre)
                t = tt(dve, e1[:, :, inn], cc, mid.to_broadcast(sh), SUB, *pre)
                t = ts(dve, e1[:, :, edge:edge + 1], mid, -1.0, None, MUL, own=False)
                actv(e2, e1[:, :, inn], ACT.Exp, t, *pre, scale=-1.0, own=False)
                actv(W["em"], mid.rearrange("p a b -> p (a b)"), ACT.Exp, own=False)
                te = actv(e1, e1, ACT.Exp)
                stt(t1, av, -1.0, bc(par("k_a", 0, 8), sh, 2), ADD, MUL)
                stt(t1, t1, 1.0, kv, ADD, MUL)
                tka = tt(dve, W["ka"][:, :, 0:CH], t1, e2, MUL, te)
                tt(dve, t1, kkv, av, MUL)
                tbe = tt(dve, W["be"][:, :, 0:CH], t1, e2, MUL)
                tt(dve, W["ar"][:, :, 0:CH], kkv, e1[:, :, prv], MUL, own=False)
                tf = tt(dve, W["ar"][:, :, 64:64 + CH], rr, e1[:, :, inn], MUL, own=False)
                idh = lambda p, f: ident[p, p]
                for x, (src, dst, sc, tw) in enumerate([
                        (lambda p, f: v[p, f, t0:t0 + 64], W["vt"], 1.0, tka), (head(W["ka"]), W["kt"], 1.0, tka),
                        (head(W["be"]), W["bt"], -1.0, tbe)]):
                    b = z + x
                    t = each(bankof(b), src, idh, tw, *take(b))
                    free[b] = [actv(flat(dst), PS[:, b, :], ACT.Copy, t, *pre, scale=sc, own=False)]
                for x, (src, dst) in enumerate([("ka", "akp"), ("be", "abp")]):
                    for fh in range(2):
                        b = z + (3, 0, 1, 2)[2 * x + fh]
                        pe.wait(tf, *take(b))
                        for h in range(8):
                            p, f = slice(64 * (h % 2), 64 * (h % 2) + 64), 4 * fh + h // 2
                            t = mm(PS[p, b, (h // 2) * 128:(h // 2 + 1) * 128], W[src][p, f, :], W["ar"][p, f, :], True,
                                   True, inc=(h == 7))
                        o = C_AM + (2 * d + x) * 128
                        t = tt(dve, W[dst][:, 4 * fh:4 * fh + 4, :], PS[:, b, :].rearrange("p (f x) -> p f x", f=4),
                               bc(cst[:, o:o + 128], [128, 4, 128], 1), MUL, t, own=False)
                        free[b] = [t]
                return t

            def level(g, l, part, tw):
                d, ci = groups[g]
                W = B[g % NB]
                z = 4 * (g % 2)
                X, XT, Wm = W["X"], W["XT"], W["W"]
                if part == 0:
                    rhs = head(X) if l else (lambda p, f: ident[p, p])
                    t = each(bankof(z), head(W["abp"]), rhs, tw, *take(z))
                    t2 = tt(dve, Wm, whole(z), lvl(d, l, 0), MUL, t, own=False)
                    free[z] = [t2]
                    if l == 0:
                        tt(dve, XT, W["abp"][:, :, 0:64], lvl(d, l, 1), MUL, own=False)
                        tt(dve, X, ib, Wm, SUB)
                        t2 = tt(dve, XT, ib, XT, SUB)
                    return t2
                if l == 0:
                    return tw
                last = l == len(SCAN_LEVELS) - 1
                if not last:
                    tx = each(bankof(z + 1), head(XT), head(Wm), tw, *take(z + 1))
                t = each(bankof(z + 2), head(Wm), head(XT), tw, *take(z + 2))
                if not last:
                    free[z + 1] = [tt(dve, X, X, whole(z + 1), SUB, tx, t, own=False)]
                t3 = tt(dve, XT, XT, whole(z + 2), SUB, t, own=False)
                free[z + 2] = [t3]
                return t3

            def seq1(g, tw):
                d, ci = groups[g]
                W = B[g % NB]
                z = 4 * (g % 2)
                tsm = tt(dve, W["sm"], St[d], bc(W["em"], [128, KC, 64], 2), MUL, act.last(), pe.last())
                t = each(bankof(z), head(W["ar"]), head(W["sm"]), tsm, tw, *take(z),
                         add=[(head(W["akp"]), head(W["vt"]))])
                t = actv(flat(W["R"]), PS[:, z, :], ACT.Copy, t, own=False)
                free[z] = [t]
                return t

            def seq2(g, t):
                W = B[g % NB]
                z = 4 * (g % 2)
                t = each(bankof(z + 2), head(W["XT"]), head(W["R"]), t, *take(z + 2))
                t = actv(flat(W["U"]), PS[:, z + 2, :], ACT.Copy, t, own=False)
                free[z + 2] = [t]
                return t

            def seq3(g, t):
                d, ci = groups[g]
                W = B[g % NB]
                z = 4 * (g % 2)
                t0 = ci * CH
                S, sm = St[d], W["sm"]
                ts_ = each(bankof(z + 3), head(W["kt"]), head(W["vt"]), t, *take(z + 3),
                           add=[(head(W["bt"]), head(W["U"]))])
                ty = each(lambda p, f: PS[p, z, f * 64:f * 64 + CH], head(sm), head(W["ar"], 64, CH), *take(z),
                          add=[(head(W["vt"]), head(W["akp"], 64, CH)), (head(W["U"]), head(W["abp"], 64, CH))])
                end = W["e1"][:, :, CH if d == 0 else 0]
                t1 = tt(dve, S, sm, whole(z + 3), ADD, ts_)
                free[z + 3] = [t1]
                tt(dve, S, S, bc(end, [128, KC, 64], 2), MUL)
                yv = y[:, :, t0:t0 + CH]
                src = whole(z)[:, :, 0:CH]
                if g // 2 < NCH // 2 or (g // 2 == NCH // 2 and d == 0):
                    t2 = cp(yv, src, ty, own=False)
                else:
                    t2 = tt(dve, yv, yv, src, ADD, ty)
                free[z] = [t2]
                last_seq[g] = [t2, ty, t]

            for g0 in range(0, len(groups), NB):
                gs = list(range(g0, g0 + NB))
                tw = {g: prep(g) for g in gs}
                for l in range(len(SCAN_LEVELS)):
                    for part in range(2):
                        for g in gs:
                            tw[g] = level(g, l, part, tw[g])
                for step in (seq1, seq2, seq3):
                    for g in gs:
                        tw[g] = step(g, tw[g])
            barrier()
            top[0] = m1 + KC * TS
            Q, G, E2 = ar3(KC, T), ar3(KC, T), ar3(KC, T)
            sh = [128, KC, T]
            y, r, k, v, a0, a1 = [x[:, :, 0:T] for x in (y, r, k, v, *a)]

            def heads(X, t):
                for f in range(KC):
                    t2 = mm(PS[:, f, 0:T], blk, X[:, f, :], True, True, t, *take(f), inc=(f == KC - 1))
                return t2

            def freed(t):
                for f in range(8):
                    free[f] = [t]
                return t
            t = heads(y, dve.last())
            t = freed(stt(y, PS[:, :, 0:T], -1.0 / 64, y, MUL, ADD, t))
            t = actv(Q, y, ACT.Square, t)
            t = heads(Q, t)
            t = freed(ts(dve, G, PS[:, :, 0:T], 1.0 / 64, 64e-5, MUL, ADD, t))
            t = actv(flat(G), flat(G), ACT.Sqrt, t)
            dve.op(lambda e: e.reciprocal(flat(E2), flat(G)), t)
            tt(dve, y, y, E2, MUL)
            tt(dve, y, y, bc(par("lnx_g", 0, 8), sh, 2), MUL)
            tt(dve, y, y, bc(par("lnx_b", 0, 8), sh, 2), ADD)
            tt(dve, Q, a0, a1, ADD)
            stt(Q, Q, -2.0, bc(par("k_a", 0, 8), sh, 2), ADD, MUL)
            stt(Q, Q, 2.0, k, ADD, MUL)
            tt(dve, Q, Q, r, MUL)
            t = tt(dve, Q, Q, bc(par("r_k", 0, 8), sh, 2), MUL)
            t = heads(Q, t)
            t = freed(tt(dve, Q, v, PS[:, :, 0:T], MUL, t))
            tt(dve, y, y, Q, ADD)
            s, slot, tok = load([(lambda sl: sl[:, 0:D], A["rw_g2"][0, 0:128, :]),
                                 (lambda sl: sl[0:32, D:2 * D], A["rw_g2"][0, 128:160, :])])
            for f in range(KC):
                w = take(f)
                mm(PS[:, f, 0:T], slot[:, f * 128:(f + 1) * 128], gh[:, 0, :], True, False, tok, *w)
                t = mm(PS[:, f, 0:T], slot[0:32, D + f * 128:D + (f + 1) * 128], gh[0:32, 1, :], False, True, inc=True)
            done(s, t)
            t = freed(tt(dve, y, y, PS[:, :, 0:T], MUL, t))

            def add(i, o, t):
                return stt(H[:, i, :], H[:, i, :], ALPHA, o, MUL, ADD, t)
            project(A["rw_w_o"][0], 0, D, y, T, add, t)
            barrier()
            top[0] = m0
            layer_norm(H, 2, T, H, dve.last())

        def moe():
            m0 = top[0]
            bars = barrier()
            for i in range(NMORE):
                slots.append(ar(2048))
                ring_free[NRING + i] = list(bars)
            acc, GB = ar3(KC, T), ar3(KC, T)
            cst = ar(224)
            gt, rt = ar(T), ar(T)
            sc = [ar(64) for _ in range(3)]
            mk = [x[:, 40:48] for x in sc]
            rk = [ar(8) for _ in range(3)]
            cn = ar(9)
            t_c = sp.start(cst, A["c_moe"], s_in[5], 16, *bars)
            tri, iota_r, iota_p = cst[:, 0:96], cst[:, 96:96 + CAP], cst[:, 192:193]
            ws, wr, tok = cols(A["moe_w_router"][0], 0, NE)
            for i, (q0, qn) in enumerate(QT):
                b = bank()
                x = sc[i][0:qn]
                for kc in range(KC):
                    t = mm(PS[0:qn, b, 0:NE], H[:, kc, q0:q0 + qn], wr[:, kc, :], kc == 0, kc == KC - 1, tok,
                           *bars, *take(b), inc=(kc == KC - 1))
                free[b] = [tt(dve, x[:, 0:8], PS[0:qn, b, 0:NE], par("b_router", 0, 8, qn), ADD, t)]
                dve.op(lambda e, x=x: e.max(x[:, 8:16], x[:, 0:8]))
                t = ts(dve, x[:, 16:17], x[:, 8:9], -1.0, None, MUL)
                t = actv(x[:, 24:32], x[:, 0:8], ACT.Exp, t, bias=x[:, 16:17], accum=x[:, 17:18])
                dve.op(lambda e, x=x: e.reciprocal(x[:, 18:19], x[:, 17:18]), t)
                ts(dve, x[:, 24:32], x[:, 24:32], x[:, 18:19], None, MUL)
                dve.op(lambda e, x=x: e.max(x[:, 32:40], x[:, 24:32]))
                tt(dve, x[:, 19:20], x[:, 32:33], x[:, 33:34], ADD)
                dve.op(lambda e, x=x: e.reciprocal(x[:, 20:21], x[:, 19:20]))
                cp(x[:, 40:42], x[:, 32:34])
                dve.op(lambda e, x=x: e.memset(x[:, 42:48], -2.0))
                dve.op(lambda e, x=x: e.match_replace(x[:, 48:56], x[:, 40:48], x[:, 24:32], -1.0))
                ts(dve, x[:, 40:48], x[:, 48:56], -1.0, None, ALU.is_equal)
                ts(dve, x[:, 48:56], x[:, 40:48], x[:, 20:21], None, MUL)
                t = tt(dve, x[:, 56:64], x[:, 48:56], x[:, 24:32], MUL)
                b = bank()
                t = tr(PS[0:NE, b, 0:qn], x[:, 56:64], ident[0:qn, 0:qn], t, *take(b), inc=True)
                free[b] = [cp(gt[0:NE, q0:q0 + qn], PS[0:NE, b, 0:qn], t)]
            done(ws, pe.last())
            b = bank()
            for i, (q0, qn) in enumerate(QT):
                t = mm(PS[:, b, 0:8], ones[0:qn, :], mk[i][0:qn], i == 0, i == 2, t_c, dve.last(), *take(b),
                       inc=(i == 2))
            cp(cn[:, 0:8], PS[:, b, 0:8], t)
            dve.op(lambda e: e.tensor_reduce(cn[:, 8:9], cn[:, 0:8], AX, MAX))
            t_flag = ts(dve, flag, cn[:, 8:9], CAP + 0.5, None, ALU.is_gt)
            free[b] = [t_flag]
            for i, (q0, qn) in enumerate(QT):
                b = bank()
                for j in range(i + 1):
                    jn = QT[j][1]
                    t = mm(PS[0:qn, b, 0:8], tri[0:jn, 0:qn] if j == i else ones[0:jn, 0:qn], mk[j][0:jn], j == 0,
                           j == i, *take(b), inc=(j == i))
                free[b] = [cp(rk[i][0:qn], PS[0:qn, b, 0:8], t)]
                b = bank()
                t = tr(PS[0:NE, b, 0:qn], rk[i][0:qn], ident[0:qn, 0:qn], dve.last(), *take(b), inc=True)
                free[b] = [cp(rt[0:NE, q0:q0 + qn], PS[0:NE, b, 0:qn], t)]
            for e_ in range(NE):
                b = bank()
                t = mm(PS[:, b, 0:T], ident[0:NE, e_:e_ + 1].to_broadcast([NE, 128]), gt[0:NE, :], True, True,
                       dve.last(), *take(b), inc=True)
                t = cp(GB[:, e_, :], PS[:, b, 0:T], t)
                free[b] = [t]

            def dense():
                hT = ar3(FE // 128, T)
                tmp = [ar(T) for _ in range(3)]
                for e_ in range(NE):
                    def add(i, o, t, e_=e_):
                        if e_ == 0:
                            return tt(dve, acc[:, i, :], GB[:, e_, :], o, MUL, t)
                        x = tmp[0]
                        t = tt(dve, x, GB[:, e_, :], o, MUL, t)
                        tt(dve, acc[:, i, :], acc[:, i, :], x, ADD)
                        return t
                    gated(A["moe_w_gate"][0, e_], A["moe_w_up"][0, e_], A["moe_w_down"][0, e_], FE // 128, hT, tmp,
                          add)

            def sparse():
                Ht = ar3(3, D)
                xe = [ar3(KC, CAP) for _ in range(2)]
                P1 = [ar3(3, CAP) for _ in range(2)]
                PG = [ar(T) for _ in range(2)]
                hT = ar3(FE // 128, CAP)
                tmp = [ar(2 * CAP) for _ in range(3)]
                Y = ar(D)
                for i, (q0, qn) in enumerate(QT):
                    for hf in range(2):
                        b = bank()
                        for f in range(4):
                            t = tr(PS[0:qn, b, f * 128:(f + 1) * 128], H[:, 4 * hf + f, q0:q0 + qn], ident, *take(b),
                                   inc=(f == 3))
                        free[b] = [actv(Ht[0:qn, i, hf * 512:(hf + 1) * 512], PS[0:qn, b, :], ACT.Copy, t, own=False)]
                t_ht = act.last()
                t_x, t_pg, t_sc = {}, {}, {}

                def gather(e_):
                    w = [t_sc[e_ - 2]] if e_ >= 2 else []
                    x = xe[e_ % 2]
                    for i, (q0, qn) in enumerate(QT):
                        t = ts(dve, P1[e_ % 2][0:qn, i, :], iota_r[0:qn], rk[i][0:qn, e_:e_ + 1],
                               mk[i][0:qn, e_:e_ + 1], ALU.is_equal, MUL, *w, own=(i == 0))
                    for hf in range(2):
                        b = bank()
                        wb = take(b)
                        for f in range(4):
                            for i, (q0, qn) in enumerate(QT):
                                t2 = mm(PS[:, b, f * CAP:(f + 1) * CAP], Ht[0:qn, i, (4 * hf + f) * 128:(4 * hf + f + 1) * 128],
                                        P1[e_ % 2][0:qn, i, :], i == 0, i == 2, t, t_ht, *wb, inc=(f == 3 and i == 2))
                        free[b] = [actv(flat(x[:, 4 * hf:4 * hf + 4, :]), PS[:, b, 0:4 * CAP], ACT.Copy, t2, *w,
                                        own=False)]
                    t_x[e_] = act.last()
                    b = bank()
                    t = mm(PS[:, b, 0:T], ident[0:NE, e_:e_ + 1].to_broadcast([NE, 128]), rt[0:NE, :], True, True,
                           *take(b), inc=True)
                    t_pg[e_] = stt(PG[e_ % 2], PS[:, b, 0:T], iota_p, GB[:, e_, :], ALU.is_equal, MUL, t, *w)
                    free[b] = [t_pg[e_]]

                used = [None] * 3
                t_h, t_dn = None, None
                gather(0)
                for e_ in range(NE):
                    Wg, Wu, Wd = A["moe_w_gate"][0, e_], A["moe_w_up"][0, e_], A["moe_w_down"][0, e_]
                    x = xe[e_ % 2]
                    for f0 in range(0, FE // 128, 2):
                        sg, wg, tg = cols(Wg, f0 * 128, 256)
                        su, wu, tu = cols(Wu, f0 * 128, 256)
                        bs = []
                        for wv, tok in ((wg, tg), (wu, tu)):
                            b = bank()
                            wb = take(b)
                            for j in range(2):
                                for k in range(KC):
                                    t = mm(PS[:, b, j * CAP:(j + 1) * CAP], wv[:, k, j * 128:(j + 1) * 128], x[:, k, :],
                                           k == 0, k == KC - 1, tok, t_x[e_], *wb, inc=(j == 1 and k == KC - 1))
                            bs.append((b, t))
                        done(sg, bs[0][1])
                        done(su, bs[1][1])
                        n = f0 // 2 % 3
                        w = [t_dn] if t_dn else []
                        t = actv(tmp[n], PS[:, bs[0][0], 0:2 * CAP], ACT.Silu, bs[0][1],
                                 *([used[n]] if used[n] else []), own=False)
                        free[bs[0][0]] = [t]
                        t_h = tt(dve, flat(hT[:, f0:f0 + 2, :]), tmp[n], PS[:, bs[1][0], 0:2 * CAP], MUL, t, bs[1][1],
                                 *w, own=False)
                        used[n] = t_h
                        free[bs[1][0]] = [t_h]
                    if e_ + 1 < NE:
                        gather(e_ + 1)
                    ty = []
                    for hf in range(2):
                        b = bank()
                        wb = take(b)
                        for f0 in range(0, FE // 128, 4):
                            s, wv, tok = rows(Wd, f0, 4, hf * 512)
                            for f in range(4):
                                t = mm(PS[0:CAP, b, :], hT[:, f0 + f, :], wv[:, f, :], f0 + f == 0,
                                       f0 + f == FE // 128 - 1, tok, t_h, *wb, inc=(f == 3))
                            done(s, t)
                        t2 = actv(Y[0:CAP, hf * 512:(hf + 1) * 512], PS[0:CAP, b, :], ACT.Copy, t,
                                  *([t_sc[e_ - 1]] if e_ else []), own=False)
                        free[b] = [t2]
                    t_dn = t
                    for f in range(KC):
                        b = bank()
                        t = mm(PS[:, b, 0:T], Y[0:CAP, f * 128:(f + 1) * 128], PG[e_ % 2][0:CAP, :], True, True, t2,
                               t_pg[e_], *take(b), inc=True)
                        if e_ == 0:
                            free[b] = [cp(acc[:, f, :], PS[:, b, 0:T], t, own=False)]
                        else:
                            free[b] = [tt(dve, acc[:, f, :], acc[:, f, :], PS[:, b, 0:T], ADD, t, own=(f == 0))]
                    t_sc[e_] = t

            for x in (pe, dve, act):
                x.wait(t_flag, dve.last(), act.last())
            sp.items.append(t_flag)
            branch(flag[0:1, 0:1], dense, sparse)
            barrier()
            del slots[NRING:]
            nload[0] = 0
            dve.wait(pe.last())
            stt(flat(H[:, :, :]), flat(H[:, :, :]), ALPHA, flat(acc), MUL, ADD)
            barrier()
            top[0] = m0
            layer_norm(H, 3, T, H, dve.last())

        B2 = {}

        def tables():
            cst = ar(NC_B2)
            B2["cs"] = [(ar(SEQ), ar(SEQ)) for _ in range(2)]
            m0 = top[0]
            pos = ar(SEQ)
            bars = barrier()
            t_c = sp.start(cst, A["c_b2"], s_in[4], 32, *bars)
            t_c = sp.start(pos.bitcast(I32), A["pos"], s_in[4], 32)
            B2.update(rot=[cst[:, 0:128], cst[:, 128:256]], causal=cst[:, 256:768].rearrange("p (a b) -> p a b", a=2))
            pf, y, kf = ar(SEQ), ar(SEQ), ar(SEQ)
            cp(pf, pos.bitcast(I32), t_c)
            c1 = 6.28125
            c2 = float(np.float32(round((TWO_PI - c1) * 2 ** 20) / 2 ** 20))
            c3 = float(TWO_PI - c1 - c2)
            for i in range(2):
                co, si = B2["cs"][i]
                ts(dve, y, pf, cst[:, 768 + i:769 + i], None, MUL)
                ts(dve, kf, y, float(1.0 / TWO_PI), None, MUL)
                ts(dve, kf, kf, 12582912.0, None, ADD)
                ts(dve, kf, kf, -12582912.0, None, ADD)
                for cc in (c1, c2, c3):
                    stt(y, kf, -cc, y, MUL, ADD)
                ts(dve, y, y, 3.1415925, -3.1415925, ALU.min, MAX)
                t = ts(dve, co, y, -1.0, None, MUL)
                tt(dve, co, co, y, MAX)
                t = ts(dve, co, co, -1.0, float(np.pi / 2), MUL, ADD)
                actv(si, y, ACT.Sin, t)
                t = actv(co, co, ACT.Sin)
                dve.wait(t)
            barrier()
            top[0] = m0

        X2 = H[:, :, NMETA:T]

        def rms(O, gain, *waits):
            m0 = top[0]
            Q, R, R2 = ar3(KC, SEQ), ar(SEQ), ar(SEQ)
            tq = actv(Q, X2, ACT.Square, *waits)
            b, s, t = sum_rows(Q, KC, SEQ, ones, tq)
            t1, t2 = rsqrt(R, s, 1.0 / D, 1e-6, R2, t)
            free[b] = [t1]
            tt(dve, Q, X2, bc(R, [128, KC, SEQ], 1), MUL)
            t = tt(dve, O, Q, bc(gain, [128, KC, SEQ], 2), MUL)
            top[0] = m0
            return t

        def second(l):
            m0 = top[0]
            W = A["w_in_2"][l]
            o_q, o_k, o_v, o_ga, o_iq, o_ik, o_xr, o_gr, o_ma, o_mb = (
                0, 1024, 2048, 3072, 4096, 5120, 5200, 6608, 8016, 9040)
            hn, M, q, k, iq, raw, t1 = [ar3(KC, SEQ) for _ in range(7)]
            ik, ik_raw, iw = ar(SEQ), ar3(1, SEQ), ar(32).rearrange("p (a b) -> p a b", a=2)
            score, bias = [ar3(2, SEQ) for _ in range(2)]
            m8 = ar(16)
            GA, V = iq, flat(t1).rearrange("p (a b) -> p a b", a=2)
            m1 = top[0]
            barrier()
            rms(hn, par("norm_g", l * 8, 8))
            barrier()
            XR = ar3(NRB, SEQ + 3)
            GR, CX, RR, II = [ar3(NRB, SEQ) for _ in range(4)]
            AA = flat(XR)[:, 0:NRB * SEQ].rearrange("p (a b) -> p a b", a=NRB)
            HC = flat(RR)[:, 0:11 * SEQ].rearrange("p (a b) -> p a b", a=11)
            XR_, GR_, CX_, RR_, II_, AA_ = [x[0:RB] for x in (XR, GR, CX, RR, II, AA)]
            spv = ar(NRB * 6).rearrange("p (a b) -> p a b", a=6)[0:RB]
            rel = [ar(SEQ) for _ in range(4)]

            def on_act(dst, func=ACT.Copy):
                return lambda i, o, t: actv(dst(i), o, func, t, own=False)

            def on_dve(dst):
                return lambda i, o, t: cp(dst(i), o, t, own=False)

            project(W, o_iq, D, hn, SEQ, copy_to(lambda f: raw[:, f, :]))
            t_raw = [act.last(), dve.last()]
            s, slot, tok = load([
                (lambda sl, c=c, n=n: sl[:, 0:KC * 144].rearrange("p (k n) -> p k n", k=KC)[:, :, c:c + n],
                 W[:, o:o + n].rearrange("(k p) n -> p k n", p=128))
                for c, o, n in ((0, o_ik, 64), (64, o_ik, 80))])
            wv = slot[:, 0:KC * 144].rearrange("p (k n) -> p k n", k=KC)
            b = bank()
            for kc in range(KC):
                t = mm(PS[:, b, 0:SEQ], wv[:, kc, 0:128], hn[:, kc, :], kc == 0, kc == KC - 1, tok, *take(b),
                       inc=(kc == KC - 1))
            free[b] = [actv(ik_raw[:, 0, :], PS[:, b, 0:SEQ], ACT.Copy, t, own=False)]
            t_ikr = act.last()
            for i in range(2):
                b = bank()
                for kc in range(KC):
                    t = mm(PS[:, b, 0:16], hn[:, kc, i * 128:(i + 1) * 128], wv[:, kc, 128:144], kc == 0, kc == KC - 1,
                           *take(b), inc=(kc == KC - 1))
                free[b] = [ts(dve, iw[:, i, :], PS[:, b, 0:16], 1.0 / 32, None, MUL, ALU.bypass, t)]
            done(s, t)

            dve.op(lambda e: e.memset(XR_[:, :, 0:3], 0.0))
            project(W, o_xr, RB * NRB, hn, SEQ, on_act(lambda i: XR_[:, i, 3:SEQ + 3]), step=RB)
            t_xr = act.last()

            def rotate(dst, src, i, *waits):
                co, si = B2["cs"][i]
                n = src.shape[1]
                nb = (n + 1) // 2
                while turn[0] % 8 > 8 - nb:
                    turn[0] += 1
                b0 = turn[0] % 8
                turn[0] += nb
                pe.wait(*waits)
                for f in range(n):
                    b = b0 + f // 2
                    t = mm(PS[:, b, (f % 2) * 256:(f % 2 + 1) * 256], B2["rot"][i], src[:, f, :], True, True,
                           *take(b), inc=(f == n - 1))
                x = PS[:, b0:b0 + nb, :].rearrange("p b (c t) -> p (b c) t", c=2)[:, 0:n, :]
                sh = [128, n, SEQ]
                t = tt(dve, t1[:, 0:n, :], x, bc(si, sh, 1), MUL, t)
                for b in range(b0, b0 + nb):
                    free[b] = [t]
                tt(dve, src, src, bc(co, sh, 1), MUL)
                return tt(dve, dst, src, t1[:, 0:n, :], ADD)

            rotate(iq, raw, 1, *t_raw)
            t_rot = rotate(ik.unsqueeze(1), ik_raw, 1, t_ikr)
            for i in range(4):
                for n in range(NRB):
                    w = par("conv_w", (l * 4 + i) * NRB + n, 1, RB)
                    if i == 0:
                        ts(dve, CX_[:, n, :], XR_[:, n, 0:SEQ], w, par("conv_b", l * NRB + n, 1, RB), MUL, ADD, t_xr,
                           own=(n == 0))
                    else:
                        t_cx = stt(CX_[:, n, :], XR_[:, n, i:i + SEQ], w, CX_[:, n, :], MUL, ADD, own=(n == 0))
            lamp = par("lam", l * NRB, NRB, RB)
            e0, ab, u1, mk, ln, nsp = [spv[:, i, :] for i in range(6)]
            ts(dve, ab, lamp, -1.0, None, MUL)
            t = tt(dve, ab, ab, lamp, ALU.min)
            t = actv(e0, ab, ACT.Exp, t)
            t = ts(dve, u1, e0, 1.0, None, ADD, ALU.bypass, t)
            t = actv(ln, u1, ACT.Ln, t)
            ts(dve, u1, u1, -1.0, None, ADD, ALU.bypass, t)
            ts(dve, mk, u1, 0.0, None, ALU.is_equal)
            tt(dve, u1, u1, mk, ADD)
            tt(dve, ln, ln, mk, ADD)
            dve.op(lambda e: e.reciprocal(u1, u1))
            tt(dve, ln, ln, u1, MUL)
            tt(dve, ln, ln, e0, MUL)
            ts(dve, mk, lamp, -1.0, 0.0, MUL, MAX)
            tt(dve, nsp, ln, mk, ADD)
            ts(dve, nsp, nsp, -8.0, None, MUL)
            project(W, o_gr, RB * NRB, hn, SEQ, on_act(lambda i: GR_[:, i, :], ACT.Silu), step=RB)
            t_gr = act.last()
            used = [None] * 4
            pe.wait(t_rot)
            for i in range(2):
                nk = 128 * (i + 1)
                for h in range(16):
                    p0 = 64 * (h % 2)
                    b = bank()
                    t = mm(PS[:, b, 0:nk], iq[p0:p0 + 64, h // 2, i * 128:(i + 1) * 128], ik[p0:p0 + 64, 0:nk], True,
                           True, *take(b), inc=True)
                    x = rel[h % 4][:, 0:nk]
                    t = actv(x, PS[:, b, 0:nk], ACT.Relu, t, *([used[h % 4]] if used[h % 4] else []), own=False)
                    free[b] = [t]
                    o = score[:, i, 0:nk]
                    if h == 0:
                        t = ts(dve, o, x, iw[:, i, h:h + 1], None, MUL, ALU.bypass, t)
                    else:
                        t = stt(o, x, iw[:, i, h:h + 1], o, MUL, ADD, t)
                    used[h % 4] = t
            t_idx = pe.last()
            project(W, o_q, D, hn, SEQ, on_act(lambda f: raw[:, f, :]), t_rot)
            t_raw = act.last()
            pe.wait(t_cx)
            for nm, dst, bn in (("w_rg_2", RR_, "b_rg"), ("w_ig_2", II_, "b_ig")):
                def view(slot):
                    return slot[0:RB, 0:NRB * RB].rearrange("p (n d) -> p n d", n=NRB)
                s, slot, tok = load([(view, A[nm][l].rearrange("n c d -> c n d"))])
                for n in range(NRB):
                    b = bank()
                    t = mm(PS[0:RB, b, 0:SEQ], view(slot)[:, n, :], CX_[:, n, :], True, True, tok, *take(b), inc=True)
                    free[b] = [actv(dst[:, n, :], PS[0:RB, b, 0:SEQ], ACT.Sigmoid, t,
                                    bias=par(bn, l * NRB + n, 1, RB), own=False)]
                done(s, t)
            t_ri, t_gate = act.last(), pe.last()
            t_rot = rotate(q, raw, 0, t_raw)
            t = tt(dve, RR_, RR_, bc(nsp, [RB, NRB, SEQ], 2), MUL, t_ri)
            t = actv(flat(AA_), flat(RR_), ACT.Exp, t)
            t = actv(flat(RR_), flat(RR_), ACT.Tanh, scale=-1.0)
            project(W, o_k, D, hn, SEQ, on_act(lambda f: raw[:, f, :]), t_rot)
            t_raw = act.last()
            tt(dve, flat(II_), flat(II_), flat(CX_), MUL)
            tt(dve, flat(CX_), flat(AA_), flat(AA_), MUL, t, t_gate)
            t = stt(flat(CX_), flat(CX_), 1.0, flat(RR_), ADD, MUL)
            t = actv(flat(CX_), flat(CX_), ACT.Sqrt, t, own=False)
            project(W, o_mb, D, hn, SEQ, on_act(lambda i: M[:, i, :], ACT.Sigmoid))
            t_mb = act.last()
            t_rot = rotate(k, raw, 0, t_raw)
            dve.op(lambda e: e.memset(AA_[:, :, 0:1], 0.0))
            tt(dve, flat(II_), flat(II_), flat(CX_), MUL, t)
            dve.op(lambda e: e.tensor_tensor_scan(flat(CX_), flat(AA_), flat(II_), 0.0, MUL, ADD))
            t = tt(dve, flat(CX_), flat(CX_), flat(GR_), MUL, t_gr)
            moves = []
            for n in range(NRB):
                f = n * RB
                while f < (n + 1) * RB:
                    m = min((n + 1) * RB, (f // 128 + 1) * 128) - f
                    moves.append((HC[f % 128:f % 128 + m, f // 128, :], CX[f - n * RB:f - n * RB + m, n, :]))
                    f += m
            pool.wait(t)
            for o, i in moves:
                pool.op(lambda e, o=o, i=i: e.dma_start(o, i).then_inc(s_move, 16), own=False, inc=False)
            nmove[0] += 16 * len(moves)
            t_hc = (s_move, nmove[0])
            for i in range(2):
                nk = 128 * (i + 1)
                o, ca = score[:, i, 0:nk], B2["causal"][:, i, 0:nk]
                tt(dve, o, o, ca, ADD)
                for r in range(8):
                    mx = m8[:, 8 * (r % 2):8 * (r % 2) + 8]
                    dve.op(lambda e, mx=mx, o=o: e.max(mx, o))
                    dve.op(lambda e, mx=mx, o=o: e.match_replace(o, mx, o, TAKEN))
                ts(dve, o, o, TAKEN, -NEG, ALU.is_equal, MUL)
                stt(bias[:, i, 0:nk], o, NEG, ca, ADD, ADD)
            act.wait(t_rot)
            for u in range(4):
                s, wv, tok = cols(W, o_v + u * 256, 256)
                for i in range(2):
                    b = bank()
                    for kc in range(KC):
                        t = mm(PS[:, b, 0:256], hn[:, kc, i * 128:(i + 1) * 128], wv[:, kc, :], kc == 0, kc == KC - 1,
                               tok, *take(b), inc=(kc == KC - 1))
                    free[b] = [actv(V[:, i, u * 256:(u + 1) * 256], PS[:, b, 0:256], ACT.Copy, t, own=False)]
                done(s, t)
            act.wait(t_idx)
            project(W, o_ga, D, hn, SEQ, on_act(lambda i: GA[:, i, :], ACT.Silu))
            barrier()
            top[0] = m1
            NP_ = 4
            S = [ar(SEQ) for _ in range(NP_)]
            Ex = [ar(SEQ) for _ in range(NP_)]
            st = [ar(4) for _ in range(NP_)]
            pT = [ar3(2, 128) for _ in range(2)]
            top[0] = m1 + NRB * (SEQ + 3)
            MA = ar3(KC, SEQ)
            project(W, o_ma, D, hn, SEQ, on_act(lambda i: MA[:, i, :], ACT.Sigmoid))
            oT = raw
            items = [(h, i) for h in range(8) for i in range(2)]
            t_ex, t_nrm, t_tr, t_pc, t_pv = {}, {}, {}, {}, {}
            SC = float(128 ** -0.5)
            other = contract_units(A["w_out_rnn_2"][l], 11, HC, SEQ,
                                   lambda i, o, t: tt(dve, M[:, i, :], M[:, i, :], o, MUL, t, own=False),
                                   t_hc, banks=[4, 5, 6, 7])

            def first(n):
                h, i = items[n]
                nk = 128 * (i + 1)
                b = n % 2
                t = mm(PS[:, b, 0:nk], q[:, h, i * 128:(i + 1) * 128], k[:, h, 0:nk], True, True, *take(b), inc=True)
                s_, x_ = S[n % NP_][:, 0:nk], st[n % NP_]
                w = [t_ex[n - NP_]] if n >= NP_ else []
                t = tt(dve, s_, PS[:, b, 0:nk], bias[:, i, 0:nk], ADD, t, *w)
                free[b] = [t]
                dve.op(lambda e: e.tensor_reduce(x_[:, 0:1], s_, AX, MAX))
                t = ts(dve, x_[:, 1:2], x_[:, 0:1], -SC, None, MUL)
                w = [t_nrm[n - NP_], t_tr[n - NP_]] if n >= NP_ else []
                t_ex[n] = actv(Ex[n % NP_][:, 0:nk], s_, ACT.Exp, t, *w, bias=x_[:, 1:2], scale=SC,
                               accum=x_[:, 2:3], own=False)

            def second_(n):
                h, i = items[n]
                nk = 128 * (i + 1)
                e_, x_ = Ex[n % NP_][:, 0:nk], st[n % NP_]
                dve.op(lambda e: e.reciprocal(x_[:, 3:4], x_[:, 2:3]), t_ex[n])
                t_nrm[n] = ts(dve, e_, e_, x_[:, 3:4], None, MUL)

            def third(n):
                h, i = items[n]
                e_ = Ex[n % NP_]
                w = take(2)
                for kt in range(i + 1):
                    t = tr(PS[:, 2, kt * 128:(kt + 1) * 128], e_[:, kt * 128:(kt + 1) * 128], ident, t_nrm[n], *w,
                           inc=(kt == i))
                t_tr[n] = t
                p_ = pT[n % 2]
                t = actv(flat(p_)[:, 0:128 * (i + 1)], PS[:, 2, 0:128 * (i + 1)], ACT.Copy, t,
                         *([t_pv[n - 2]] if n >= 2 else []), own=False)
                free[2] = [t]
                t_pc[n] = t

            def fourth(n):
                h, i = items[n]
                p_ = pT[n % 2]
                for kt in range(i + 1):
                    t = mm(PS[:, 3, 0:128], V[:, kt, h * 128:(h + 1) * 128], p_[:, kt, :], kt == 0, kt == i, t_pc[n],
                           *take(3), inc=(kt == i))
                t_pv[n] = t
                g = GA[:, h, i * 128:(i + 1) * 128]
                free[3] = [tt(dve, oT[:, h, i * 128:(i + 1) * 128], PS[:, 3, 0:128], g, MUL, t, own=False)]

            act.wait(t_mb)
            for n in range(len(items) + 3):
                if n < len(items):
                    first(n)
                if 1 <= n <= len(items):
                    second_(n - 1)
                if n >= 3:
                    fourth(n - 3)
                if 2 <= n < len(items) + 2:
                    third(n - 2)
                if n % 3 == 1:
                    next(other, None)
            for _ in other:
                pass
            tmp = [ar(SEQ) for _ in range(2)]

            def merge(i, o, t):
                x = tmp[i % 2]
                t = tt(dve, x, MA[:, i, :], o, MUL, t)
                tt(dve, M[:, i, :], M[:, i, :], x, ADD)
                return t
            project(A["w_out_attn_2"][l], 0, D, oT, SEQ, merge, dve.last())

            def residual(i, o, t):
                return tt(dve, X2[:, i, :], X2[:, i, :], o, ADD, t)
            project(A["w_o_2"][l], 0, D, M, SEQ, residual, dve.last())
            barrier()
            top[0] = m0

        def final():
            O = ar3(KC, SEQ)
            t = rms(O, par("final_g", 0, 8), dve.last())
            B2["out"] = O

        stage_list = [attention, ffn, rwkv, moe, tables, lambda: second(0), lambda: second(1), final]
        for st_ in stage_list[SKIP or 0:stages]:
            st_()
        toks = [x.last() for x in (pe, dve, act, pool) if x.n]
        src = B2["out"] if stages > 7 else H
        fin = sp.start(out, src, s_out, 16, *toks)
        sp.items.append(fin)

        block = ctx.enter_context(nc.Block())

        @block.sync
        def _(e):
            sp.emit(e)

        @block.tensor
        def _(e):
            pe.emit(e)

        @block.vector
        def _(e):
            dve.emit(e)

        @block.scalar
        def _(e):
            act.emit(e)

        @block.gpsimd
        def _(e):
            pool.emit(e)


def constants():
    f = np.float32
    base = np.zeros((128, 448), f)
    base[:, 0:128] = np.eye(128)
    base[:, 128:256] = 1.0
    base[0:64, 256:320] = 1.0
    base[:, 384:448] = np.tile(np.eye(64), (2, 1))
    base[64:128, 320:384] = 1.0
    dist = np.zeros((128, 3, T), f)
    for i, (q0, qn) in enumerate(QT):
        dist[0:qn, i, :] = np.abs(np.arange(q0, q0 + qn)[:, None] - np.arange(T)[None, :])
    rw = np.zeros((128, NC_RW), f)
    rw[:, C_SCAN:C_SCAN + TS] = (np.arange(TS) % CH != 0)
    i = np.arange(64)
    for l, s in enumerate(SCAN_LEVELS):
        same = (i[:, None] // (2 * s)) == (i[None, :] // (2 * s))
        low = same & (i[:, None] % (2 * s) >= s) & (i[None, :] % (2 * s) < s)
        for x, m in enumerate([low, low.T]):
            o = C_LVL + (x * len(SCAN_LEVELS) + l) * 64
            rw[:, o:o + 64] = np.tile(m, (2, 1))
    for d in range(2):
        j, t = i[:, None], i[None, :]
        strict, incl = (j < t, j <= t) if d == 0 else (j > t, j >= t)
        for x in range(2):
            o = C_AM + (2 * d + x) * 128
            rw[:, o:o + 64] = np.tile(strict, (2, 1))
            rw[:, o + 64:o + 128] = np.tile(incl * (-1.0 if x else 1.0), (2, 1))
    b2 = np.zeros((128, NC_B2), f)
    for x, half in enumerate((64, 32)):
        for m in range(128):
            if m % (2 * half) < half:
                b2[m + half, x * 128 + m] = -1.0
            else:
                b2[m - half, x * 128 + m] = 1.0
        dim = 2 * half
        inv = np.float32(10000.0) ** (-np.arange(0, dim, 2, dtype=f) / np.float32(dim))
        b2[:, 768 + x] = inv[np.arange(128) % half]
    for x in range(2):
        qp = x * 128 + np.arange(128)
        b2[:, 256 + x * 256:512 + x * 256] = np.where(np.arange(SEQ)[None, :] <= qp[:, None], 0.0, NEG)
    moe = np.zeros((128, 224), f)
    moe[0:96, 0:96] = np.arange(96)[:, None] < np.arange(96)[None, :]
    moe[:, 96:192] = np.arange(96)
    moe[:, 192] = np.arange(128)
    return {"c_moe": moe, "c_b2": b2, "c_base": base, "c_dist": dist.reshape(128, 3 * T), "c_rw": rw}


def by_partition(v, p=128):
    return np.ascontiguousarray(v.reshape(-1, p).T)


def lay_out(inputs):
    g = {k: np.asarray(v) for k, v in inputs.items()}
    par = np.zeros((128, NPAR), np.float32)

    def put(name, m):
        o = POFF[name]
        par[0:m.shape[0], o:o + m.shape[1]] = m
    for name, src in (("ln_g", "ln_g"), ("ln_b", "ln_b"), ("subln", "attn_subln_g"), ("mu", "rw_mu"), ("w0", "rw_w0"),
                      ("a0", "rw_a0"), ("k_k", "rw_k_k"), ("k_a", "rw_k_a"), ("r_k", "rw_r_k"),
                      ("lnx_g", "rw_lnx_g"), ("lnx_b", "rw_lnx_b"), ("norm_g", "norm_g_2"), ("final_g", "final_g_2")):
        put(name, by_partition(g[src]))
    for name, src in (("conv_w", "conv_w_2"), ("conv_b", "conv_b_2"), ("b_rg", "b_rg_2"), ("b_ig", "b_ig_2"),
                      ("lam", "lru_lambda_2")):
        put(name, by_partition(g[src], RB))
    lam = np.concatenate([g[n].reshape(-1) for n in ("attn_lam_q1", "attn_lam_k1", "attn_lam_q2", "attn_lam_k2")])
    put("lamv", np.broadcast_to(lam, (128, 256)))
    put("b_router", np.broadcast_to(g["moe_b_router"].reshape(-1), (128, NE)))
    h = np.concatenate([g["meta"], g["x"][0]], 0)
    hT = h.T.reshape(KC, 128, T).transpose(1, 0, 2).reshape(128, KC * T)
    arrays = {"par": par, "hT": np.ascontiguousarray(hT)}
    arrays["pos"] = np.ascontiguousarray(np.broadcast_to(g["positions_2"].reshape(1, SEQ), (128, SEQ)))
    arrays.update(constants())
    for n in BIG:
        arrays[n] = np.ascontiguousarray(g[n])
    return arrays


BIG = ["attn_w_in", "attn_w_o", "ffn_w_gate", "ffn_w_up", "ffn_w_down", "rw_w_rkv", "rw_w1", "rw_w2", "rw_a1", "rw_a2",
       "rw_g1", "rw_g2", "rw_w_o", "moe_w_router", "moe_w_gate", "moe_w_up", "moe_w_down",
       "w_in_2", "w_rg_2", "w_ig_2", "w_out_attn_2", "w_out_rnn_2", "w_o_2"]


def kernel(**inputs):
    import concourse.bacc as bacc
    from concourse.bass_utils import run_bass_kernel_spmd

    arrays = lay_out(inputs)
    nc = bacc.Bacc("TRN2", target_bir_lowering=False, num_devices=1)
    A = {n: nc.dram_tensor(f"in_{n}", a.shape, mybir.dt.from_np(a.dtype), kind="ExternalInput").ap()
         for n, a in arrays.items()}
    out = nc.dram_tensor("out_dram", (128, KC, SEQ), F32, kind="ExternalOutput").ap()
    build(nc, A, out)
    r = run_bass_kernel_spmd(nc, [{f"in_{n}": a for n, a in arrays.items()}], core_ids=[0])
    o = r.results[0]["out_dram"]
    return np.ascontiguousarray(o.transpose(2, 1, 0).reshape(1, SEQ, D))
```

```python
import concourse.bass as bass
from concourse import mybir
from contextlib import ExitStack
import numpy as np

F32 = mybir.dt.float32
I32 = mybir.dt.int32
F32R = mybir.dt.float32r
ALU = mybir.AluOpType
ACT = mybir.ActivationFunctionType
AX = mybir.AxisListType.X
MUL, ADD, SUB, MAX = ALU.mult, ALU.add, ALU.subtract, ALU.max

D = 1024
KC = 8
NMETA = 16
SEQ = 256
T = NMETA + SEQ
ALPHA = 4.0 ** 0.25
QT = [(0, 96), (96, 96), (192, 80)]
CH = 55
NCH = 5
TS = 284
MID = CH // 2
NRING = 3
NMORE = 4
CAP = 96
NEG = -1.0e30
TAKEN = -3.0e38
FFN = 2816
FE = 3584
NE = 8
RB = 88
NRB = 16
SCAN_LEVELS = [1, 2, 4, 8, 16, 32]
TWO_PI = 2.0 * np.pi

PARAMS = [("ln_g", 32), ("ln_b", 32), ("subln", 1), ("mu", 96), ("w0", 16), ("a0", 16), ("k_k", 8), ("k_a", 8),
          ("r_k", 8), ("lnx_g", 8), ("lnx_b", 8), ("norm_g", 16), ("final_g", 8), ("conv_w", 128),
          ("conv_b", 32), ("b_rg", 32), ("b_ig", 32), ("lam", 32), ("lamv", 256), ("b_router", 8)]
POFF = {}
_o = 0
for _n, _w in PARAMS:
    POFF[_n] = _o
    _o += _w
NPAR = _o

C_SCAN = 0
C_LVL = C_SCAN + TS
C_AM = C_LVL + 2 * len(SCAN_LEVELS) * 64
C_SPREAD = C_AM + 4 * 128
NC_RW = C_SPREAD + D
NC_B2 = 256 + 512 + 2


class Engine:

    def __init__(self, sem):
        self.sem, self.n, self.items, self.passed = sem, 0, [], {}

    def wait(self, *toks):
        for sem, val in toks:
            if self.passed.get(id(sem), 0) < val:
                self.passed[id(sem)] = val
                self.items.append((sem, val))

    def op(self, fn, *waits, own=True, inc=True):
        self.wait(*waits)
        if own and self.n:
            self.wait((self.sem, self.n))
        if inc:
            self.n += 1
        self.items.append((fn, inc))
        return self.last()

    def last(self):
        return (self.sem, self.n)

    def emit(self, e, items=None):
        for it in self.items if items is None else items:
            a, b = it[0], it[1]
            if a == "branch":
                flag = e.value_load(b)
                with e.If(flag != 0):
                    self.emit(e, it[2])
                with e.Else():
                    self.emit(e, it[3])
            elif callable(a):
                ins = a(e)
                if b:
                    ins.then_inc(self.sem, 1)
            else:
                e.wait_ge(a, b)


class Loads:

    def __init__(self):
        self.items = []

    def start(self, dst, src, sem, count, *waits):
        for s, v in waits:
            self.items.append((s, v))
        self.items.append((lambda e: e.dma_start(dst, src), sem))
        return (sem, count)

    def emit(self, e, items=None):
        for it in self.items if items is None else items:
            a, b = it[0], it[1]
            if a == "branch":
                flag = e.value_load(b)
                with e.If(flag != 0):
                    self.emit(e, it[2])
                with e.Else():
                    self.emit(e, it[3])
            elif callable(a):
                a(e).then_inc(b, 16)
            else:
                e.wait_ge(a, b)


def build(nc, A, out, stages=99):
    ctx = ExitStack()
    with ctx:
        def sb(name, shape, dt=F32):
            return ctx.enter_context(nc.sbuf_tensor(name, shape, dt))

        def sem(name):
            return ctx.enter_context(nc.semaphore(name))

        RING = sb("RING", [128, NRING, 2048])
        PAR = sb("PAR", [128, NPAR])
        CB = sb("CB", [128, 592])
        H = sb("H", [128, KC, T])[:, :, :]
        flag = sb("flag", [128, 1], I32)[:, :]
        NAR = 41904
        at = -(-nc.sbuf_base // 32) * 32
        AR = sb("AR", [128, NAR])
        part_tensors = {}
        PS = ctx.enter_context(nc.psum_tensor("PS", [128, 8, 512], F32))

        ident = CB[:, 0:128]
        ones = CB[:, 128:256]
        blk = CB[:, 256:384]
        one_of_8 = CB[:, 576:591]
        by_head = CB[:, 448:576].rearrange("p (f h) -> p f h", f=KC)

        s_pe, s_dve, s_act, s_pool = sem("s_pe"), sem("s_dve"), sem("s_act"), sem("s_pool")
        s_ring = [sem(f"s_ring{i}") for i in range(NRING + NMORE)]
        s_in = [sem(f"s_in{i}") for i in range(8)]
        s_out = sem("s_out")
        s_move = sem("s_move")
        def program(plan):
            pe, dve, act, pool, sp = Engine(s_pe), Engine(s_dve), Engine(s_act), Engine(s_pool), Loads()

            def par(name, i=0, n=1, p=128):
                o = POFF[name] + i
                return PAR[0:p, o:o + n]

            nmove = [0]
            top = [0]

            def ar(cols):
                o = top[0]
                top[0] += -(-cols // 8) * 8
                assert top[0] <= NAR, (top[0], NAR)
                return AR[:, o:o + cols]

            def ar3(a, b):
                return ar(a * b).rearrange("p (a b) -> p a b", a=a)

            def barrier():
                toks = [x.last() for x in (pe, dve, act, pool) if x.n]
                for x in (pe, dve, act, pool):
                    x.wait(*toks)
                return toks

            parted = []

            def extent(a):
                return a.offset % NAR, 1 + sum((n - 1) * st for st, n in a.ap[1:])

            def two_parts(*tiles):
                for a in tiles:
                    key = extent(a)
                    parted.insert(0, key)
                    if key not in part_tensors:
                        part_tensors[key] = nc.alloc_sbuf_tensor_at(f"PART_{key[0]}_{key[1]}", [128, key[1]], F32R,
                                                                    offset=at + 4 * key[0])
                return tiles

            def rounded(a):
                c, n = extent(a)
                key = next(k for k in parted if k[0] <= c and c + n <= k[0] + k[1])
                return bass.AP(part_tensors[key], a.offset // NAR * key[1] + c - key[0],
                               [[key[1], a.ap[0][1]]] + [list(x) for x in a.ap[1:]])

            free = [[] for _ in range(8)]
            turn = [0]

            def bank():
                b = turn[0] % 8
                turn[0] += 1
                return b

            def take(b):
                t, free[b] = free[b], []
                return t

            nload = [0]
            slots = [RING[:, i, :] for i in range(NRING)]
            ring_count = [0] * (NRING + NMORE)
            ring_free = [[] for _ in range(NRING + NMORE)]
            asked = []
            sec = {}

            def section(ring=()):
                toks = [x.last() for x in (pe, dve, act, pool) if x.n]
                asked.append([])
                sec.update(want=plan[len(asked) - 1] if plan else asked[-1], loads=[], taken=0, parts=[], nsplit=0,
                           nused=0, ring=list(ring), free=[list(toks) for _ in ring])

            def ring_of(n, width=1024):
                return [two_parts(ar(width), ar(width)) for _ in range(n)]

            def start_loads(upto):
                while len(sec["loads"]) < min(upto, len(sec["want"])):
                    pairs, views = sec["want"][len(sec["loads"])]
                    s = nload[0] % len(slots)
                    nload[0] += 1
                    waits, ring_free[s] = ring_free[s], None
                    for view, src in pairs:
                        ring_count[s] += 16
                        sp.start(view(slots[s]), src, s_ring[s], ring_count[s], *waits)
                        waits = []
                    sec["loads"].append((s, slots[s], (s_ring[s], ring_count[s])))
                    for n, view in enumerate(views):
                        sec["parts"].append((len(sec["loads"]) - 1, view, n == len(views) - 1, []))

            def ask(pairs, views=()):
                asked[-1].append((pairs, views))
                sec["taken"] += 1
                start_loads(sec["taken"])
                return sec["loads"][sec["taken"] - 1]

            def load(pairs):
                return ask(pairs)

            def done(s, tok):
                ring_free[s] = [tok]

            def high_low(hi, lo, x, *waits, own=True, eng=None):
                t = actv(rounded(hi), x, ACT.Copy, *waits, own=own)
                return tt(eng or dve, rounded(lo), x, rounded(hi).bitcast(F32), SUB, t, own=own)

            def part():
                n = sec["nused"]
                sec["nused"] += 1
                ring = sec["ring"]
                run_ahead(n + len(ring))
                for _ in range(pace[0]):
                    if beside:
                        beside.pop(0)()
                hi, lo = sec["parts"][n][4]

                def release(tok):
                    sec["free"][n % len(ring)] = [tok]
                return hi, lo, sec["parts"][n][3][0], release

            beside, pace = [], [1]

            def rest():
                while beside:
                    beside.pop(0)()

            def run_ahead(upto=None):
                ring = sec["ring"]
                while sec["nsplit"] < (len(ring) if upto is None else upto):
                    if sec["nsplit"] >= len(sec["parts"]):
                        if len(sec["loads"]) >= len(sec["want"]):
                            break
                        start_loads(len(sec["loads"]) + 1)
                        continue
                    i = sec["nsplit"]
                    sec["nsplit"] += 1
                    ld, view, last, _ = sec["parts"][i]
                    s, slot, tok = sec["loads"][ld]
                    x = view(slot)
                    tiles = [r[0:x.shape[0], 0:x.shape[1] * x.shape[2]].rearrange("p (a b) -> p a b", a=x.shape[1])
                             for r in ring[i % len(ring)]]
                    waits, sec["free"][i % len(ring)] = sec["free"][i % len(ring)], None
                    t = high_low(*tiles, x, tok, *waits, own=False)
                    sec["parts"][i] = (ld, view, last, [t], tiles)
                    if last:
                        ring_free[s] = [p[3][0] for p in sec["parts"] if p[0] == ld]
            def mm3(o, wh, wl, xh, xl, start, stop, *waits, inc=False):
                wh, wl, xh, xl = [rounded(v) for v in (wh, wl, xh, xl)]
                mm(o, wh, xh, start, False, *waits)
                mm(o, wh, xl, False, False)
                return mm(o, wl, xh, False, stop, inc=inc)

            def cols(W, c0, n):
                def view(slot):
                    return slot[:, 0:KC * n].rearrange("p (k n) -> p k n", k=KC)
                s, slot, tok = load([(view, W[:, c0:c0 + n].rearrange("(k p) n -> p k n", p=128))])
                return s, view(slot), tok

            def rows(W, f0, nf, c0, p=128):
                def view(slot):
                    return slot[0:p, 0:nf * 512].rearrange("p (k n) -> p k n", k=nf)
                s, slot, tok = load([(view, W[f0 * p:(f0 + nf) * p, c0:c0 + 512].rearrange("(k p) n -> p k n", p=p))])
                return s, view(slot), tok

            def split_cols(W, c0, n, views):
                def view(slot):
                    return slot[:, 0:KC * n].rearrange("p (k n) -> p k n", k=KC)
                ask([(view, W[:, c0:c0 + n].rearrange("(k p) n -> p k n", p=128))],
                    [lambda slot, v=v: v(view(slot)) for v in views])

            def split_rows(W, f0, nf, c0):
                def view(slot):
                    return slot[:, 0:nf * 512].rearrange("p (k n) -> p k n", k=nf)
                ask([(view, W[f0 * 128:(f0 + nf) * 128, c0:c0 + 512].rearrange("(k p) n -> p k n", p=128))],
                    [lambda slot, f=f: view(slot)[:, f:min(f + 2, nf), :] for f in range(0, nf, 2)])

            def mm(o, lhsT, rhs, start, stop, *waits, inc=False):
                return pe.op(lambda e: e.matmul(o, lhsT, rhs, start=start, stop=stop), *waits, own=False, inc=inc)

            def tr(o, i, idn, *waits, inc=False):
                return pe.op(lambda e: e.transpose(o, i, idn), *waits, own=False, inc=inc)

            def tt(eng, o, a, b, op, *waits, own=True):
                return eng.op(lambda e: e.tensor_tensor(o, a, b, op), *waits, own=own)

            def ts(eng, o, a, s1, s2, op0, op1=ALU.bypass, *waits, own=True):
                return eng.op(lambda e: e.tensor_scalar(o, a, s1, s2, op0, op1), *waits, own=own)

            def stt(o, a, s, b, op0, op1, *waits, own=True):
                return dve.op(lambda e: e.scalar_tensor_tensor(o, a, s, b, op0, op1), *waits, own=own)

            def actv(o, i, f, *waits, bias=0.0, scale=1.0, accum=None, own=True):
                if accum is None:
                    return act.op(lambda e: e.activation(o, i, f, bias=bias, scale=scale), *waits, own=own)
                return act.op(lambda e: e.activation(o, i, f, bias=bias, scale=scale, accum_out=accum), *waits, own=own)

            def cp(o, i, *waits, own=True):
                return dve.op(lambda e: e.tensor_copy(o, i), *waits, own=own)

            def bc(a, shape, axis):
                return a.unsqueeze(axis).to_broadcast(shape)

            def flat(a):
                return a.rearrange("p a b -> p (a b)")

            def branch(flag, *sides):
                engines = (pe, dve, act, pool)
                begin = [(x.n, dict(x.passed), x.items) for x in engines]
                sp_items, mem, start = sp.items, top[0], (list(ring_count), list(ring_free), nload[0], list(free))
                ends, queues, counts = [], [], []
                tiles = list(parted)
                for side in sides:
                    for x, (n, passed, _) in zip(engines, begin):
                        x.n, x.passed, x.items = n, dict(passed), []
                    sp.items, top[0], nload[0] = [], mem, start[2]
                    parted[:] = tiles
                    ring_count[:], ring_free[:], free[:] = start[0], start[1], start[3]
                    side()
                    ends.append([x.n for x in engines])
                    queues.append([x.items for x in engines] + [sp.items])
                    counts.append((list(ring_count), nload[0]))
                assert counts[0] == counts[1]
                for i, (x, (n, passed, items)) in enumerate(zip(engines, begin)):
                    most = max(e[i] for e in ends)
                    for e, q in zip(ends, queues):
                        if e[i] < most:
                            q[i].append((x.sem, e[i]))
                            q[i].append((lambda eng, x=x, k=most - e[i]: eng.sem_inc(x.sem, k), False))
                    x.n, x.passed, x.items = most, dict(passed), items
                    if queues[0][i] or queues[1][i]:
                        items.append(("branch", flag, queues[0][i], queues[1][i]))
                sp.items = sp_items
                sp.items.append(("branch", flag, queues[0][4], queues[1][4]))
                top[0] = mem
                toks = [x.last() for x in engines if x.n]
                for f in range(8):
                    free[f] = list(toks)
                for f in range(len(ring_free)):
                    ring_free[f] = list(toks)

            def project(*args, **kw):
                for _ in project_units(*args, **kw):
                    pass

            def project_units(W, c0, n, X, Tn, evac, *waits, step=128, banks=None, xt=None):
                xh, xl = X
                per = 256 // step
                pe.wait(*waits)
                i = 0
                for u0 in range(0, n, per * step):
                    w = min(per * step, n - u0)
                    js = range(0, w, step)
                    split_cols(W, c0 + u0, w, [lambda v, j=j, w=w: v[:, :, j:min(j + step, w)] for j in js])
                    for j0 in js:
                        m = min(step, w - j0)
                        wh, wl, tok, release = part()
                        b = banks[i % len(banks)] if banks else bank()
                        o = PS[0:m, b, 0:Tn]
                        for k in range(KC):
                            t = mm3(o, wh[:, k, :], wl[:, k, :], xh[:, k, :], xl[:, k, :], k == 0, k == KC - 1, tok,
                                    *take(b), *([xt[k]] if xt else []), inc=(k == KC - 1))
                        release(t)
                        free[b] = [evac(i, o, t)]
                        i += 1
                        yield

            def contract(*args, **kw):
                for _ in contract_units(*args, **kw):
                    pass

            def contract_units(W, nf, X, Tn, evac, *waits, banks=None):
                xh, xl = X
                pe.wait(*waits)
                for half in range(2):
                    bs = banks or [bank() for _ in range(4)]
                    for f0 in range(0, nf, 4):
                        n = min(4, nf - f0)
                        split_rows(W, f0, n, half * 512)
                        for g0 in range(f0, f0 + n, 2):
                            wh, wl, tok, release = part()
                            for f in range(g0, min(g0 + 2, f0 + n)):
                                end = f == nf - 1
                                last = f == min(g0 + 2, f0 + n) - 1
                                for j in range(4):
                                    c = slice(j * 128, (j + 1) * 128)
                                    t = mm3(PS[:, bs[j], 0:Tn], wh[:, f - g0, c], wl[:, f - g0, c], xh[:, f, :],
                                            xl[:, f, :], f == 0, end, tok, *take(bs[j]),
                                            inc=(last and j == 3 or end))
                                    if end and j < 3:
                                        free[bs[j]] = [evac(half * 4 + j, PS[:, bs[j], 0:Tn], t)]
                            release(t)
                            if end:
                                free[bs[3]] = [evac(half * 4 + 3, PS[:, bs[3], 0:Tn], t)]
                            yield

            def values(W, c0, X, tiles, V):
                xh, xl = X
                for u in range(4):
                    split_cols(W, c0 + u * 256, 256, [lambda v, k0=k0: v[:, k0:k0 + 4, :] for k0 in (0, 4)])
                    bs = [bank() for _ in tiles]
                    for k0 in (0, 4):
                        wh, wl, tok, release = part()
                        for b, (q0, qn) in zip(bs, tiles):
                            for k in range(4):
                                t = mm3(PS[0:qn, b, 0:256], xh[:, k0 + k, q0:q0 + qn], xl[:, k0 + k, q0:q0 + qn],
                                        wh[:, k, :], wl[:, k, :], k0 + k == 0, k0 + k == KC - 1, tok, *take(b),
                                        inc=(k == 3))
                            if k0:
                                i = bs.index(b)
                                free[b] = [actv(V[0:qn, i, u * 256:(u + 1) * 256], PS[0:qn, b, 0:256], ACT.Copy, t,
                                                own=False)]
                        release(t)

            def copy_to(dst):
                def evac(i, o, t):
                    if i % 2:
                        return actv(dst(i), o, ACT.Copy, t)
                    return cp(dst(i), o, t)
                return evac

            def sum_rows(X, n, Tn, lhsT, *waits):
                b = bank()
                pe.wait(*waits)
                for k in range(n):
                    t = mm(PS[:, b, 0:Tn], lhsT, X[:, k, :], k == 0, k == n - 1, *take(b), inc=(k == n - 1))
                return b, PS[:, b, 0:Tn], t

            def rsqrt(dst, src, scale, eps, tmp, *waits):
                t = ts(dve, tmp, src, scale, eps, MUL, ADD, *waits)
                t1 = actv(tmp, tmp, ACT.Sqrt, t)
                return t, dve.op(lambda e: e.reciprocal(dst, tmp), t1)

            def layer_norm(Z, gi, Tn, O, *waits):
                m0 = top[0]
                Q, R, R2 = ar3(KC, Tn), ar(Tn), ar(Tn)
                b, s, t = sum_rows(Z, KC, Tn, ones, *waits)
                td = stt(Z, bc(s, [128, KC, Tn], 1), -1.0 / D, Z, MUL, ADD, t)
                free[b] = [td]
                tq = actv(flat(Q), flat(Z), ACT.Square, td)
                b, s, t = sum_rows(Q, KC, Tn, ones, tq)
                t1, t2 = rsqrt(R, s, 1.0 / D, 1e-5, R2, t)
                free[b] = [t1]
                tt(dve, Z, Z, bc(R, [128, KC, Tn], 1), MUL)
                for k in range(KC):
                    t = ts(dve, O[:, k, :], Z[:, k, :], par("ln_g", gi * 8 + k), par("ln_b", gi * 8 + k), MUL, ADD,
                           own=(k == 0))
                barrier()
                top[0] = m0
                return t

            t_par = sp.start(PAR[:, :], A["par"], s_in[0], 32)
            t_par = sp.start(CB[:, :], A["c_base"], s_in[0], 32)
            t_h = sp.start(flat(H[:, :, :]), A["hT"], s_in[1], 16)
            for x in (pe, dve, act):
                x.wait(t_par, t_h)

            def attention():
                m0 = top[0]
                q, k, oT = ar3(KC, T), ar3(KC, T), ar3(KC, T)
                V = ar3(3, D)
                dist = ar3(3, T)
                NP_ = 4
                S = [ar3(2, T) for _ in range(NP_)]
                Ex = [ar3(2, T) for _ in range(NP_)]
                Ac = [ar(T) for _ in range(NP_)]
                aT = [ar3(3, T) for _ in range(2)]
                st = [ar(8) for _ in range(NP_)]
                sm = ar(64)
                lam = ar(4)
                osq, n8, r8 = ar3(KC, T), ar(T)[0:8], ar(T)[0:8]
                X = two_parts(*[ar3(KC, T) for _ in range(2)])
                section(ring_of(4))
                t_x = {k: high_low(X[0][:, k, :], X[1][:, k, :], H[:, k, :], own=False) for k in range(KC)}
                run_ahead(1)
                t_dist = sp.start(flat(dist), A["c_dist"], s_in[2], 16)
                W = A["attn_w_in"][0]
                lv = POFF["lamv"]
                for i in range(2):
                    a, b = PAR[:, lv + i * 128:lv + i * 128 + 64], PAR[:, lv + i * 128 + 64:lv + i * 128 + 128]
                    tt(dve, sm, a, b, MUL)
                    t = dve.op(lambda e, i=i: e.tensor_reduce(lam[:, i:i + 1], sm, AX, ADD))
                t = actv(lam[:, 0:2], lam[:, 0:2], ACT.Exp, t)
                tt(dve, lam[:, 2:3], lam[:, 1:2], lam[:, 0:1], SUB, t)
                ts(dve, lam[:, 2:3], lam[:, 2:3], -0.2, None, ADD)
                project(W, 0, D, X, T, copy_to(lambda i: q[:, i, :]), xt=t_x)
                project(W, D, D, X, T, copy_to(lambda i: k[:, i, :]))
                values(W, 2 * D, X, QT, V)
                barrier()
                dve.wait(t_dist)
                items = [(h, i) for h in range(8) for i in range(3)]
                t_ex, t_comb, t_aT, t_trcp, t_pv, t_sq = {}, {}, {}, {}, {}, {}

                def first(n):
                    h, i = items[n]
                    q0, qn = QT[i]
                    b = (n % 2) * 2
                    slot = n % NP_
                    slope = 2.0 ** (-(h + 1))
                    for c in range(2):
                        t = mm(PS[0:qn, b + c, 0:T], q[64 * c:64 * c + 64, h, q0:q0 + qn], k[64 * c:64 * c + 64, h, :],
                               True, True, *take(b + c), inc=(c == 1))
                    s_, e_, x_ = S[slot][0:qn], Ex[slot][0:qn], st[slot][0:qn]
                    w = [t_comb[n - NP_]] if n >= NP_ else []
                    t = stt(s_, bc(dist[0:qn, i, :], [qn, 2, T], 1), -slope * 8.0, PS[0:qn, b:b + 2, 0:T], MUL, ADD, t,
                            *w, *([t_ex[n - NP_]] if n >= NP_ else []))
                    free[b], free[b + 1] = [t], [t]
                    dve.op(lambda e: e.tensor_reduce(x_[:, 0:2], s_, AX, MAX))
                    t = ts(dve, x_[:, 2:4], x_[:, 0:2], -0.125, None, MUL)
                    for c in range(2):
                        t_ex[n] = actv(e_[:, c, :], s_[:, c, :], ACT.Exp, t, bias=x_[:, 2 + c:3 + c], scale=0.125,
                                       accum=x_[:, 4 + c:5 + c], own=False)

                def second(n):
                    h, i = items[n]
                    q0, qn = QT[i]
                    slot = n % NP_
                    e_, x_, a_ = Ex[slot][0:qn], st[slot][0:qn], Ac[slot][0:qn]
                    dve.op(lambda e: e.reciprocal(x_[:, 6:8], x_[:, 4:6]), t_ex[n],
                           *([t_aT[n - NP_]] if n >= NP_ else []))
                    ts(dve, x_[:, 7:8], x_[:, 7:8], lam[0:qn, 2:3], None, MUL)
                    ts(dve, a_, e_[:, 1, :], x_[:, 7:8], None, MUL)
                    t_comb[n] = stt(a_, e_[:, 0, :], x_[:, 6:7], a_, MUL, ADD)

                def third(n):
                    h, i = items[n]
                    q0, qn = QT[i]
                    a_ = Ac[n % NP_][0:qn]
                    b = 4 + n % 2
                    w = take(b)
                    for kt, (k0, kn) in enumerate(QT):
                        t = tr(PS[0:kn, b, kt * 128:kt * 128 + qn], a_[:, k0:k0 + kn], ident[0:qn, 0:qn], t_comb[n], *w,
                               inc=(kt == 2))
                    t_aT[n] = t
                    dst = aT[h % 2]
                    wv = [t_pv[h - 2]] if h >= 2 else []
                    src = PS[:, b, 0:384].rearrange("p (a b) -> p a b", a=3)
                    actv(dst[0:96, 0:2, q0:q0 + qn], src[0:96, 0:2, 0:qn], ACT.Copy, t, *wv, own=False)
                    t_trcp[n] = actv(dst[0:80, 2, q0:q0 + qn], src[0:80, 2, 0:qn], ACT.Copy, own=False)
                    free[b] = [t_trcp[n]]

                def values_of(h):
                    b = 6 + h % 2
                    for kt, (k0, kn) in enumerate(QT):
                        t = mm(PS[:, b, 0:T], V[0:kn, kt, h * 128:(h + 1) * 128], aT[h % 2][0:kn, kt, :], kt == 0,
                               kt == 2, t_trcp[3 * h + 2], *take(b), inc=(kt == 2))
                    t_pv[h] = t

                def keep(h):
                    b = 6 + h % 2
                    free[b] = [cp(oT[:, h, :], PS[:, b, 0:T], t_pv[h])]
                    t_sq[h] = actv(osq[:, h, :], oT[:, h, :], ACT.Square, *free[b], own=False)

                for n in range(len(items) + 6):
                    if n < len(items):
                        first(n)
                    if n >= 6 and n % 3 == 0:
                        values_of(n // 3 - 2)
                    if 1 <= n <= len(items):
                        second(n - 1)
                    if n >= 7 and n % 3 == 1:
                        keep(n // 3 - 2)
                    if 3 <= n < len(items) + 3:
                        third(n - 3)
                b = bank()
                for h in range(8):
                    t = mm(PS[0:8, b, 0:T], one_of_8[:, 7 - h:15 - h], osq[:, h, :], h == 0, h == 7, t_sq[h], *take(b),
                           inc=(h == 7))
                t = ts(dve, n8, PS[0:8, b, 0:T], 1.0 / 128, 1e-5, MUL, ADD, t)
                free[b] = [t]
                t = actv(n8, n8, ACT.Sqrt, t)
                dve.op(lambda e: e.reciprocal(r8, n8), t)
                t_r = ts(dve, r8, r8, 0.8, None, MUL)
                xt = {}
                act.wait(pe.last())
                for h in range(8):
                    b = bank()
                    t = mm(PS[:, b, 0:T], ident[0:8, h:h + 1].to_broadcast([8, 128]), r8, True, True, t_r, *take(b),
                           inc=True)
                    t = stt(oT[:, h, :], oT[:, h, :], par("subln"), PS[:, b, 0:T], MUL, MUL, t, own=(h == 0))
                    free[b] = [t]
                    xt[h] = high_low(X[0][:, h, :], X[1][:, h, :], oT[:, h, :], t, own=False)

                def add(i, o, t):
                    return stt(H[:, i, :], H[:, i, :], ALPHA, o, MUL, ADD, t)
                project(A["attn_w_o"][0], 0, D, X, T, add, xt=xt)
                barrier()
                top[0] = m0
                layer_norm(H, 0, T, H, dve.last())

            def gated(Wg, Wu, Wd, nf, X, hT, tmp, evac, xt=None):
                used = [None] * len(tmp)
                xh, xl = X
                n = 0
                for f0 in range(0, nf, 2):
                    ps = []
                    for W in (Wg, Wu):
                        split_cols(W, f0 * 128, 256, [lambda v, j=j: v[:, :, j * 128:(j + 1) * 128] for j in range(2)])
                        for j in range(2):
                            wh, wl, tok, release = part()
                            b = bank()
                            for k in range(KC):
                                t = mm3(PS[:, b, 0:T], wh[:, k, :], wl[:, k, :], xh[:, k, :], xl[:, k, :], k == 0,
                                        k == KC - 1, tok, *take(b), *([xt[k]] if xt else []), inc=(k == KC - 1))
                            release(t)
                            ps.append((b, t))
                            if W is Wu:
                                (bg, t1), (bu, t2) = ps[j], ps[2 + j]
                                x = n % len(tmp)
                                t = actv(tmp[x], PS[:, bg, 0:T], ACT.Silu, t1, *([used[x]] if used[x] else []),
                                         own=False)
                                free[bg] = [t]
                                t = tt(dve, tmp[x], tmp[x], PS[:, bu, 0:T], MUL, t, t2, own=False)
                                free[bu] = [t]
                                used[x] = high_low(hT[0][:, f0 + j, :], hT[1][:, f0 + j, :], tmp[x], t, own=False)
                                n += 1
                contract(Wd, nf, hT, T, evac, dve.last())

            def ffn():
                m0 = top[0]
                hT = two_parts(*[ar3(FFN // 128, T) for _ in range(2)])
                tmp = [ar(T) for _ in range(4)]
                X = two_parts(*[ar3(KC, T) for _ in range(2)])
                section(ring_of(4))
                run_ahead(1)
                xt = {k: high_low(X[0][:, k, :], X[1][:, k, :], H[:, k, :], own=False) for k in range(KC)}

                def add(i, o, t):
                    return stt(H[:, i, :], H[:, i, :], ALPHA, o, MUL, ADD, t)
                gated(A["ffn_w_gate"][0], A["ffn_w_up"][0], A["ffn_w_down"][0], FFN // 128, X, hT, tmp, add, xt)
                barrier()
                top[0] = m0
                layer_norm(H, 1, T, H, dve.last())

            def rwkv():
                m0 = top[0]
                cst = ar(NC_RW)
                t_c = sp.start(cst, A["c_rw"], s_in[3], 16, *barrier())
                r, k, v, kk = [ar3(KC, TS) for _ in range(4)]
                a = [ar3(KC, TS) for _ in range(2)]
                c = [ar3(KC, TS) for _ in range(2)]
                for x in (r, k, v, kk, *a, *c):
                    dve.op(lambda e, x=x: e.memset(x[:, :, T:TS], 0.0), own=False)
                gh = ar(2 * T).rearrange("p (a b) -> p a b", a=2)
                m1 = top[0]
                E = ar3(KC, T + 1)
                xs = [ar3(KC, T) for _ in range(2)]
                lh = ar(T)
                LD, Q, tot = ar3(KC, TS), ar3(KC, T), ar3(KC, NCH)
                n16, r16 = ar(T)[0:16], ar(T)[0:16]
                section(ring_of(4))
                run_ahead(1)
                tt(dve, E[:, :, 1:T], H[:, :, 0:T - 1], H[:, :, 1:T], SUB)
                ts(dve, E[:, :, 0:1], H[:, :, 0:1], -1.0, None, MUL, own=False)
                cp(E[:, :, T:T + 1], H[:, :, T - 1:T], own=False)
                dve.wait(t_c, dve.last())
                used = [[], []]

                def mix(i, slot, parts=None):
                    X, toks = xs[slot], {}

                    def piece(kc):
                        stt(X[:, kc, :], E[:, kc, 1:T + 1], par("mu", 48 + i * 8 + kc), H[:, kc, :], MUL, SUB, *used[slot],
                            own=False)
                        toks[kc] = stt(X[:, kc, :], E[:, kc, 0:T], par("mu", i * 8 + kc), X[:, kc, :], MUL, SUB)
                        if parts:
                            toks[kc] = high_low(parts[0][:, kc, :], parts[1][:, kc, :], X[:, kc, :], toks[kc], *used[2],
                                                own=False)
                    return X, [lambda kc=kc: piece(kc) for kc in range(KC)], toks
                used.append([])

                def parts_of(*xs):
                    return two_parts(*[x[:, :, 0:T] for x in xs])

                def rkv(i, dst, parts, toks):
                    project(A["rw_w_rkv"][0, i], 0, D, parts, T, copy_to(lambda f: dst[:, f, 0:T]), xt=toks)

                def half(n):
                    return lambda slot: slot[:, 0:D].rearrange("p (k q r) -> p k q r", k=KC, q=2)[:, :, n, :]

                def lora(X, toks, n1, n2, func, fin):
                    s, slot, tok = load([(half(n), A[n1][0, n].rearrange("(k p) r -> p k r", p=128)) for n in range(2)]
                                        + [(lambda sl: sl[:, D:2 * D], A[n2][0].rearrange("n r d -> (n r) d"))])
                    w1v, w2v = slot[:, 0:D].rearrange("p (k q) -> p k q", k=KC), slot[:, D:2 * D]
                    b = bank()
                    for kc in range(KC):
                        t1 = mm(PS[:, b, 0:T], w1v[:, kc, :], X[:, kc, :], kc == 0,
                                kc == KC - 1, toks[kc], tok, *take(b), inc=(kc == KC - 1))
                    t2 = actv(lh, PS[:, b, 0:T], func, t1, pe.last())
                    free[b] = [t2]
                    for f in range(KC):
                        for n in range(2):
                            b = bank()
                            t3 = mm(PS[:, b, 0:T], w2v[64 * n:64 * n + 64, f * 128:(f + 1) * 128],
                                    lh[64 * n:64 * n + 64, :], True, True, t2, *take(b), inc=True)
                            free[b] = [fin(n, f, PS[:, b, 0:T], t3)]
                        if beside:
                            beside.pop(0)()
                    done(s, t3)
                    return t1, t3

                P0, P1 = (v, kk), (a[0], a[1])
                parts = parts_of(*P0)
                _, pieces, toks = mix(0, 0, parts)
                for p in pieces:
                    p()
                parts1 = parts_of(*P1)
                _, pieces, toks1 = mix(1, 1, parts1)
                beside.extend(pieces)
                pace[0] = 1
                rkv(0, r, parts, toks)
                rest()
                X3, pieces, toks3 = mix(3, 0)
                beside.extend(pieces)
                rkv(1, k, parts1, toks1)
                rest()
                t_k = [act.last(), dve.last()]
                used[2] = [pe.last()]
                _, pieces, toks2 = mix(2, 1, parts1)
                beside.extend(pieces)
                t1, t3 = lora(X3, toks3, "rw_w1", "rw_w2", ACT.Tanh, lambda n, f, o, t: actv(
                    c[n][:, f, 0:T], o, ACT.Sigmoid, t, bias=par("w0", n * 8 + f), own=False))
                t_w = act.last()
                used[0] = [t1]
                rest()
                c4 = [128, KC, NCH, CH]

                def by_chunk(x):
                    return x[:, :, 0:NCH * CH].rearrange("p f (c t) -> p f c t", t=CH)

                def decay(n, f0):
                    fs = slice(f0, f0 + 4)
                    ts(dve, LD[:, fs, :], c[n][:, fs, :], -float(np.exp(-0.5)), None, MUL, ALU.bypass, t_w)
                    for f in range(f0, f0 + 4):
                        dve.op(lambda e, f=f: e.tensor_tensor_scan(
                            c[n][:, f, :], cst[:, C_SCAN:C_SCAN + TS], LD[:, f, :], 0.0, MUL, ADD), own=(f == f0))
                    if n == 1:
                        x = by_chunk(c[n])[:, fs]
                        tt(dve, LD[:, fs, :], LD[:, fs, :], c[n][:, fs, :], SUB)
                        cp(tot[:, fs, :], x[:, :, :, CH - 1])
                        tt(dve, x, by_chunk(LD)[:, fs], bc(tot[:, fs, :], [128, 4, NCH, CH], 3), ADD)
                beside.extend([lambda n=n, f0=f0: decay(n, f0) for n in range(2) for f0 in (0, 4)])
                X4, pieces, toks4 = mix(4, 0)
                beside.extend(pieces)
                pace[0] = 2
                rkv(2, v, parts1, toks2)
                rest()
                kT, kkT = k[:, :, 0:T], kk[:, :, 0:T]
                t_q = {}

                def square(f0):
                    fs = slice(f0, f0 + 4)
                    t = tt(dve, kkT[:, fs], kT[:, fs], bc(par("k_k", f0, 4), [128, 4, T], 2), MUL, *t_k)
                    t_q[f0] = actv(Q[:, fs], kkT[:, fs], ACT.Square, t, own=False)
                X5, pieces, toks5 = mix(5, 1)
                beside.extend([lambda f0=f0: square(f0) for f0 in (0, 4)] + pieces)
                t1, t3 = lora(X4, toks4, "rw_a1", "rw_a2", ACT.Copy, lambda n, f, o, t: actv(
                    a[n][:, f, 0:T], o, ACT.Sigmoid, t, bias=par("a0", n * 8 + f), own=False))
                rest()
                b = bank()
                for f in range(KC):
                    t = mm(PS[0:16, b, 0:T], by_head[:, f, :], Q[:, f, :], f == 0, f == KC - 1, t_q[f // 4 * 4], *take(b),
                           inc=(f == KC - 1))
                t = ts(dve, n16, PS[0:16, b, 0:T], 1e-24, None, MAX, ALU.bypass, t)
                free[b] = [t]
                t = actv(n16, n16, ACT.Sqrt, t)
                t_r = dve.op(lambda e: e.reciprocal(r16, n16), t)
                sg, gv, tokg = cols(A["rw_g1"][0], 0, 160)
                for j, m in enumerate([128, 32]):
                    b = bank()
                    for kc in range(KC):
                        t1 = mm(PS[0:m, b, 0:T], gv[:, kc, j * 128:j * 128 + m], X5[:, kc, :], kc == 0, kc == KC - 1,
                                toks5[kc], tokg, *take(b), inc=(kc == KC - 1))
                    free[b] = [actv(gh[0:m, j, :], PS[0:m, b, 0:T], ACT.Sigmoid, t1)]
                done(sg, t1)

                def over_heads(f, row, t):
                    b = bank()
                    t = mm(PS[:, b, 0:T], cst[0:16, C_SPREAD + f * 128:C_SPREAD + (f + 1) * 128], row, True, True,
                           t, *take(b), inc=True)
                    return b, PS[:, b, 0:T], t
                for f in range(KC):
                    b, x, t = over_heads(f, r16, t_r)
                    free[b] = [tt(dve, kkT[:, f, :], kkT[:, f, :], x, MUL, t, own=(f == 0))]
                sh = [128, KC, T]
                bonus = flat(RING[:, 1:3, :])[:, 0:KC * T].rearrange("p (f t) -> p f t", f=KC)
                r_, k_, a0_, a1_ = [x[:, :, 0:T] for x in (r, k, *a)]
                pool.wait(act.last(), dve.last(), pe.last(), *ring_free[1], *ring_free[2])
                tt(pool, bonus, a0_, a1_, ADD)
                ts(pool, bonus, bonus, -2.0, None, ADD)
                tt(pool, bonus, bonus, bc(par("k_a", 0, 8), sh, 2), MUL)
                ts(pool, bonus, bonus, 2.0, None, ADD)
                tt(pool, bonus, bonus, k_, MUL)
                tt(pool, bonus, bonus, r_, MUL)
                t_bonus = tt(pool, bonus, bonus, bc(par("r_k", 0, 8), sh, 2), MUL)
                pool_n = pool.last()
                toks = [x.last() for x in (pe, dve, act)]
                for x in (pe, dve, act):
                    x.wait(*toks)
                top[0] = m1
                y = ar3(KC, TS)
                spare = flat(RING[:, :, :])

                def of_ring(o):
                    return spare[:, o:o + 512].rearrange("p (a b) -> p a b", a=KC)
                for x in (dve, act):
                    x.wait(*[t for s_ in range(3) for t in ring_free[s_]])
                St = [of_ring(2048 + KC * T + 512 * n) for n in range(2)]
                NB = 2
                B = []
                for n in range(NB):
                    w = dict(X=ar3(KC, 128), XT=ar3(KC, 128), W=ar3(KC, 128), L=ar3(KC, 128), akp=ar3(KC, 128),
                             abq=ar3(KC, 64), ar=ar3(KC, 128), R=ar3(KC, 64), U=ar3(KC, 64), e1=ar3(KC, CH + 1),
                             t1=ar(KC * 64), kt=of_ring(1024 * n), bt=of_ring(1024 * n + 512), vt=ar3(KC, 64), em=ar(8))
                    w.update(e2=flat(w["X"])[:, 0:KC * CH].rearrange("p (f t) -> p f t", f=KC))
                    w.update(ka=w["XT"], be=w["W"])
                    w.update(sm=w["t1"].rearrange("p (f v) -> p f v", f=KC))
                    B.append(w)
                    for nm in ("L", "XT", "W"):
                        dve.op(lambda e, x=w[nm]: e.memset(flat(x), 0.0), own=False)
                    for x in (w["ar"][:, :, 0:64], w["ar"][:, :, 64:128]):
                        dve.op(lambda e, x=x: e.memset(x[:, :, CH:64], 0.0), own=False)
                for n in range(2):
                    dve.op(lambda e, n=n: e.memset(flat(St[n]), 0.0), own=False)
                act.wait(dve.last())
                pe.wait(dve.last())
                ib = bc(ident, [128, KC, 128], 1)

                def lvl(d, l, tr_):
                    o = C_LVL + ((d ^ tr_) * len(SCAN_LEVELS) + l) * 64
                    return bc(cst[:, o:o + 64], [128, 16, 64], 1)

                def blocks(x):
                    return flat(x).rearrange("p (f t) -> p f t", t=64)

                def pairs(b, lhsT, rhs, *waits):
                    pe.wait(*waits)
                    for f in range(KC):
                        t = mm(PS[:, b + f // 4, f % 4 * 128:(f % 4 + 1) * 128], lhsT[:, f, :], rhs(f), True, True,
                               inc=(f == KC - 1))
                    return t, PS[:, b:b + 2, :].rearrange("p b (f t) -> p (b f) t", t=128)

                groups = []
                for i in range(NCH):
                    groups += [(0, i), (1, NCH - 1 - i)]
                last_seq, last_prep, t_x, t_xt = {}, {}, {}, {}

                def each(o, lhsT, rhs, *waits, add=None):
                    pe.wait(*waits)
                    for h in range(16):
                        p, f = slice(64 * (h % 2), 64 * (h % 2) + 64), h // 2
                        terms = [(lhsT, rhs)] + (add or [])
                        for n, (a_, b_) in enumerate(terms):
                            t = mm(o(p, f), a_(p, f), b_(p, f), n == 0, n == len(terms) - 1,
                                   inc=(h == 15 and n == len(terms) - 1))
                    return t

                def head(x, o=0, n=64):
                    return lambda p, f: x[p, f, o:o + n]

                def diag(x):
                    return lambda p, f: x[p, f, p]

                def bankof(b, n=64):
                    return lambda p, f: PS[p, b, f * n:(f + 1) * n]

                def whole(b):
                    return PS[:, b, :].rearrange("p (f t) -> p f t", f=KC)

                def on_diagonal(x, a_, b_, *waits):
                    for p in (0, 64):
                        dve.op(lambda e, p=p: e.memset(x[p:p + 64, :, p + CH:p + 64], 0.0), own=False)
                        t = tt(dve, x[p:p + 64, :, p:p + CH], a_[p:p + 64], b_[p:p + 64], MUL, *waits, own=(p == 0))
                    return t

                def prep(g):
                    d, ci = groups[g]
                    W = B[g % NB]
                    z = 4 * (g % 2)
                    t0 = ci * CH
                    sl = (slice(None), slice(None), slice(t0, t0 + CH))
                    cc, rr, kv, kkv, av = c[d][sl], r[sl], k[sl], kk[sl], a[d][sl]
                    sh = [128, KC, CH]
                    e1, e2, t1 = W["e1"], W["e2"], W["t1"][:, 0:KC * CH].rearrange("p (f t) -> p f t", f=KC)
                    inn, prv = (slice(1, CH + 1), slice(0, CH)) if d == 0 else (slice(0, CH), slice(1, CH + 1))
                    edge = 0 if d == 0 else CH
                    mid = cc[:, :, MID:MID + 1]
                    pre = last_seq.get(g - NB, [])
                    pe.wait(*pre)
                    t = tt(dve, e1[:, :, inn], cc, mid.to_broadcast(sh), SUB, *pre)
                    t = ts(dve, e1[:, :, edge:edge + 1], mid, -1.0, None, MUL, own=False)
                    actv(e2, e1[:, :, inn], ACT.Exp, t, *pre, scale=-1.0, own=False)
                    actv(W["em"], mid.rearrange("p a b -> p (a b)"), ACT.Exp, own=False)
                    te = actv(e1, e1, ACT.Exp)
                    stt(t1, av, -1.0, bc(par("k_a", 0, 8), sh, 2), ADD, MUL)
                    stt(t1, t1, 1.0, kv, ADD, MUL)
                    tka = on_diagonal(W["ka"], t1, e2, te)
                    tt(dve, t1, kkv, av, MUL)
                    tbe = on_diagonal(W["be"], t1, e2)
                    tt(dve, W["ar"][:, :, 0:CH], kkv, e1[:, :, prv], MUL, own=False)
                    tf = tt(dve, W["ar"][:, :, 64:64 + CH], rr, e1[:, :, inn], MUL, own=False)
                    yield
                    idh = lambda p, f: ident[p, p]
                    for x, (src, dst, sc, tw) in enumerate([
                            (lambda p, f: v[p, f, t0:t0 + 64], W["vt"], 1.0, tka), (diag(W["ka"]), W["kt"], 1.0, tka),
                            (diag(W["be"]), W["bt"], -1.0, tbe)]):
                        b = z + x
                        t = each(bankof(b), src, idh, tw, *take(b))
                        free[b] = [actv(flat(dst), PS[:, b, :], ACT.Copy, t, *pre, scale=sc, own=False)]
                    for x, (src, dst) in enumerate([("ka", "akp"), ("be", "abp")]):
                        for fh in range(2):
                            b = z + (3, 0, 1, 2)[2 * x + fh]
                            pe.wait(tf, *take(b))
                            for f in range(4):
                                t = mm(PS[:, b, f * 128:(f + 1) * 128], W[src][:, 4 * fh + f, :], W["ar"][:, 4 * fh + f, :],
                                       True, True, inc=(f == 3))
                            o = C_AM + (2 * d + x) * 128
                            ps, fs = PS[:, b, :].rearrange("p (f x) -> p f x", f=4), slice(4 * fh, 4 * fh + 4)
                            if x == 0:
                                t = tt(dve, W[dst][:, fs, :], ps, bc(cst[:, o:o + 128], [128, 4, 128], 1), MUL, t,
                                       own=False)
                            else:
                                for p in (slice(0, 64), slice(64, 128)):
                                    tt(dve, W["L"][p, fs, p], ps[p, :, 0:64], bc(cst[p, o:o + 64], [64, 4, 64], 1), MUL, t,
                                       *pre, own=False)
                                t = tt(dve, W["abq"][:, fs, :], ps[:, :, 64:128],
                                       bc(cst[:, o + 64:o + 128], [128, 4, 64], 1), MUL, own=False)
                            free[b] = [t]
                    last_prep[g] = [pe.last()]
                    yield t

                def level(g, l, part, tw):
                    d, ci = groups[g]
                    W = B[g % NB]
                    z = 4 * (g % 2)
                    X, XT, Wm = W["X"], W["XT"], W["W"]
                    if part == 0:
                        t, ps = pairs(z, W["L"], (lambda f: X[:, f, :]) if l else (lambda f: ident), t_x[g], *take(z),
                                      *take(z + 1))
                        if l == 0:
                            tt(pool, blocks(XT), blocks(W["L"]), lvl(d, l, 1), MUL, t_x[g], *last_prep[g])
                            t_xt[g] = tt(pool, XT, ib, XT, SUB)
                        t2 = tt(dve, blocks(Wm), ps.rearrange("p f (c t) -> p (f c) t", t=64), lvl(d, l, 0), MUL, t,
                                own=False)
                        free[z], free[z + 1] = [t2], [t2]
                        if l == 0:
                            t_x[g] = t2 = tt(dve, X, ib, Wm, SUB)
                        return t2
                    if l == 0:
                        return tw
                    last = l == len(SCAN_LEVELS) - 1
                    if not last:
                        tx, px = pairs(z + 2, XT, lambda f: Wm[:, f, :], tw, t_xt[g], *take(z + 2), *take(z + 3))
                    t, pt = pairs(z, Wm, lambda f: XT[:, f, :], tw, *take(z), *take(z + 1))
                    if not last:
                        t_x[g] = tt(dve, X, X, px, SUB, tx, own=False)
                        free[z + 2], free[z + 3] = [t_x[g]], [t_x[g]]
                    t3 = tt(dve, XT, XT, pt, SUB, t, own=False)
                    free[z], free[z + 1] = [t3], [t3]
                    return t3

                def seq1(g, tw):
                    d, ci = groups[g]
                    W = B[g % NB]
                    z = 4 * (g % 2)
                    tsm = tt(dve, W["sm"], St[d], bc(W["em"], [128, KC, 64], 2), MUL, act.last(), pe.last())
                    t = each(bankof(z), head(W["ar"]), head(W["sm"]), tsm, tw, *take(z),
                             add=[(head(W["akp"]), head(W["vt"]))])
                    t = actv(flat(W["R"]), PS[:, z, :], ACT.Copy, t, own=False)
                    free[z] = [t]
                    return t

                def seq2(g, t):
                    W = B[g % NB]
                    z = 4 * (g % 2)
                    t = each(bankof(z + 2), diag(W["XT"]), head(W["R"]), t, *take(z + 2))
                    t = actv(flat(W["U"]), PS[:, z + 2, :], ACT.Copy, t, own=False)
                    free[z + 2] = [t]
                    return t

                def seq3(g, t):
                    d, ci = groups[g]
                    W = B[g % NB]
                    z = 4 * (g % 2)
                    t0 = ci * CH
                    S, sm = St[d], W["sm"]
                    ts_ = each(bankof(z + 3), head(W["kt"]), head(W["vt"]), t, *take(z + 3),
                               add=[(head(W["bt"]), head(W["U"]))])
                    ty = each(lambda p, f: PS[p, z, f * 64:f * 64 + CH], head(sm), head(W["ar"], 64, CH), *take(z),
                              add=[(head(W["vt"]), head(W["akp"], 64, CH)), (head(W["U"]), head(W["abq"], 0, CH))])
                    end = W["e1"][:, :, CH if d == 0 else 0]
                    t1 = tt(dve, S, sm, whole(z + 3), ADD, ts_)
                    free[z + 3] = [t1]
                    tt(dve, S, S, bc(end, [128, KC, 64], 2), MUL)
                    yv = y[:, :, t0:t0 + CH]
                    src = whole(z)[:, :, 0:CH]
                    if g // 2 < NCH // 2 or (g // 2 == NCH // 2 and d == 0):
                        t2 = cp(yv, src, ty, own=False)
                    else:
                        t2 = tt(dve, yv, yv, src, ADD, ty)
                    free[z] = [t2]
                    last_seq[g] = [t2, ty, t]

                preps = {}

                def prepare(g):
                    if g < len(groups):
                        preps[g] = prep(g)
                        next(preps[g])
                for g in range(NB):
                    prepare(g)
                for g0 in range(0, len(groups), NB):
                    gs = list(range(g0, g0 + NB))
                    tw = {g: next(preps[g]) for g in gs}
                    t_x.update(tw)
                    for l in range(len(SCAN_LEVELS)):
                        for part in range(2):
                            for g in gs:
                                tw[g] = level(g, l, part, tw[g])
                    for step in (seq1, seq2):
                        for g in gs:
                            tw[g] = step(g, tw[g])
                    for g in gs:
                        seq3(g, tw[g])
                        prepare(g + NB)
                barrier()
                top[0] = m1 + -(-KC * TS // 8) * 8
                Q, V2 = ar3(KC, T), ar3(KC, T)
                m16, s16 = ar(T)[0:16], ar(T)[0:16]
                Yh, Yl = two_parts(ar3(KC, T), ar3(KC, T))
                y, v = [x[:, :, 0:T] for x in (y, v)]

                def heads(X, t):
                    for f in range(KC):
                        t2 = mm(PS[:, f, 0:T], blk, X[:, f, :], True, True, t, *take(f), inc=(f == KC - 1))
                    return t2

                def freed(t):
                    for f in range(8):
                        free[f] = [t]
                    return t
                t = heads(y, dve.last())
                t = freed(stt(y, PS[:, :, 0:T], -1.0 / 64, y, MUL, ADD, t))
                tq = actv(Q, y, ACT.Square, t)
                t = heads(bonus, t_bonus)
                t_v = freed(tt(dve, V2, v, PS[:, :, 0:T], MUL, t))
                for s_ in range(3):
                    ring_free[s_] = [t_v, pe.last(), act.last()]
                section(ring_of(4))
                b = bank()
                for f in range(KC):
                    t = mm(PS[0:16, b, 0:T], by_head[:, f, :], Q[:, f, :], f == 0, f == KC - 1, tq, *take(b),
                           inc=(f == KC - 1))
                t = ts(dve, m16, PS[0:16, b, 0:T], 1.0 / 64, 64e-5, MUL, ADD, t)
                free[b] = [t]
                t = actv(m16, m16, ACT.Sqrt, t)
                t_r = dve.op(lambda e: e.reciprocal(s16, m16), t)
                s, slot, tok = load([(lambda sl: sl[:, 0:D], A["rw_g2"][0, 0:128, :]),
                                     (lambda sl: sl[0:32, D:2 * D], A["rw_g2"][0, 128:160, :])])
                run_ahead(1)
                xt = {}
                for f in range(KC):
                    b, x, t = over_heads(f, s16, t_r)
                    t = free[b] = stt(y[:, f, :], y[:, f, :], par("lnx_g", f), x, MUL, MUL, t, own=(f == 0))
                    free[b] = [t]
                    stt(y[:, f, :], y[:, f, :], par("lnx_b", f), V2[:, f, :], ADD, ADD)
                    b = bank()
                    w = take(b)
                    mm(PS[:, b, 0:T], slot[:, f * 128:(f + 1) * 128], gh[:, 0, :], True, False, tok, *w)
                    t = mm(PS[:, b, 0:T], slot[0:32, D + f * 128:D + (f + 1) * 128], gh[0:32, 1, :], False, True,
                           inc=True)
                    t = tt(dve, y[:, f, :], y[:, f, :], PS[:, b, 0:T], MUL, t)
                    free[b] = [t]
                    xt[f] = high_low(Yh[:, f, :], Yl[:, f, :], y[:, f, :], t, own=False)
                done(s, pe.last())

                def add(i, o, t):
                    return stt(H[:, i, :], H[:, i, :], ALPHA, o, MUL, ADD, t)
                project(A["rw_w_o"][0], 0, D, (Yh, Yl), T, add, xt=xt)
                barrier()
                top[0] = m0
                layer_norm(H, 2, T, H, dve.last())

            def moe():
                m0 = top[0]
                section()
                bars = barrier()
                for i in range(NMORE):
                    slots.append(ar(2048))
                    ring_free[NRING + i] = list(bars)
                acc, GB = ar3(KC, T), ar3(KC, T)
                ht_copies = []
                cst = ar(224)
                gt, rt = ar(T), ar(T)
                sc = [ar(64) for _ in range(3)]
                mk = [x[:, 40:48] for x in sc]
                rk = [ar(8) for _ in range(3)]
                cn = ar(9)
                t_c = sp.start(cst, A["c_moe"], s_in[5], 16, *bars)
                tri, iota_r, iota_p = cst[:, 0:96], cst[:, 96:96 + CAP], cst[:, 192:193]
                ws, wr, tok = cols(A["moe_w_router"][0], 0, NE)
                m_ht = top[0]
                Ht = two_parts(ar3(3, D), ar3(3, D))
                for x in (pe, act, dve):
                    x.wait(*bars)

                def logits(i):
                    q0, qn = QT[i]
                    for kc in range(KC):
                        t = mm(PS[0:qn, b, i * NE:(i + 1) * NE], H[:, kc, q0:q0 + qn], wr[:, kc, :], kc == 0, kc == KC - 1, tok, *take(b),
                               inc=(kc == KC - 1))
                    return t
                b = b_logit = bank()
                logit = [logits(i) for i in range(3)]
                for i, (q0, qn) in enumerate(QT):
                    for hf in range(2):
                        b = bank()
                        for f in range(4):
                            t = tr(PS[0:qn, b, f * 128:(f + 1) * 128], H[:, 4 * hf + f, q0:q0 + qn], ident, *take(b),
                                   inc=(f == 3))
                        free[b] = [t]
                        c = slice(hf * 512, (hf + 1) * 512)
                        ht_copies.append((Ht[0][0:qn, i, c], Ht[1][0:qn, i, c], PS[0:qn, b, :], t, b))

                def route(i):
                    q0, qn = QT[i]
                    x = sc[i][0:qn]
                    b, t = b_logit, logit[2]
                    t = tt(dve, x[:, 0:8], PS[0:qn, b, i * NE:(i + 1) * NE], par("b_router", 0, 8, qn), ADD, t, own=False)
                    free[b] = [t]
                    yield
                    t = dve.op(lambda e: e.max(x[:, 8:16], x[:, 0:8]), t, own=False)
                    yield
                    t = ts(dve, x[:, 16:17], x[:, 8:9], -1.0, None, MUL, ALU.bypass, t, own=False)
                    t = actv(x[:, 24:32], x[:, 0:8], ACT.Exp, t, bias=x[:, 16:17], accum=x[:, 17:18], own=False)
                    yield
                    t = dve.op(lambda e: e.reciprocal(x[:, 18:19], x[:, 17:18]), t, own=False)
                    yield
                    t = ts(dve, x[:, 24:32], x[:, 24:32], x[:, 18:19], None, MUL, ALU.bypass, t, own=False)
                    yield
                    t = dve.op(lambda e: e.max(x[:, 32:40], x[:, 24:32]), t, own=False)
                    yield
                    t1 = cp(x[:, 40:42], x[:, 32:34], t, own=False)
                    t1 = dve.op(lambda e: e.memset(x[:, 42:48], -2.0), own=False)
                    t = tt(dve, x[:, 19:20], x[:, 32:33], x[:, 33:34], ADD, t, own=False)
                    yield
                    t = dve.op(lambda e: e.match_replace(x[:, 48:56], x[:, 40:48], x[:, 24:32], -1.0), t1, own=False)
                    yield
                    t = ts(dve, x[:, 40:48], x[:, 48:56], -1.0, None, ALU.is_equal, ALU.bypass, t, own=False)
                    t_mk.append(t)
                    t1 = dve.op(lambda e: e.reciprocal(x[:, 20:21], x[:, 19:20]), t, own=False)
                    yield
                    t = ts(dve, x[:, 48:56], x[:, 40:48], x[:, 20:21], None, MUL, ALU.bypass, t1, own=False)
                    yield
                    t = tt(dve, x[:, 56:64], x[:, 48:56], x[:, 24:32], MUL, t, own=False)
                    t_gate.append(t)
                t_mk, t_gate = [], []
                routes = [route(i) for i in range(3)]
                while routes:
                    for x in list(routes):
                        if next(x, 0) == 0:
                            routes.remove(x)
                done(ws, pe.last())
                b = bank()
                for i, (q0, qn) in enumerate(QT):
                    t = mm(PS[:, b, 0:8], ones[0:qn, :], mk[i][0:qn], i == 0, i == 2, t_c, t_mk[i], *take(b),
                           inc=(i == 2))
                cp(cn[:, 0:8], PS[:, b, 0:8], t)
                dve.op(lambda e: e.tensor_reduce(cn[:, 8:9], cn[:, 0:8], AX, MAX))
                t_rk = {}
                t_flag = ts(dve, flag, cn[:, 8:9], CAP + 0.5, None, ALU.is_gt)
                free[b] = [t_flag]
                for hi, lo, src, t, b in ht_copies:
                    t_ht = high_low(hi, lo, src, t, own=False)
                    free[b] = [t_ht]
                for i, (q0, qn) in enumerate(QT):
                    b = bank()
                    for j in range(i + 1):
                        jn = QT[j][1]
                        t = mm(PS[0:qn, b, 0:8], tri[0:jn, 0:qn] if j == i else ones[0:jn, 0:qn], mk[j][0:jn], j == 0,
                               j == i, *take(b), inc=(j == i))
                    t_rk[i] = cp(rk[i][0:qn], PS[0:qn, b, 0:8], t, own=False)
                    free[b] = [t_rk[i]]
                for i, (q0, qn) in enumerate(QT):
                    for src, dst, t in ((rk[i], rt, t_rk[i]), (sc[i][:, 56:64], gt, t_gate[i])):
                        b = bank()
                        t = tr(PS[0:NE, b, 0:qn], src[0:qn], ident[0:qn, 0:qn], t, *take(b), inc=True)
                        free[b] = [cp(dst[0:NE, q0:q0 + qn], PS[0:NE, b, 0:qn], t, own=False)]
                t_rows = dve.last()

                def gate_rows(e_):
                    b = bank()
                    t = mm(PS[:, b, 0:T], ident[0:NE, e_:e_ + 1].to_broadcast([NE, 128]), gt[0:NE, :], True, True,
                           t_rows, *take(b), inc=True)
                    t = cp(GB[:, e_, :], PS[:, b, 0:T], t, own=False)
                    free[b] = [t]
                    return t

                def dense():
                    top[0] = m_ht
                    X = two_parts(*[ar3(KC, T) for _ in range(2)])
                    hT = two_parts(*[ar3(FE // 128, T) for _ in range(2)])
                    tmp = [ar(T) for _ in range(2)]
                    section(ring_of(2))
                    pe.wait(high_low(*X, H))
                    for e_ in range(NE):
                        dve.wait(gate_rows(e_))
                    for e_ in range(NE):
                        def add(i, o, t, e_=e_):
                            if e_ == 0:
                                return tt(dve, acc[:, i, :], GB[:, e_, :], o, MUL, t)
                            x = tmp[0]
                            t = tt(dve, x, GB[:, e_, :], o, MUL, t)
                            tt(dve, acc[:, i, :], acc[:, i, :], x, ADD)
                            return t
                        if e_:
                            pe.wait(dve.last())
                            act.wait(pe.last(), dve.last())
                        gated(A["moe_w_gate"][0, e_], A["moe_w_up"][0, e_], A["moe_w_down"][0, e_], FE // 128, X, hT,
                              tmp, add)

                def sparse():
                    xe = [two_parts(ar3(KC, CAP), ar3(KC, CAP)) for _ in range(2)]
                    P1 = two_parts(ar3(3, CAP), ar3(3, CAP))
                    G = ar(D)
                    PG = [ar(T) for _ in range(2)]
                    hid = [ar(512) for _ in range(2)]
                    hT = two_parts(ar3(FE // 128, CAP), ar3(FE // 128, CAP))
                    Y = ar(D)
                    section(ring_of(4))
                    g_free = [[], []]
                    t_x, t_pg, t_sc, t_gu, t_dn = {}, {}, {}, {}, {}

                    def gather(e_):
                        w = [t_sc[e_ - 2], t_gu[e_ - 2]] if e_ >= 2 else []
                        xh, xl = xe[e_ % 2]
                        for i, (q0, qn) in enumerate(QT):
                            t = ts(dve, rounded(P1[e_ % 2][0:qn, i, :]), iota_r[0:qn], rk[i][0:qn, e_:e_ + 1],
                                   mk[i][0:qn, e_:e_ + 1], ALU.is_equal, MUL, *w, own=(i == 0))
                        for hf in range(2):
                            b = bank()
                            c = slice(hf * 512, (hf + 1) * 512)
                            for i, (q0, qn) in enumerate(QT):
                                for x in Ht:
                                    t2 = mm(PS[0:CAP, b, :], rounded(P1[e_ % 2][0:qn, i, :]), rounded(x[0:qn, i, c]),
                                            i == 0 and x is Ht[0], i == 2 and x is Ht[1], t, t_ht, *take(b),
                                            inc=(i == 2 and x is Ht[1]))
                            t2 = actv(G[0:CAP, c], PS[0:CAP, b, :], ACT.Copy, t2, *g_free[hf], own=False)
                            free[b] = [t2]
                            b = bank()
                            for f in range(4):
                                t2 = tr(PS[:, b, f * CAP:(f + 1) * CAP], G[0:CAP, (4 * hf + f) * 128:(4 * hf + f + 1) * 128],
                                        ident[0:CAP, 0:CAP], t2, *take(b), inc=(f == 3))
                            g_free[hf] = [t2]
                            o = slice(4 * hf, 4 * hf + 4)
                            t_x[e_] = high_low(flat(xh[:, o, :]), flat(xl[:, o, :]), PS[:, b, 0:4 * CAP], t2, *w,
                                               own=False)
                            free[b] = [t_x[e_]]
                        t1 = gate_rows(e_)
                        b = bank()
                        t = mm(PS[:, b, 0:T], ident[0:NE, e_:e_ + 1].to_broadcast([NE, 128]), rt[0:NE, :], True, True,
                               *take(b), inc=True)
                        t_pg[e_] = stt(PG[e_ % 2], PS[:, b, 0:T], iota_p, GB[:, e_, :], ALU.is_equal, MUL, t, t1, *w)
                        free[b] = [t_pg[e_]]

                    def scatter(e_, t_y):
                        for f in range(KC):
                            b = bank()
                            t = mm(PS[:, b, 0:T], Y[0:CAP, f * 128:(f + 1) * 128], PG[e_ % 2][0:CAP, :], True, True,
                                   t_y, t_pg[e_], *take(b), inc=True)
                            if e_ == 0:
                                free[b] = [cp(acc[:, f, :], PS[:, b, 0:T], t, own=False)]
                            else:
                                free[b] = [tt(dve, acc[:, f, :], acc[:, f, :], PS[:, b, 0:T], ADD, t, own=(f == 0))]
                        t_sc[e_] = t

                    hid_free = [[], []]
                    t_hT = {}

                    def turned(e_, g, t_h):
                        b = bank()
                        for f in range(4):
                            t = tr(PS[:, b, f * CAP:(f + 1) * CAP], hid[g % 2][0:CAP, f * 128:(f + 1) * 128],
                                   ident[0:CAP, 0:CAP], t_h, *take(b), inc=(f == 3))
                        hid_free[g % 2] = [t]
                        o = slice(4 * g, 4 * g + 4)
                        w = [t_dn[e_ - 1]] if e_ else []
                        t_hT[g] = high_low(flat(hT[0][:, o, :]), flat(hT[1][:, o, :]), PS[:, b, 0:4 * CAP], t, *w,
                                           own=False)
                        free[b] = [t_hT[g]]

                    gather(0)
                    t_y = None
                    NG = FE // 512
                    for e_ in range(NE):
                        Wg, Wu, Wd = A["moe_w_gate"][0, e_], A["moe_w_up"][0, e_], A["moe_w_down"][0, e_]
                        xh, xl = xe[e_ % 2]
                        late = None
                        for g in range(NG):
                            ps = []
                            for W in (Wg, Wu):
                                b = bank()
                                for k0 in (0, 4):
                                    split_rows(W, k0, 4, g * 512)
                                    for k1 in (k0, k0 + 2):
                                        wh, wl, tok, release = part()
                                        for k in range(2):
                                            t = mm3(PS[0:CAP, b, :], xh[:, k1 + k, :], xl[:, k1 + k, :], wh[:, k, :],
                                                    wl[:, k, :], k1 + k == 0, k1 + k == KC - 1, tok, t_x[e_], *take(b),
                                                    inc=(k == 1))
                                        release(t)
                                ps.append((b, t))
                                if W is Wg:
                                    if late:
                                        turned(*late)
                                    h = hid[g % 2][0:CAP]
                                    t1 = actv(h, PS[0:CAP, b, :], ACT.Silu, t, *hid_free[g % 2], own=False)
                                    free[b] = [t1]
                            t_gu[e_] = t
                            t = tt(dve, h, h, PS[0:CAP, ps[1][0], :], MUL, t1, t, own=False)
                            free[ps[1][0]] = [t]
                            late = (e_, g, t)
                            if g == 0 and e_:
                                scatter(e_ - 1, t_y)
                        for hf in range(2):
                            b = bank()
                            for f0 in range(0, FE // 128, 4):
                                split_rows(Wd, f0, 4, hf * 512)
                                for f1 in (f0, f0 + 2):
                                    wh, wl, tok, release = part()
                                    for f in (f1, f1 + 1):
                                        t = mm3(PS[0:CAP, b, :], hT[0][:, f, :], hT[1][:, f, :], wh[:, f - f1, :],
                                                wl[:, f - f1, :], f == 0, f == FE // 128 - 1, tok, t_hT[f // 4],
                                                *take(b), inc=(f == f1 + 1))
                                    release(t)
                                if late:
                                    turned(*late)
                                    late = None
                            if hf == 1:
                                t_dn[e_] = t
                            t_y = actv(Y[0:CAP, hf * 512:(hf + 1) * 512], PS[0:CAP, b, :], ACT.Copy, t,
                                       *([t_sc[e_ - 1]] if e_ else []), own=False)
                            free[b] = [t_y]
                            if hf == 0 and e_ + 1 < NE:
                                gather(e_ + 1)
                    scatter(NE - 1, t_y)

                for x in (pe, dve, act):
                    x.wait(t_flag, dve.last(), act.last())
                sp.items.append(t_flag)
                branch(flag[0:1, 0:1], dense, sparse)
                barrier()
                del slots[NRING:]
                nload[0] = 0
                section()
                dve.wait(pe.last())
                stt(flat(H[:, :, :]), flat(H[:, :, :]), ALPHA, flat(acc), MUL, ADD)
                barrier()
                top[0] = m0
                layer_norm(H, 3, T, H, dve.last())

            B2 = {}

            def tables():
                cst = ar(NC_B2)
                B2["cs"] = [(ar(SEQ), ar(SEQ)) for _ in range(2)]
                m0 = top[0]
                pos = ar(SEQ)
                bars = barrier()
                t_c = sp.start(cst, A["c_b2"], s_in[4], 32, *bars)
                t_c = sp.start(pos.bitcast(I32), A["pos"], s_in[4], 32)
                B2.update(rot=[cst[:, 0:128], cst[:, 128:256]], causal=cst[:, 256:768].rearrange("p (a b) -> p a b", a=2))
                pf, y, kf = ar(SEQ), ar(SEQ), ar(SEQ)
                cp(pf, pos.bitcast(I32), t_c)
                c1 = 6.28125
                c2 = float(np.float32(round((TWO_PI - c1) * 2 ** 20) / 2 ** 20))
                c3 = float(TWO_PI - c1 - c2)
                for i in range(2):
                    co, si = B2["cs"][i]
                    ts(dve, y, pf, cst[:, 768 + i:769 + i], None, MUL)
                    ts(dve, kf, y, float(1.0 / TWO_PI), None, MUL)
                    ts(dve, kf, kf, 12582912.0, None, ADD)
                    ts(dve, kf, kf, -12582912.0, None, ADD)
                    for cc in (c1, c2, c3):
                        stt(y, kf, -cc, y, MUL, ADD)
                    ts(dve, y, y, 3.1415925, -3.1415925, ALU.min, MAX)
                    t = ts(dve, co, y, -1.0, None, MUL)
                    tt(dve, co, co, y, MAX)
                    t = ts(dve, co, co, -1.0, float(np.pi / 2), MUL, ADD)
                    actv(si, y, ACT.Sin, t)
                    t = actv(co, co, ACT.Sin)
                    dve.wait(t)
                barrier()
                top[0] = m0

            X2 = H[:, :, NMETA:T]

            def rms(O, gain, gi, each=None):
                m0 = top[0]
                Q, R, R2 = ar3(KC, SEQ), ar(SEQ), ar(SEQ)
                tq = actv(Q, X2, ACT.Square)
                b, s, t = sum_rows(Q, KC, SEQ, ones, tq)
                t1, t2 = rsqrt(R, s, 1.0 / D, 1e-6, R2, t)
                free[b] = [t1]
                for k in range(KC):
                    t = stt(O[:, k, :], X2[:, k, :], par(gain, gi + k), R, MUL, MUL, own=(k == 0))
                    if each:
                        t = each(k, t)
                top[0] = m0
                return t

            def second(l):
                m0 = top[0]
                W = A["w_in_2"][l]
                o_q, o_k, o_v, o_ga, o_iq, o_ik, o_xr, o_gr, o_ma, o_mb = (
                    0, 1024, 2048, 3072, 4096, 5120, 5200, 6608, 8016, 9040)
                hh, hl, M, q, k, iq, t1 = [ar3(KC, SEQ) for _ in range(7)]
                ik, iw = ar3(1, SEQ), ar(32).rearrange("p (a b) -> p a b", a=2)
                score, bias = [ar3(2, SEQ) for _ in range(2)]
                m8 = ar(16)
                GA, V = iq, flat(t1).rearrange("p (a b) -> p a b", a=2)
                rel = [ar(SEQ) for _ in range(2)]
                spv = ar(NRB * 6).rearrange("p (a b) -> p a b", a=6)[0:RB]
                section(ring_of(3))
                run_ahead(1)
                m1 = top[0]
                hn = ar3(KC, SEQ)
                barrier()
                two_parts(hh, hl)
                t_hn = {}

                def split_hn(k, t):
                    t_hn[k] = high_low(hh[:, k, :], hl[:, k, :], hn[:, k, :], t, own=False)
                rms(hn, "norm_g", l * 8, split_hn)
                for x in (act, dve):
                    x.wait(act.last(), dve.last())
                top[0] = m1
                X = two_parts(hh, hl)
                XR = ar3(NRB, SEQ + 3)
                CX, RR, II = [ar3(NRB, SEQ) for _ in range(3)]
                top[0] = m1
                AA = flat(XR)[:, 0:NRB * SEQ].rearrange("p (a b) -> p a b", a=NRB)
                GR = RR
                HC = flat(II)[:, 0:11 * SEQ].rearrange("p (a b) -> p a b", a=11)
                HH = flat(CX)[:, 0:11 * SEQ].rearrange("p (a b) -> p a b", a=11)
                XR_, GR_, CX_, RR_, II_, AA_ = [x[0:RB] for x in (XR, GR, CX, RR, II, AA)]

                def on_act(dst, func=ACT.Copy):
                    return lambda i, o, t: actv(dst(i), o, func, t, own=False)

                dve.op(lambda e: e.memset(XR_[:, :, 0:3], 0.0))
                project(W, o_iq, D, X, SEQ, on_act(lambda f: iq[:, f, :]), xt=t_hn)
                t_iq = act.last()

                def view(slot):
                    return slot[:, 0:KC * 144].rearrange("p (k n) -> p k n", k=KC)
                ask([(lambda sl, c=c, n=n: view(sl)[:, :, c:c + n], W[:, o:o + n].rearrange("(k p) n -> p k n", p=128))
                     for c, o, n in ((0, o_ik, 64), (64, o_ik, 80))],
                    [lambda sl, k0=k0: view(sl)[:, k0:k0 + 4, :] for k0 in (0, 4)])
                bs = [bank() for _ in range(2)]
                for k0 in (0, 4):
                    wh, wl, tok, release = part()
                    for b, m0_, m in ((bs[0], 0, 128), (bs[1], 128, 16)):
                        for x in range(4):
                            kc = k0 + x
                            t = mm3(PS[0:m, b, 0:SEQ], wh[:, x, m0_:m0_ + m], wl[:, x, m0_:m0_ + m], hh[:, kc, :],
                                    hl[:, kc, :], kc == 0, kc == KC - 1, tok, *take(b), inc=(x == 3))
                    release(t)
                free[bs[0]] = [actv(ik[:, 0, :], PS[:, bs[0], 0:SEQ], ACT.Copy, t, own=False)]
                t_ikr = act.last()
                iwT = rel[0][0:16, :]
                free[bs[1]] = [actv(iwT, PS[0:16, bs[1], 0:SEQ], ACT.Copy, t, scale=1.0 / 32, own=False)]
                t_iw = act.last()

                def weights():
                    b = bank()
                    for i in range(2):
                        t = tr(PS[:, b, i * 16:(i + 1) * 16], iwT[:, i * 128:(i + 1) * 128], ident[0:16, 0:16], t_iw,
                               *take(b), inc=(i == 1))
                    free[b] = [cp(flat(iw), PS[:, b, 0:32], t)]
                beside.append(weights)

                def rotate(x, i, f0, n, *waits):
                    co, si = B2["cs"][i]
                    nb = (n + 1) // 2
                    while turn[0] % 8 > 8 - nb:
                        turn[0] += 1
                    b0 = turn[0] % 8
                    turn[0] += nb
                    src = x[:, f0:f0 + n, :]
                    pe.wait(*waits)
                    for f in range(n):
                        b = b0 + f // 2
                        t = mm(PS[:, b, (f % 2) * 256:(f % 2 + 1) * 256], B2["rot"][i], src[:, f, :], True, True,
                               *take(b), inc=(f == n - 1))
                    y = PS[:, b0:b0 + nb, :].rearrange("p b (c t) -> p (b c) t", c=2)[:, 0:n, :]
                    sh = [128, n, SEQ]
                    t = tt(dve, t1[:, f0:f0 + n, :], y, bc(si, sh, 1), MUL, t)
                    for b in range(b0, b0 + nb):
                        free[b] = [t]
                    tt(dve, src, src, bc(co, sh, 1), MUL)
                    return tt(dve, src, src, t1[:, f0:f0 + n, :], ADD)
                t_rot = {}

                def rotations(name, x, i, t):
                    for f0 in range(0, x.shape[1], 2):
                        n = min(2, x.shape[1] - f0)
                        beside.append(lambda f0=f0, n=n: t_rot.update({name: rotate(x, i, f0, n, t)}))

                t_cx = {}

                def conv(n):
                    for i in range(4):
                        w = par("conv_w", (l * 4 + i) * NRB + n, 1, RB)
                        if i == 0:
                            ts(dve, CX_[:, n, :], XR_[:, n, 0:SEQ], w, par("conv_b", l * NRB + n, 1, RB), MUL, ADD,
                               t_xr[n], own=False)
                        else:
                            t = stt(CX_[:, n, :], XR_[:, n, i:i + SEQ], w, CX_[:, n, :], MUL, ADD)
                    t_cx[n] = t

                def softplus():
                    lamp = par("lam", l * NRB, NRB, RB)
                    e0, ab, u1, mk, ln, nsp = [spv[:, i, :] for i in range(6)]
                    ts(dve, ab, lamp, -1.0, None, MUL)
                    t = tt(dve, ab, ab, lamp, ALU.min)
                    t = actv(e0, ab, ACT.Exp, t)
                    t = ts(dve, u1, e0, 1.0, None, ADD, ALU.bypass, t)
                    t = actv(ln, u1, ACT.Ln, t)
                    ts(dve, u1, u1, -1.0, None, ADD, ALU.bypass, t)
                    ts(dve, mk, u1, 0.0, None, ALU.is_equal)
                    tt(dve, u1, u1, mk, ADD)
                    tt(dve, ln, ln, mk, ADD)
                    dve.op(lambda e: e.reciprocal(u1, u1))
                    tt(dve, ln, ln, u1, MUL)
                    tt(dve, ln, ln, e0, MUL)
                    ts(dve, mk, lamp, -1.0, 0.0, MUL, MAX)
                    tt(dve, nsp, ln, mk, ADD)
                    ts(dve, nsp, nsp, -8.0, None, MUL)
                nsp = spv[:, 5, :]
                softplus()
                t_xr = {}

                def take_xr(i, o, t):
                    t_xr[i] = actv(XR_[:, i, 3:SEQ + 3], o, ACT.Copy, t, own=False)
                    beside.append(lambda: conv(i))
                    return t_xr[i]
                pace[0] = 1
                project(W, o_xr, RB * NRB, X, SEQ, take_xr, step=RB)
                rotations("iq", iq, 1, t_iq)
                rotations("ik", ik, 1, t_ikr)
                project(W, o_q, D, X, SEQ, on_act(lambda f: q[:, f, :]))
                t_q = act.last()
                used = [None] * 2
                rotations("q", q, 0, t_q)

                def index(i, h):
                    nk = 128 * (i + 1)
                    p0 = 64 * (h % 2)
                    b = bank()
                    t = mm(PS[:, b, 0:nk], iq[p0:p0 + 64, h // 2, i * 128:(i + 1) * 128], ik[p0:p0 + 64, 0, 0:nk], True,
                           True, t_rot["iq"], t_rot["ik"], *take(b), inc=True)
                    x = rel[h % 2][:, 0:nk]
                    t = actv(x, PS[:, b, 0:nk], ACT.Relu, t, *([used[h % 2]] if used[h % 2] else []), own=False)
                    free[b] = [t]
                    o = score[:, i, 0:nk]
                    if h == 0:
                        t = ts(dve, o, x, iw[:, i, h:h + 1], None, MUL, ALU.bypass, t)
                    else:
                        t = stt(o, x, iw[:, i, h:h + 1], o, MUL, ADD, t)
                    used[h % 2] = t
                beside.extend([lambda i=i, h=h: index(i, h) for i in range(2) for h in range(16)])
                pace[0] = 2
                project(W, o_k, D, X, SEQ, on_act(lambda f: k[:, f, :]))
                t_k = act.last()
                rotations("k", k, 0, t_k)
                t_ri = {}
                for nm, dst, bn in (("w_rg_2", RR_, "b_rg"), ("w_ig_2", II_, "b_ig")):
                    def view2(slot):
                        return slot[0:RB, 0:NRB * RB].rearrange("p (n d) -> p n d", n=NRB)
                    s, slot, tok = load([(view2, A[nm][l].rearrange("n c d -> c n d"))])
                    for n in range(NRB):
                        b = bank()
                        t = mm(PS[0:RB, b, 0:SEQ], view2(slot)[:, n, :], CX_[:, n, :], True, True, tok, t_cx[n], *take(b),
                               inc=True)
                        free[b] = [actv(dst[:, n, :], PS[0:RB, b, 0:SEQ], ACT.Sigmoid, t,
                                        bias=par(bn, l * NRB + n, 1, RB), own=False)]
                        if beside:
                            beside.pop(0)()
                    done(s, t)
                    t_ri[nm] = act.last()
                t_gate = pe.last()
                rest()
                t_idx = pe.last()
                act.wait(t_rot["k"])
                tk = {}
                pairs = [slice(n, n + 2) for n in range(0, NRB, 2)]

                def step1(n):
                    if n < len(pairs):
                        c = pairs[n]
                        tk["l", n] = tt(dve, RR_[:, c, :], RR_[:, c, :], bc(nsp[:, c], [RB, 2, SEQ], 2), MUL,
                                        t_ri["w_rg_2"])
                    if n:
                        c = pairs[n - 1]
                        actv(AA_[:, c, :], RR_[:, c, :], ACT.Exp, tk["l", n - 1], own=False)
                        tk["a", n - 1] = actv(RR_[:, c, :], RR_[:, c, :], ACT.Tanh, scale=-1.0)

                def step2(n):
                    c = pairs[n]
                    tt(dve, II_[:, c, :], II_[:, c, :], CX_[:, c, :], MUL, t_ri["w_ig_2"])
                    tt(dve, CX_[:, c, :], AA_[:, c, :], AA_[:, c, :], MUL, tk["a", n], t_gate)
                    tk["q"] = stt(CX_[:, c, :], CX_[:, c, :], 1.0, RR_[:, c, :], ADD, MUL)

                def roots(h):
                    c = slice(8 * h, 8 * h + 8)
                    tk["s", h] = actv(CX_[:, c, :], CX_[:, c, :], ACT.Sqrt, tk["q"], own=False)

                def step3(n):
                    c = pairs[n]
                    dve.op(lambda e: e.memset(AA_[:, c, 0:1], 0.0), own=False)
                    tt(dve, II_[:, c, :], II_[:, c, :], CX_[:, c, :], MUL, tk["s", n // 4])
                    dve.op(lambda e: e.tensor_tensor_scan(flat(CX_[:, c, :]), flat(AA_[:, c, :]), flat(II_[:, c, :]), 0.0,
                                                          MUL, ADD))
                beside.extend([lambda n=n: step1(n) for n in range(9)])
                pace[0] = 1
                values(W, o_v, X, [(0, 128), (128, 128)], V)
                rest()
                beside.extend([lambda n=n: step2(n) for n in range(8)])
                project(W, o_mb, D, X, SEQ, on_act(lambda i: M[:, i, :], ACT.Sigmoid))
                t_mb = act.last()
                rest()
                beside.extend([lambda h=h: roots(h) for h in range(2)])

                def start_top(i):
                    tt(dve, score[:, i, 0:128 * (i + 1)], score[:, i, 0:128 * (i + 1)],
                       B2["causal"][:, i, 0:128 * (i + 1)], ADD)

                def top8(i, r):
                    o = score[:, i, 0:128 * (i + 1)]
                    mx = m8[:, 8 * (r % 2):8 * (r % 2) + 8]
                    dve.op(lambda e: e.max(mx, o))
                    dve.op(lambda e: e.match_replace(o, mx, o, TAKEN))

                def end_top(i):
                    o, ca = score[:, i, 0:128 * (i + 1)], B2["causal"][:, i, 0:128 * (i + 1)]
                    ts(dve, o, o, TAKEN, -NEG, ALU.is_equal, MUL)
                    stt(bias[:, i, 0:128 * (i + 1)], o, NEG, ca, ADD, ADD)
                for i in range(2):
                    if i:
                        beside.extend([lambda n=n: step3(n) for n in range(8)])
                    beside.append(lambda i=i: start_top(i))
                    beside.extend([lambda i=i, r=r: top8(i, r) for r in range(8)])
                    beside.append(lambda i=i: end_top(i))
                act.wait(dve.last())
                pace[0] = 2
                project(W, o_gr, RB * NRB, X, SEQ, on_act(lambda i: GR_[:, i, :], ACT.Silu), step=RB)
                t_gr = act.last()
                rest()
                for n in range(0, NRB, 4):
                    beside.append(lambda c=slice(n, n + 4): tt(dve, CX_[:, c, :], CX_[:, c, :], GR_[:, c, :], MUL, t_gr))
                moves = []
                for n in range(NRB):
                    f = n * RB
                    while f < (n + 1) * RB:
                        m = min((n + 1) * RB, (f // 128 + 1) * 128) - f
                        moves.append((HC[f % 128:f % 128 + m, f // 128, :], CX[f - n * RB:f - n * RB + m, n, :]))
                        f += m
                def relay():
                    pool.wait(dve.last())
                    for o, i in moves:
                        pool.op(lambda e, o=o, i=i: e.dma_start(o, i).then_inc(s_move, 16), own=False, inc=False)
                beside.append(relay)
                nmove[0] += 16 * len(moves)
                t_hc = (s_move, nmove[0])
                act.wait(t_idx)
                project(W, o_ga, D, X, SEQ, on_act(lambda i: GA[:, i, :], ACT.Silu))
                rest()
                MA = XR[:, :, :].rearrange("p a b -> p (a b)")[:, 0:KC * SEQ].rearrange("p (a b) -> p a b", a=KC)
                NP_ = 4
                scratch = flat(XR)[:, KC * SEQ:]
                S = [scratch[:, n * SEQ:(n + 1) * SEQ] for n in range(NP_)]
                Ex = [scratch[:, (NP_ + n) * SEQ:(NP_ + n + 1) * SEQ] for n in range(NP_)]
                st = [m8[:, 4 * n:4 * n + 4] for n in range(NP_)]
                pT = [x.rearrange("p (a b) -> p a b", a=2) for x in rel]
                spare = flat(CX)[:, 11 * SEQ:]
                oT = [flat(RR)[:, n * KC * SEQ:(n + 1) * KC * SEQ].rearrange("p (a b) -> p a b", a=KC) for n in range(2)]
                two_parts(HH, HC)
                two_parts(*oT)
                items = [(h, i) for h in range(8) for i in range(2)]
                t_ex, t_nrm, t_tr, t_pc, t_pv = {}, {}, {}, {}, {}
                SC = float(128 ** -0.5)

                def others():
                    split_hc = list(range(0, 11, 2))
                    for n, _ in enumerate(project_units(W, o_ma, D, X, SEQ, on_act(lambda i: MA[:, i, :]),
                                                        banks=[4, 5, 6, 7])):
                        if n >= 5:
                            for _ in range(2):
                                f = split_hc.pop(0)
                                c = slice(f, min(f + 2, 11))
                                t = high_low(HH[:, c, :], HC[:, c, :], HC[:, c, :], t_hc, own=False)
                        yield
                    t_ma.append(act.last())
                    yield from contract_units(A["w_out_rnn_2"][l], 11, (HH, HC), SEQ,
                                              lambda i, o, t: tt(dve, M[:, i, :], M[:, i, :], o, MUL, t, own=False),
                                              t, banks=[4, 5, 6, 7])
                t_ma = []
                other = others()

                def first(n):
                    h, i = items[n]
                    nk = 128 * (i + 1)
                    b = n % 2
                    t = mm(PS[:, b, 0:nk], q[:, h, i * 128:(i + 1) * 128], k[:, h, 0:nk], True, True, *take(b), inc=True)
                    s_, x_ = S[n % NP_][:, 0:nk], st[n % NP_]
                    w = [t_ex[n - NP_]] if n >= NP_ else []
                    t = tt(dve, s_, PS[:, b, 0:nk], bias[:, i, 0:nk], ADD, t, *w)
                    free[b] = [t]
                    dve.op(lambda e: e.tensor_reduce(x_[:, 0:1], s_, AX, MAX))
                    t = ts(dve, x_[:, 1:2], x_[:, 0:1], -SC, None, MUL)
                    w = [t_nrm[n - NP_], t_tr[n - NP_]] if n >= NP_ else []
                    t_ex[n] = actv(Ex[n % NP_][:, 0:nk], s_, ACT.Exp, t, *w, bias=x_[:, 1:2], scale=SC,
                                   accum=x_[:, 2:3], own=False)

                def second_(n):
                    h, i = items[n]
                    nk = 128 * (i + 1)
                    e_, x_ = Ex[n % NP_][:, 0:nk], st[n % NP_]
                    dve.op(lambda e: e.reciprocal(x_[:, 3:4], x_[:, 2:3]), t_ex[n])
                    t_nrm[n] = ts(dve, e_, e_, x_[:, 3:4], None, MUL)

                def third(n):
                    h, i = items[n]
                    e_ = Ex[n % NP_]
                    w = take(2)
                    for kt in range(i + 1):
                        t = tr(PS[:, 2, kt * 128:(kt + 1) * 128], e_[:, kt * 128:(kt + 1) * 128], ident, t_nrm[n], *w,
                               inc=(kt == i))
                    t_tr[n] = t
                    p_ = pT[n % 2]
                    t = actv(flat(p_)[:, 0:128 * (i + 1)], PS[:, 2, 0:128 * (i + 1)], ACT.Copy, t,
                             *([t_pv[n - 2]] if n >= 2 else []), own=False)
                    free[2] = [t]
                    t_pc[n] = t

                def fourth(n):
                    h, i = items[n]
                    p_ = pT[n % 2]
                    for kt in range(i + 1):
                        t = mm(PS[:, 3, 0:128], V[:, kt, h * 128:(h + 1) * 128], p_[:, kt, :], kt == 0, kt == i, t_pc[n],
                               *take(3), inc=(kt == i))
                    t_pv[n] = t
                    c = slice(i * 128, (i + 1) * 128)
                    x = flat(score)[:, (n % 4) * 128:(n % 4 + 1) * 128]
                    t = tt(dve, x, PS[:, 3, 0:128], GA[:, h, c], MUL, t, *([t_o[n - 4]] if n >= 4 else []), own=False)
                    free[3] = [t]
                    t_o[n] = high_low(oT[0][:, h, c], oT[1][:, h, c], x, t, own=False)
                t_o = {}
                dve.wait(t_mb, act.last())
                act.wait(dve.last(), pe.last())
                pe.wait(act.last(), dve.last())
                for n in range(len(items) + 3):
                    if n < len(items):
                        first(n)
                    if 1 <= n <= len(items):
                        second_(n - 1)
                    if n >= 3:
                        fourth(n - 3)
                    if 2 <= n < len(items) + 2:
                        third(n - 2)
                    next(other, None)
                for _ in other:
                    pass
                t_ma[0] = actv(flat(MA), flat(MA), ACT.Sigmoid, own=False)
                tmp = [spare[:, 512 + n * SEQ:512 + (n + 1) * SEQ] for n in range(2)]

                def merge(i, o, t):
                    x = tmp[i % 2]
                    t = tt(dve, x, MA[:, i, :], o, MUL, t, *([t_sum[i - 2]] if i > 1 else []), own=False)
                    t_sum[i] = tt(pool, M[:, i, :], M[:, i, :], x, ADD, t, own=False)
                    if i:
                        split_m(i - 1)
                    return t

                def split_m(i):
                    t_m[i] = high_low(q[:, i, :], k[:, i, :], M[:, i, :], t_sum[i], own=False, eng=pool)
                t_m, t_sum = {}, {}
                two_parts(q, k)
                pool.wait(dve.last(), act.last(), pe.last())
                act.wait(pe.last())
                dve.wait(*t_ma)
                project(A["w_out_attn_2"][l], 0, D, oT, SEQ, merge, dve.last())
                split_m(KC - 1)

                def residual(i, o, t):
                    return tt(dve, X2[:, i, :], X2[:, i, :], o, ADD, t)
                project(A["w_o_2"][l], 0, D, (q, k), SEQ, residual, xt=t_m)
                barrier()
                top[0] = m0

            def final():
                O = ar3(KC, SEQ)
                rms(O, "final_g", 0)
                B2["out"] = O

            stage_list = [attention, ffn, rwkv, moe, tables, lambda: second(0), lambda: second(1), final]
            for st_ in stage_list[:stages]:
                st_()
            toks = [x.last() for x in (pe, dve, act, pool) if x.n]
            src = B2["out"] if stages > 7 else H
            fin = sp.start(out, src, s_out, 16, *toks)
            sp.items.append(fin)
            return pe, dve, act, pool, sp, asked

        plan = program(None)[-1]
        pe, dve, act, pool, sp, _ = program(plan)

        block = ctx.enter_context(nc.Block())

        @block.sync
        def _(e):
            sp.emit(e)

        @block.tensor
        def _(e):
            pe.emit(e)

        @block.vector
        def _(e):
            dve.emit(e)

        @block.scalar
        def _(e):
            act.emit(e)

        @block.gpsimd
        def _(e):
            pool.emit(e)


def constants():
    f = np.float32
    base = np.zeros((128, 592), f)
    base[:, 583] = 1.0
    base[:, 0:128] = np.eye(128)
    base[:, 128:256] = 1.0
    base[0:64, 256:320] = 1.0
    base[:, 384:448] = np.tile(np.eye(64), (2, 1))
    base[64:128, 320:384] = 1.0
    for h in range(16):
        base[64 * (h % 2):64 * (h % 2) + 64, 448 + 16 * (h // 2) + h] = 1.0
    dist = np.zeros((128, 3, T), f)
    for i, (q0, qn) in enumerate(QT):
        dist[0:qn, i, :] = np.abs(np.arange(q0, q0 + qn)[:, None] - np.arange(T)[None, :])
    rw = np.zeros((128, NC_RW), f)
    rw[:, C_SCAN:C_SCAN + TS] = (np.arange(TS) % CH != 0)
    rw[0:16, C_SPREAD:] = np.arange(D)[None, :] // 64 == np.arange(16)[:, None]
    i = np.arange(64)
    for l, s in enumerate(SCAN_LEVELS):
        same = (i[:, None] // (2 * s)) == (i[None, :] // (2 * s))
        low = same & (i[:, None] % (2 * s) >= s) & (i[None, :] % (2 * s) < s)
        for x, m in enumerate([low, low.T]):
            o = C_LVL + (x * len(SCAN_LEVELS) + l) * 64
            rw[:, o:o + 64] = np.tile(m, (2, 1))
    for d in range(2):
        j, t = i[:, None], i[None, :]
        strict, incl = (j < t, j <= t) if d == 0 else (j > t, j >= t)
        for x in range(2):
            o = C_AM + (2 * d + x) * 128
            rw[:, o:o + 64] = np.tile(strict, (2, 1))
            rw[:, o + 64:o + 128] = np.tile(incl * (-1.0 if x else 1.0), (2, 1))
    b2 = np.zeros((128, NC_B2), f)
    for x, half in enumerate((64, 32)):
        for m in range(128):
            if m % (2 * half) < half:
                b2[m + half, x * 128 + m] = -1.0
            else:
                b2[m - half, x * 128 + m] = 1.0
        dim = 2 * half
        inv = np.float32(10000.0) ** (-np.arange(0, dim, 2, dtype=f) / np.float32(dim))
        b2[:, 768 + x] = inv[np.arange(128) % half]
    for x in range(2):
        qp = x * 128 + np.arange(128)
        b2[:, 256 + x * 256:512 + x * 256] = np.where(np.arange(SEQ)[None, :] <= qp[:, None], 0.0, NEG)
    moe = np.zeros((128, 224), f)
    moe[0:96, 0:96] = np.arange(96)[:, None] < np.arange(96)[None, :]
    moe[:, 96:192] = np.arange(96)
    moe[:, 192] = np.arange(128)
    return {"c_moe": moe, "c_b2": b2, "c_base": base, "c_dist": dist.reshape(128, 3 * T), "c_rw": rw}


def by_partition(v, p=128):
    return np.ascontiguousarray(v.reshape(-1, p).T)


def lay_out(inputs):
    g = {k: np.asarray(v) for k, v in inputs.items()}
    par = np.zeros((128, NPAR), np.float32)

    def put(name, m):
        o = POFF[name]
        par[0:m.shape[0], o:o + m.shape[1]] = m
    for name, src in (("ln_g", "ln_g"), ("ln_b", "ln_b"), ("subln", "attn_subln_g"), ("mu", "rw_mu"), ("w0", "rw_w0"),
                      ("a0", "rw_a0"), ("k_k", "rw_k_k"), ("k_a", "rw_k_a"), ("r_k", "rw_r_k"),
                      ("lnx_g", "rw_lnx_g"), ("lnx_b", "rw_lnx_b"), ("norm_g", "norm_g_2"), ("final_g", "final_g_2")):
        put(name, by_partition(g[src]))
    for name, src in (("conv_w", "conv_w_2"), ("conv_b", "conv_b_2"), ("b_rg", "b_rg_2"), ("b_ig", "b_ig_2"),
                      ("lam", "lru_lambda_2")):
        put(name, by_partition(g[src], RB))
    lam = np.concatenate([g[n].reshape(-1) for n in ("attn_lam_q1", "attn_lam_k1", "attn_lam_q2", "attn_lam_k2")])
    put("lamv", np.broadcast_to(lam, (128, 256)))
    put("b_router", np.broadcast_to(g["moe_b_router"].reshape(-1), (128, NE)))
    h = np.concatenate([g["meta"], g["x"][0]], 0)
    hT = h.T.reshape(KC, 128, T).transpose(1, 0, 2).reshape(128, KC * T)
    arrays = {"par": par, "hT": np.ascontiguousarray(hT)}
    arrays["pos"] = np.ascontiguousarray(np.broadcast_to(g["positions_2"].reshape(1, SEQ), (128, SEQ)))
    arrays.update(constants())
    for n in BIG:
        arrays[n] = np.ascontiguousarray(g[n])
    return arrays


BIG = ["attn_w_in", "attn_w_o", "ffn_w_gate", "ffn_w_up", "ffn_w_down", "rw_w_rkv", "rw_w1", "rw_w2", "rw_a1", "rw_a2",
       "rw_g1", "rw_g2", "rw_w_o", "moe_w_router", "moe_w_gate", "moe_w_up", "moe_w_down",
       "w_in_2", "w_rg_2", "w_ig_2", "w_out_attn_2", "w_out_rnn_2", "w_o_2"]


def kernel(**inputs):
    import concourse.bacc as bacc
    from concourse.bass_utils import run_bass_kernel_spmd

    arrays = lay_out(inputs)
    nc = bacc.Bacc("TRN2", target_bir_lowering=False, num_devices=1)
    A = {n: nc.dram_tensor(f"in_{n}", a.shape, mybir.dt.from_np(a.dtype), kind="ExternalInput").ap()
         for n, a in arrays.items()}
    out = nc.dram_tensor("out_dram", (128, KC, SEQ), F32, kind="ExternalOutput").ap()
    build(nc, A, out)
    r = run_bass_kernel_spmd(nc, [{f"in_{n}": a for n, a in arrays.items()}], core_ids=[0])
    o = r.results[0]["out_dram"]
    return np.ascontiguousarray(o.transpose(2, 1, 0).reshape(1, SEQ, D))
```
